# Optimizing a Trainium2 kernel written in Bass

```python
import math
import jax
import jax.numpy as jnp
from jax import lax
import numpy as np

D_MODEL = 2048
BATCH = 1
SEQ = 256
DEPTH = 2

N_A_LAYERS = DEPTH // 2
N_B_LAYERS = DEPTH - N_A_LAYERS
HEAD_DIM = 128
ROT_DIM = HEAD_DIM // 4
ROPE_THETA = 500000.0
NORM_EPS = 1e-6
NEG_INF = -1e30
A_PATTERNS = ((128, 1), (512, 4), (2048, 16))
N_A_GROUPS = len(A_PATTERNS)
A_HEADS = 8
A_GROUP_WIDTH = A_HEADS * HEAD_DIM
A_QKV_WIDTH = N_A_GROUPS * 3 * A_GROUP_WIDTH
BAND_BLOCK = 128
B_HEADS = 8
B_QK_WIDTH = B_HEADS * 2 * HEAD_DIM
B_V_DIM = 2 * HEAD_DIM
B_V_WIDTH = B_HEADS * B_V_DIM
Q_BLOCK = 128
D_FF = 4 * D_MODEL
N_MOD = 6

kernel_name = "yoco_dilated_diffattn_adaln_trunk"

def rms_norm(t, gain):
    t32 = t.astype(jnp.float32)
    y = t32 * lax.rsqrt(jnp.mean(t32 * t32, axis=-1, keepdims=True) + NORM_EPS)
    return (y * gain.astype(jnp.float32)).astype(t.dtype)

def modulate(h, shift, scale):
    return h * (1.0 + scale[:, None, :]) + shift[:, None, :]

def rope_tables(positions):
    inv_freq = ROPE_THETA ** (-jnp.arange(0, ROT_DIM, 2, dtype=jnp.float32) / ROT_DIM)
    ang = positions.astype(jnp.float32)[..., None] * inv_freq
    return jnp.cos(ang)[:, :, None, :], jnp.sin(ang)[:, :, None, :]

def apply_rope(t, cos, sin):
    half = ROT_DIM // 2
    cos = cos.astype(t.dtype)
    sin = sin.astype(t.dtype)
    t1 = t[..., :half]
    t2 = t[..., half:ROT_DIM]
    return jnp.concatenate([t1 * cos - t2 * sin, t2 * cos + t1 * sin, t[..., ROT_DIM:]], axis=-1)

def rope_pairs(t, cos, sin):
    b, s, h, two, e = t.shape
    return apply_rope(t.reshape(b, s, h * two, e), cos, sin).reshape(b, s, h, two, e)

def dilated_window_attention(q, k, v, window, dilation):
    bsz, seq, heads, hd = q.shape
    sub_len = seq // dilation
    sub_win = window // dilation
    n_blk = -(-sub_len // BAND_BLOCK)
    pad = n_blk * BAND_BLOCK - sub_len

    def to_blocks(t):
        e = t.shape[-1]
        t = t.reshape(bsz, sub_len, dilation, heads, e).transpose(0, 2, 1, 3, 4)
        t = jnp.pad(t, ((0, 0), (0, 0), (0, pad), (0, 0), (0, 0)))
        return t.reshape(bsz, dilation, n_blk, BAND_BLOCK, heads, e)

    def with_prev(t):
        prev = jnp.pad(t[:, :, :-1], ((0, 0), (0, 0), (1, 0), (0, 0), (0, 0), (0, 0)))
        return jnp.concatenate([prev, t], axis=3)

    def from_blocks(t):
        e = t.shape[-1]
        t = t.reshape(bsz, dilation, n_blk * BAND_BLOCK, heads, e)[:, :, :sub_len]
        return t.transpose(0, 2, 1, 3, 4).reshape(bsz, seq, heads, e)

    qb = to_blocks(q)
    kb = with_prev(to_blocks(k))
    vb = with_prev(to_blocks(v))
    s = jnp.einsum('brnqhe,brnkhe->brnhqk', qb, kb,
                   preferred_element_type=jnp.float32) * (hd ** -0.5)
    qi = jnp.arange(BAND_BLOCK)[:, None]
    ki = jnp.arange(2 * BAND_BLOCK)[None, :]
    dist = BAND_BLOCK + qi - ki
    kpos = jnp.arange(n_blk)[:, None, None] * BAND_BLOCK - BAND_BLOCK + ki[None]
    valid = (dist >= 0) & (dist <= sub_win) & (kpos >= 0)
    s = jnp.where(valid[:, None], s, NEG_INF)
    m = jnp.max(s, axis=-1, keepdims=True)
    p = jnp.exp(s - m)
    den = jnp.sum(p, axis=-1, keepdims=True)
    o = jnp.einsum('brnhqk,brnkhe->brnqhe', p.astype(v.dtype), vb,
                   preferred_element_type=jnp.float32)
    o = o / jnp.swapaxes(den, 3, 4)
    lse = jnp.swapaxes(m + jnp.log(den), 3, 4)
    return from_blocks(o), from_blocks(lse)[..., 0]

def mixer_a(h, cos, sin, w_qkv, q_gain, k_gain, w_o):
    bsz, seq, _ = h.shape
    qkv = (h @ w_qkv).reshape(bsz, seq, N_A_GROUPS, 3, A_HEADS, HEAD_DIM)
    outs, lses = [], []
    for g, (window, dilation) in enumerate(A_PATTERNS):
        q = apply_rope(rms_norm(qkv[:, :, g, 0], q_gain[g]), cos, sin)
        k = apply_rope(rms_norm(qkv[:, :, g, 1], k_gain[g]), cos, sin)
        o, lse = dilated_window_attention(q, k, qkv[:, :, g, 2], window, dilation)
        outs.append(o)
        lses.append(lse)
    alpha = jax.nn.softmax(jnp.stack(lses), axis=0)
    o = jnp.sum(alpha[..., None] * jnp.stack(outs), axis=0)
    return o.reshape(bsz, seq, A_GROUP_WIDTH).astype(h.dtype) @ w_o

def shared_kv(x, c_act, w_ada, b_ada, g, w_k, w_v, k_gain, cos, sin):
    bsz, seq, _ = x.shape
    shift, scale = jnp.split(c_act @ w_ada + b_ada, 2, axis=-1)
    h = modulate(rms_norm(x, g), shift, scale)
    k = rms_norm((h @ w_k).reshape(bsz, seq, B_HEADS, 2, HEAD_DIM), k_gain)
    k = rope_pairs(k, cos, sin)
    v = (h @ w_v).reshape(bsz, seq, B_HEADS, B_V_DIM)
    return k, v

def differential_attention(q, k, v, lam):
    bsz, seq, heads, _, hd = q.shape
    n_blk = seq // Q_BLOCK
    qb = jnp.swapaxes(q.reshape(bsz, n_blk, Q_BLOCK, heads, 2, hd), 0, 1)
    kpos = jnp.arange(seq)

    def block(args):
        q_blk, i = args
        s = jnp.einsum('bqhce,bkhce->bhcqk', q_blk, k,
                       preferred_element_type=jnp.float32) * (hd ** -0.5)
        qpos = i * Q_BLOCK + jnp.arange(Q_BLOCK)
        s = jnp.where(kpos[None, :] <= qpos[:, None], s, NEG_INF)
        p = jax.nn.softmax(s, axis=-1)
        a = p[:, :, 0] - lam * p[:, :, 1]
        return jnp.einsum('bhqk,bkhe->bqhe', a.astype(v.dtype), v,
                          preferred_element_type=jnp.float32)

    o = lax.map(block, (qb, jnp.arange(n_blk)))
    return jnp.swapaxes(o, 0, 1).reshape(bsz, seq, heads, 2 * hd)

def mixer_b(h, k, v, cos, sin, w_q, q_gain, lam_params, subln_g, w_o, lam_init):
    bsz, seq, _ = h.shape
    q = rope_pairs(rms_norm((h @ w_q).reshape(bsz, seq, B_HEADS, 2, HEAD_DIM), q_gain), cos, sin)
    lp = lam_params.astype(jnp.float32)
    lam = jnp.exp(jnp.sum(lp[0] * lp[1])) - jnp.exp(jnp.sum(lp[2] * lp[3])) + lam_init
    o = differential_attention(q, k, v, lam)
    o = rms_norm(o, subln_g) * (1.0 - lam_init)
    return o.reshape(bsz, seq, B_V_WIDTH).astype(h.dtype) @ w_o

def sq_relu_mlp(h, w1, w2):
    return jnp.square(jax.nn.relu(h @ w1)) @ w2

def setup_inputs(seed: int = 0) -> dict:
    key = jax.random.key(seed)
    ks = jax.random.split(key, 24)
    f32 = jnp.float32
    nrm = lambda k, shape, std: jax.random.normal(k, shape, f32) * std
    ada_std = 0.5 * D_MODEL ** -0.5
    x = nrm(ks[0], (BATCH, SEQ, D_MODEL), 1.0)
    c = nrm(ks[1], (BATCH, D_MODEL), 1.0)
    positions = (jnp.arange(SEQ, dtype=jnp.int32)[None, :]
                 + jax.random.randint(ks[2], (BATCH, 1), 0, 4096, dtype=jnp.int32))
    ada_w = nrm(ks[3], (DEPTH, D_MODEL, N_MOD * D_MODEL), ada_std)
    ada_b = nrm(ks[4], (DEPTH, N_MOD * D_MODEL), 0.01)
    norm_g = 1.0 + nrm(ks[5], (DEPTH, 2, D_MODEL), 0.02)
    a_w_qkv = nrm(ks[6], (N_A_LAYERS, D_MODEL, A_QKV_WIDTH), D_MODEL ** -0.5)
    a_q_gain = 1.0 + nrm(ks[7], (N_A_LAYERS, N_A_GROUPS, HEAD_DIM), 0.02)
    a_k_gain = 1.0 + nrm(ks[8], (N_A_LAYERS, N_A_GROUPS, HEAD_DIM), 0.02)
    a_w_o = nrm(ks[9], (N_A_LAYERS, A_GROUP_WIDTH, D_MODEL), A_GROUP_WIDTH ** -0.5)
    kv_ada_w = nrm(ks[10], (D_MODEL, 2 * D_MODEL), ada_std)
    kv_ada_b = nrm(ks[11], (2 * D_MODEL,), 0.01)
    kv_norm_g = 1.0 + nrm(ks[12], (D_MODEL,), 0.02)
    kv_w_k = nrm(ks[13], (D_MODEL, B_QK_WIDTH), D_MODEL ** -0.5)
    kv_w_v = nrm(ks[14], (D_MODEL, B_V_WIDTH), D_MODEL ** -0.5)
    kv_k_gain = 1.0 + nrm(ks[15], (2, HEAD_DIM), 0.02)
    b_w_q = nrm(ks[16], (N_B_LAYERS, D_MODEL, B_QK_WIDTH), D_MODEL ** -0.5)
    b_q_gain = 1.0 + nrm(ks[17], (N_B_LAYERS, 2, HEAD_DIM), 0.02)
    b_lambda = nrm(ks[18], (N_B_LAYERS, 4, HEAD_DIM), 0.1)
    b_subln_g = 1.0 + nrm(ks[19], (N_B_LAYERS, B_V_DIM), 0.02)
    b_w_o = nrm(ks[20], (N_B_LAYERS, B_V_WIDTH, D_MODEL), B_V_WIDTH ** -0.5)
    mlp_w1 = nrm(ks[21], (DEPTH, D_MODEL, D_FF), D_MODEL ** -0.5)
    mlp_w2 = nrm(ks[22], (DEPTH, D_FF, D_MODEL), D_FF ** -0.5)
    return {"x": x, "c": c, "positions": positions, "ada_w": ada_w, "ada_b": ada_b,
            "norm_g": norm_g, "a_w_qkv": a_w_qkv, "a_q_gain": a_q_gain, "a_k_gain": a_k_gain,
            "a_w_o": a_w_o, "kv_ada_w": kv_ada_w, "kv_ada_b": kv_ada_b, "kv_norm_g": kv_norm_g,
            "kv_w_k": kv_w_k, "kv_w_v": kv_w_v, "kv_k_gain": kv_k_gain, "b_w_q": b_w_q,
            "b_q_gain": b_q_gain, "b_lambda": b_lambda, "b_subln_g": b_subln_g, "b_w_o": b_w_o,
            "mlp_w1": mlp_w1, "mlp_w2": mlp_w2}

def reference(x, c, positions, ada_w, ada_b, norm_g, a_w_qkv, a_q_gain, a_k_gain, a_w_o,
              kv_ada_w, kv_ada_b, kv_norm_g, kv_w_k, kv_w_v, kv_k_gain, b_w_q, b_q_gain,
              b_lambda, b_subln_g, b_w_o, mlp_w1, mlp_w2):
    c_act = jax.nn.silu(c)
    cos, sin = rope_tables(positions)
    k_sh = v_sh = None
    for layer in range(DEPTH):
        if layer == N_A_LAYERS:
            k_sh, v_sh = shared_kv(x, c_act, kv_ada_w, kv_ada_b, kv_norm_g, kv_w_k, kv_w_v,
                                   kv_k_gain, cos, sin)
        mod = c_act @ ada_w[layer] + ada_b[layer]
        shift_t, scale_t, gate_t, shift_m, scale_m, gate_m = jnp.split(mod, N_MOD, axis=-1)
        h = modulate(rms_norm(x, norm_g[layer, 0]), shift_t, scale_t)
        if layer < N_A_LAYERS:
            y = mixer_a(h, cos, sin, a_w_qkv[layer], a_q_gain[layer], a_k_gain[layer], a_w_o[layer])
        else:
            j = layer - N_A_LAYERS
            lam_init = 0.8 - 0.6 * math.exp(-0.3 * layer)
            y = mixer_b(h, k_sh, v_sh, cos, sin, b_w_q[j], b_q_gain[j], b_lambda[j],
                        b_subln_g[j], b_w_o[j], lam_init)
        x = x + gate_t[:, None, :] * y
        h = modulate(rms_norm(x, norm_g[layer, 1]), shift_m, scale_m)
        x = x + gate_m[:, None, :] * sq_relu_mlp(h, mlp_w1[layer], mlp_w2[layer])
    return x


_drawn_inputs = setup_inputs


def setup_inputs(seed=0):
    import zlib

    import numpy as np

    out = dict(_drawn_inputs(seed))
    spreads = {}
    factors = {'norm_g': 4.348,
     'a_q_gain': 8.0,
     'a_k_gain': 8.0,
     'kv_ada_b': 8.0,
     'kv_norm_g': 8.0,
     'kv_k_gain': 8.0,
     'b_q_gain': 8.0,
     'b_lambda': 7.625,
     'b_subln_g': 8.0}
    for name, (base, spread) in spreads.items():
        noise = np.random.default_rng([zlib.crc32(name.encode()), seed]).standard_normal(out[name].shape)
        drawn = base * np.exp(spread * noise) if base else spread * noise
        out[name] = jnp.asarray(drawn.astype(out[name].dtype))
    for name, factor in factors.items():
        out[name] = (out[name] * factor).astype(out[name].dtype)
    return out
```

```python
import math
from contextlib import ExitStack, contextmanager

import numpy as np

import concourse.bass as bass
from concourse import mybir

P = 128
SEQ = 256
T = SEQ // P
D = 2048
KT = D // P
NC = 512
PK = 2
PIECES = KT // PK
SLOTS = 4
ADA_SLOTS = 2
HD = 128
HEADS_A = 8
GROUPS = 3
D_FF = 4 * D
ROT = 32
HALF = ROT // 2
EPS = 1e-6
NEG = -1e30
SCALE = float(HD) ** -0.5
LAM_INIT = 0.8 - 0.6 * math.exp(-0.3)
LAYERS = 2
SECTIONS = 14
MAPS = 4
V_C, V_G = 0, 1
(S_SHIFT_T0, S_SCALE_T0, S_SHIFT_M0, S_SCALE_M0, S_GATE_T0, S_SHIFT_T1, S_SCALE_T1, S_SHIFT_KV, S_GATE_M0,
 S_SCALE_KV, S_SHIFT_M1, S_SCALE_M1, S_GATE_T1, S_GATE_M1) = range(SECTIONS)

ALU = mybir.AluOpType
ACT = mybir.ActivationFunctionType
F32 = mybir.dt.float32
F32R = mybir.dt.float32r
BF16 = mybir.dt.bfloat16
I32 = mybir.dt.int32


class Count:

    def __init__(self):
        self.n, self.base = 0, None

    def up(self, k=1):
        self.n += k
        return self()

    def __call__(self, at=None):
        v = self.n if at is None else at
        return v if self.base is None else self.base + v


class Counts(dict):
    def __missing__(self, name):
        self[name] = Count()
        return self[name]


@contextmanager
def repeat(eng, times, counts, **rises):
    before = {k: c.n for k, c in counts.items()}
    with eng.Fori(0, times) as i:
        for k, r in rises.items():
            counts[k].base = i * r
        yield i
        grown = {k: c.n - before.get(k, 0) for k, c in counts.items() if c.n != before.get(k, 0)}
        assert grown == rises, grown
    for k, r in rises.items():
        counts[k].n += (times - 1) * r
        counts[k].base = None


def cols(i, size):
    return slice(i * size, (i + 1) * size) if isinstance(i, int) else bass.ds(i * size, size)


ADA_QKV = [(c, j) for c, js in enumerate(((1, 4, 6), (1, 4, 6), (1, 4, 6), (1, 4, 6), (2, 5), (1, 3))) for j in js]
ADA_MLP0 = [(c, j) for c in range(8) for j in (1, 5)]
ADA_FOUR = [(c, j) for c in range(4) for j in (0, 2, 4, 5)]
ADA_MLP1 = [(c, 2) for c in (0, 2, 4, 6)]


def trunk(nc, x_in, vecs_in, pos_in, gains_in, subg_in, lamb_in, ada_in, ada_bias_in, w_in, out):
    ctx = ExitStack()
    with ctx:
        def sb(name, shape, dt=F32):
            return ctx.enter_context(nc.sbuf_tensor(name, shape, dt))

        sems = {}

        def sem(name):
            if name not in sems:
                sems[name] = ctx.enter_context(nc.semaphore(name))
            return sems[name]

        w_raw = sb("w_raw", [P, SLOTS, PK * NC])
        w_hi = sb("w_hi", [P, SLOTS, PK * NC], F32R)
        w_lo = sb("w_lo", [P, SLOTS, PK * NC], F32R)
        ada_raw = sb("ada_raw", [P, ADA_SLOTS, D])
        bias_sb = sb("bias_sb", [1, D])
        acc = sb("acc", [P, D])
        xs = sb("xs", [P, T, D])
        work = sb("work", [P, 2 * D])
        hT_hi = sb("hT_hi", [P, KT, T * P], F32R)
        hT_lo = sb("hT_lo", [P, KT, T * P], F32R)
        st_a = sb("st_a", [P, T * NC])
        st_b = sb("st_b", [P, T * NC])
        pT = sb("pT", [P, 2, 3 * P])
        masks = sb("masks", [P, 4, 3 * P], BF16)
        gain_now = sb("gain_now", [P, 2 * HD])
        mask_now = sb("mask_now", [P, 3 * P], BF16)
        gains = sb("gains_sb", [P, 10 * HD])
        subg = sb("subg_sb", [P, 2 * HD])
        ident = sb("ident", [P, P])
        ones = sb("ones", [P, P])
        cols_in = sb("cols_in", [P, P])
        vec = sb("vec", [P, 6, KT])
        c_act = sb("c_act", [P, KT])
        modc = sb("modc", [P, SECTIONS, KT])
        cos = sb("cos", [P, T * HALF])
        sin = sb("sin", [P, T * HALF])
        small = sb("small", [P, 64])
        ssq = sb("ssq", [P, 8])
        rms = sb("rms", [P, 8])
        rstd = sb("rstd", [P, 8])
        ssx = sb("ssx", [P, 2])
        rmsx = sb("rmsx", [P, 2])
        rstdx = sb("rstdx", [P, 2])
        m8 = sb("m8", [P, 8])
        mn8 = sb("mn8", [P, 8])
        neg8 = sb("neg8", [P, 8])
        diff8 = sb("diff8", [P, 8])
        corr8 = sb("corr8", [P, 8])
        d8 = sb("d8", [P, 8])
        r8 = sb("r8", [P, 8])
        m_old = sb("m_old", [P, 2, 8])
        den = sb("den", [P, 2, 8])
        rden = sb("rden", [P, 16])
        eps_t = sb("eps_t", [P, 1])
        hpi_t = sb("hpi_t", [P, 1])
        lam = sb("lam", [P, 8])
        ssv = sb("ssv", [P, 2])
        rmsv = sb("rmsv", [P, 2])
        rstdv = sb("rstdv", [P, 2])
        inv_freq = sb("inv_freq", [P, HALF])
        pos_f = sb("pos_f", [P, T])
        turns = sb("turns", [P, T * HALF])
        dist = sb("dist", [P, P], I32)
        residue_i = sb("residue_i", [P, 2 * P], I32)
        residue = sb("residue", [P, 2 * P], BF16)
        rot = sb("rot", [P, T, 4, MAPS, HALF])
        scratch = sb("scratch", [P, 1])
        marks = sb("marks", [P, PIECES])
        scratch_g = sb("scratch_g", [P, 1])
        pos_i = sb("pos_i", [P, T], I32)

        with nc.sbuf_tensor("mid_hi", [P, KT, T * P], F32R) as mid_hi, \
                nc.sbuf_tensor("mid_lo", [P, KT, T * P], F32R) as mid_lo:
            pass
        qT = sb("qT", [P, 16, T * P])
        kT = sb("kT", [P, MAPS, T * P])
        vv = sb("vv", [P, T, NC])
        sm = sb("sm", [P, MAPS, 3 * P])
        junk = qT[:, :, :].rearrange("p (t a) b -> p t (a b)", t=T)

        main = [[ctx.enter_context(nc.psum_tensor(f"main{p}{t}", [P, NC], F32)) for t in range(T)] for p in range(2)]
        tr = [ctx.enter_context(nc.psum_tensor(f"tr{b}", [P, NC], F32)) for b in range(2)]
        sc = ctx.enter_context(nc.psum_tensor("sc", [P, NC], F32))
        ov = ctx.enter_context(nc.psum_tensor("ov", [P, NC], F32))

        sta = st_a[:, :].rearrange("p (t n) -> p t n", t=T)
        stb = st_b[:, :].rearrange("p (t n) -> p t n", t=T)
        acc_rows = acc[:, :].rearrange("p (n c) -> p n c", c=NC)
        group_out = work[:, 0:D].rearrange("p (h t e) -> p h t e", t=T, e=HD)
        head_out = work[:, :].rearrange("p (h t e) -> p h t e", t=T, e=2 * HD)
        y = work[:, :].rearrange("p (t d) -> p t d", t=T)
        wv = w_in.rearrange("(n p) c -> n p c", p=P)
        av = ada_in.rearrange("(n p) c -> n p c", p=P)

        raw_in = [sem(f"raw_in{s}") for s in range(SLOTS)]
        hi_done = sem("hi_done")
        lo_done = sem("lo_done")
        mm_done = sem("mm_done")
        ada_in = [sem(f"ada_in{s}") for s in range(ADA_SLOTS)]
        ada_used = sem("ada_used")
        bias_in = sem("bias_in")
        acc_full = sem("acc_full")
        read_out = [sem(f"read_out{p}") for p in range(2)]
        tr_free = [sem(f"tr_free{b}") for b in range(2)]
        vec_full, col_full, row_full = sem("vec_full"), sem("col_full"), sem("row_full")
        hT_full, mid_full, qk_full, pt_full = sem("hT_full"), sem("mid_full"), sem("qk_full"), sem("pt_full")
        modulated = sem("modulated")
        hT_split = sem("hT_split")
        hi_part = sem("hi_part")
        sc_full, sc_free = sem("sc_full"), sem("sc_free")
        ov_full, ov_free = sem("ov_full"), sem("ov_free")
        rms_done, roped = sem("rms_done"), sem("roped")
        staged = sem("staged")
        x_rms, x_rstd, x_done = sem("x_rms"), sem("x_rstd"), sem("x_done")
        relu_done = sem("relu_done")
        smx_done, p_done, mix_done = sem("smx_done"), sem("p_done"), sem("mix_done")
        sub_rms, den_inv = sem("sub_rms"), sem("den_inv")
        mod_done, work_zero = sem("mod_done"), sem("work_zero")
        seq_v, seq_a, seq_g = sem("seq_v"), sem("seq_a"), sem("seq_g")
        small_in, x_in_done, stored = sem("small_in"), sem("x_in_done"), sem("stored")
        consts, trig, c_exp, c_done = sem("consts"), sem("trig"), sem("c_exp"), sem("c_done")
        eps_set, dist_done, residue_done = sem("eps_set"), sem("dist_done"), sem("residue_done")
        vec_done, lam_dot, lam_exp, trig_done = sem("vec_done"), sem("lam_dot"), sem("lam_exp"), sem("trig_done")

        block = ctx.enter_context(nc.Block())

        @block.sync
        def _(sp):
            n = Counts()

            def weight_piece():
                n["w"].up()
                s = (n["w"].n - 1) % SLOTS
                sp.wait_ge(lo_done, n["w"]())
                at = n["w"](n["w"].n - 1)
                src = wv[at] if isinstance(at, int) else wv[bass.ds(at, 1), :, :].rearrange("a p c -> p (a c)")
                sp.dma_start(w_raw[:, s, :], src).then_inc(raw_in[s], 16)

            def ada_piece():
                n["ada"].up()
                s = (n["ada"].n - 1) % ADA_SLOTS
                sp.wait_ge(ada_used, n["ada"]())
                at = n["ada"](n["ada"].n - 1)
                src = av[at] if isinstance(at, int) else av[bass.ds(at, 1), :, :].rearrange("a p c -> p (a c)")
                sp.dma_start(ada_raw[:, s, :], src).then_inc(ada_in[s], 16)

            def bias_row():
                n["sec"].up()
                sp.wait_ge(acc_full, n["sec"]())
                at = n["sec"](n["sec"].n - 1)
                src = ada_bias_in[at:at + 1, :] if isinstance(at, int) else ada_bias_in[bass.ds(at, 1), :]
                sp.dma_start(bias_sb[:, :], src).then_inc(bias_in, 16)

            def chunk(ch, pieces, ada=()):
                for j in range(pieces):
                    weight_piece()
                    if (ch, j) in ada:
                        ada_piece()

            sp.dma_start(cols_in[0:96, :], vecs_in).then_inc(small_in, 16)
            sp.dma_start(pos_i[:, :], pos_in).then_inc(small_in, 16)
            sp.dma_start(gains[:, :], gains_in.partition_broadcast(P)).then_inc(small_in, 16)
            sp.dma_start(subg[:, :], subg_in.partition_broadcast(P)).then_inc(small_in, 16)
            sp.dma_start(st_a[:, 0:NC], lamb_in.partition_broadcast(P)).then_inc(small_in, 16)
            sp.dma_start(xs[:, :, :], x_in.rearrange("(t p) d -> p t d", p=P)).then_inc(x_in_done, 16)
            with repeat(sp, 2, n, sec=1, ada=KT):
                bias_row()
                for _ in range(KT):
                    ada_piece()
            with repeat(sp, GROUPS, n, sec=1, ada=KT, w=6 * PIECES):
                bias_row()
                for ch in range(6):
                    chunk(ch, PIECES, ADA_QKV)
            for ch in range(4):
                chunk(ch, PIECES // 2)
            with repeat(sp, 4, n, sec=1, ada=KT, w=8 * PIECES):
                bias_row()
                for ch in range(8):
                    chunk(ch, PIECES, ADA_MLP0)
            with repeat(sp, 4, n, sec=1, ada=KT, w=4 * PIECES):
                bias_row()
                for ch in range(4):
                    chunk(ch, PIECES, ADA_FOUR)
            bias_row()
            with repeat(sp, 4, n, ada=4, w=8 * PIECES):
                for ch in range(8):
                    chunk(ch, PIECES, ADA_MLP1)
            sp.wait_ge(x_done, 4)
            sp.dma_start(out.rearrange("(t p) d -> p t d", p=P), xs[:, :, :]).then_inc(stored, 16)
            sp.wait_ge(stored, 16)

        @block.tensor
        def _(pe):
            n = Counts()

            def claim_tr(b):
                n[f"tr{b}"].up()
                pe.wait_ge(tr_free[b], n[f"tr{b}"]())

            def claim_main(par):
                n[f"ro{par}"].up()
                pe.wait_ge(read_out[par], n[f"ro{par}"]())

            def gemm(par, pairs, hi, lo, side=None, ready=None):
                claim_main(par)
                for j in range(pairs):
                    n["w"].up()
                    s = (n["w"].n - 1) % SLOTS
                    if ready:
                        ready(j)
                    pe.wait_ge(lo_done, n["w"](n["w"].n + SLOTS))
                    for k in range(PK):
                        kt = PK * j + k
                        wc = slice(k * NC, (k + 1) * NC)
                        for t in range(T):
                            acc_ps, tc = main[par][t], slice(t * P, (t + 1) * P)
                            pe.matmul(acc_ps[:, :], hi[:, kt, tc], w_hi[:, s, wc], start=(kt == 0), stop=False)
                            pe.matmul(acc_ps[:, :], hi[:, kt, tc], w_lo[:, s, wc], start=False, stop=False)
                            last = pe.matmul(acc_ps[:, :], lo[:, kt, tc], w_hi[:, s, wc], start=False,
                                             stop=(kt == PK * pairs - 1))
                    last.then_inc(mm_done, 1)
                    for step in (side or {}).get(j, ()):
                        step()

            def pair_transposes(b, source):
                for k in range(PK):
                    for t in range(T):
                        at = k * T * P + t * P
                        last = pe.transpose(tr[b][:, at:at + P], source(k, t), ident[:, :])
                return last

            def build(pairs, staged_rows=True, source=None, modulate=True):
                first = [n["tr0"].n, n["tr1"].n]
                split_before = n["split"].n
                n["split"].up(pairs if modulate else 0)
                for j in range(pairs):
                    claim_tr(j % 2)
                    if staged_rows:
                        n["staged"].up()
                        pe.wait_ge(staged, n["staged"]())
                        at = (j % 2) * NC
                        last = pair_transposes(
                            j % 2, lambda k, t: st_a[:, at + (t * PK + k) * P:at + (t * PK + k + 1) * P])
                    else:
                        last = pair_transposes(j % 2, lambda k, t: source(PK * j + k, t))
                    last.then_inc(hT_full, 1)

                def ready(j):
                    if modulate:
                        pe.wait_ge(hT_split, split_before + j + 1)
                    else:
                        pe.wait_ge(tr_free[j % 2], first[j % 2] + j // 2 + 2)
                return ready

            def sum_columns():
                n["sec"].up()
                pe.wait_ge(acc_full, n["sec"](n["sec"].n + 1))
                claim_tr(0)
                for k in range(KT):
                    last = pe.matmul(tr[0][:, k:k + 1], acc[:, k * P:(k + 1) * P], ones[:, 0:1], start=True, stop=True)
                last.then_inc(col_full, 1)

            def sum_rows(new):
                n["sec"].up(new)
                pe.wait_ge(acc_full, n["sec"](n["sec"].n + 1))
                for c in range(4):
                    claim_tr(c % 2)
                    pe.matmul(tr[c % 2][:, :], ones[:, :], acc_rows[:, c, :], start=True, stop=True).then_inc(row_full, 1)

            def qk_transposes():
                pe.wait_ge(roped, n["roped"].up())
                for t in range(T):
                    claim_tr(t)
                    for m in range(MAPS):
                        last = pe.transpose(tr[t][:, m * P:(m + 1) * P], sta[:, t, m * P:(m + 1) * P], ident[:, :])
                    last.then_inc(qk_full, 1)

            def scores(m, q0=0):
                def step():
                    if m == 0:
                        for b in range(2):
                            pe.wait_ge(tr_free[b], n[f"tr{b}"](n[f"tr{b}"].n + 1))
                    pe.wait_ge(sc_free, n["sc"].up())
                    q, k = qT[:, q0 + m, :], kT[:, m, :]
                    pe.matmul(sc[:, 0:P], q[:, 0:P], k[:, 0:P], start=True, stop=True)
                    pe.matmul(sc[:, P:3 * P], q[:, P:2 * P], k[:, :], start=True, stop=True).then_inc(sc_full, 1)
                return step

            def p_transposes(i, m, ready, name):
                def step():
                    pe.wait_ge(ready, n[name].up())
                    claim_tr(i)
                    for c in range(3):
                        last = pe.transpose(tr[i][:, c * P:(c + 1) * P], sm[:, m, c * P:(c + 1) * P], ident[:, :])
                    last.then_inc(pt_full, 1)
                return step

            def pv(i, width, at, v0):
                a, b = ov[:, at:at + width], ov[:, at + width:at + 2 * width]
                pe.matmul(a, pT[:, i, 0:P], vv[:, 0, v0:v0 + width], start=True, stop=True)
                pe.matmul(b, pT[:, i, P:2 * P], vv[:, 0, v0:v0 + width], start=True, stop=False)
                return pe.matmul(b, pT[:, i, 2 * P:3 * P], vv[:, 1, v0:v0 + width], start=False, stop=True)

            def wait_pt(i, later=0):
                pe.wait_ge(tr_free[i], n[f"tr{i}"](n[f"tr{i}"].n + 1 - later))

            def values_ready(par, back):
                pe.wait_ge(read_out[par], n[f"ro{par}"](n[f"ro{par}"].n + 1 - back))

            def pv_pair(pair, par, back):
                def step():
                    pe.wait_ge(ov_free, n["ov"].up())
                    values_ready(par, back)
                    for i in range(2):
                        wait_pt(i)
                        last = pv(i, HD, 2 * HD * i, (2 * pair + i) * HD)
                    last.then_inc(ov_full, 1)
                return step

            def pv_head(h, back, later=0):
                def step():
                    pe.wait_ge(ov_free, n["ov"].up())
                    values_ready(1, back)
                    wait_pt(h, later)
                    pv(h, 2 * HD, 0, h * 2 * HD).then_inc(ov_full, 1)
                return step

            def attn_a(par, back):
                pt = [[p_transposes(i, 2 * pair + i, p_done, "p") for i in range(2)] for pair in range(2)]
                return ({m: [scores(m)] for m in range(MAPS)},
                        {0: pt[0], 1: [pv_pair(0, par, back)], 2: pt[1], 3: [pv_pair(1, par, back)]})

            def attn_b(q0, back):
                pt = [p_transposes(h, 2 * h, mix_done, "mix") for h in range(2)]
                return ({m: [scores(m, q0)] for m in range(MAPS)},
                        {1: pt, 2: [pv_head(0, back)], 4: [pv_head(1, back, back)]})

            def also(side, j, step):
                side = dict(side)
                side[j] = side.get(j, []) + [step]
                return side

            def all_of(*sides):
                for side in sides:
                    for j in sorted(side):
                        for step in side[j]:
                            step()

            pe.sem_inc(mm_done, SLOTS)
            pe.wait_ge(consts, 2)
            pe.wait_ge(small_in, 16 * 5)
            claim_tr(0)
            pe.transpose(tr[0][:, 0:96], cols_in[0:96, :], ident[0:96, 0:96]).then_inc(vec_full, 1)
            with repeat(pe, 2, n, sec=1, tr0=1):
                sum_columns()

            h = (PIECES, hT_hi, hT_lo)
            ready = build(PIECES)
            for j in range(PIECES):
                ready(j)
            with repeat(pe, GROUPS, n, sec=1, w=6 * PIECES, ro0=3, ro1=3, roped=4, tr0=9, tr1=8, sc=8, p=8, ov=4):
                gemm(0, *h)
                gemm(1, *h, side={3: [qk_transposes]})
                gemm(0, *h, side={3: [qk_transposes]})
                gemm(1, *h)
                first, second = attn_a(0, 1)
                gemm(0, *h, side=also(first, 3, qk_transposes))
                gemm(1, *h, side=also(second, 3, qk_transposes))
                all_of(*attn_a(1, 0))
                sum_columns()
            sum_rows(0)
            ready = build(PIECES // 2, modulate=False)
            for ch in range(4):
                gemm(ch % 2, PIECES // 2, hT_hi, hT_lo, ready=ready if ch == 0 else None)

            def mlp(in_loop):
                ready = build(PIECES)
                for j in range(PIECES):
                    ready(j)
                rises = dict(w=8 * PIECES, ro0=4, ro1=4, tr0=4, tr1=4)
                if in_loop:
                    rises.update(sec=1, tr0=5)
                with repeat(pe, 4, n, **rises):
                    first = [n["tr0"].n, n["tr1"].n]

                    def hidden(par):
                        def step():
                            pe.wait_ge(read_out[par], n[f"ro{par}"](n[f"ro{par}"].n + 1))
                            for kp in range(2):
                                claim_tr(kp)
                                pair_transposes(
                                    kp, lambda k, t: stb[:, t, (PK * kp + k) * P:(PK * kp + k + 1) * P]
                                ).then_inc(mid_full, 1)
                        return step

                    def mid_ready(j):
                        pe.wait_ge(tr_free[j % 2], n[f"tr{j % 2}"](first[j % 2] + j // 2 + 2))

                    for c in range(4):
                        gemm(c % 2, *h, side={2: [hidden(1 - c % 2)]} if c else None)
                    for c in range(4):
                        gemm(c % 2, PIECES, mid_hi, mid_lo, side={2: [hidden(1)]} if c == 0 else None,
                             ready=mid_ready if c == 0 else None)
                    if in_loop:
                        sum_columns()
                sum_rows(0 if in_loop else 1)

            mlp(True)

            ready = build(PIECES)
            for ch in range(4):
                gemm(ch % 2, *h, side={3: [qk_transposes]} if ch else None, ready=ready if ch == 0 else None)
            qk_transposes()
            sum_columns()
            ready = build(PIECES)
            first = second = {}
            for u in range(4):
                gemm(0, *h, side=first, ready=ready if u == 0 else None)
                gemm(1, *h, side=also(second, 3, qk_transposes))
                first, second = attn_b(u * MAPS, 1)
                if u % 2:
                    sum_columns()
            all_of(*attn_b(3 * MAPS, 0))
            pe.wait_ge(ov_free, n["ov"](n["ov"].n + 1))
            ready = build(PIECES, False, lambda kt, t: head_out[:, kt // 2, t, (kt % 2) * P:(kt % 2 + 1) * P], False)
            for ch in range(4):
                gemm(ch % 2, *h, ready=ready if ch == 0 else None)
            sum_rows(1)
            mlp(False)

        @block.scalar
        def _(act):
            n = Counts()

            def split():
                n["w"].up()
                w, base = n["w"].n, n["w"].base
                s = (w - 1) % SLOTS
                fills = ((w - 1) // SLOTS + 1) * 16
                act.wait_ge(raw_in[s], fills if base is None else base * (16 // SLOTS) + fills)
                act.wait_ge(mm_done, n["w"]())
                act.activation(w_hi[:, s, :], w_raw[:, s, :], ACT.Copy).then_inc(hi_done, 1)

            def chunk(pieces, side=None):
                for j in range(pieces + 1):
                    for step in (side or {}).get(j, ()):
                        step()
                    if j < pieces:
                        split()

            def ended(back):
                act.wait_ge(mm_done, n["w"](n["w"].n + SLOTS - back))

            def chained(ins):
                ins.then_inc(seq_a, 1)
                act.wait_ge(seq_a, n["seq"].up())

            def qk_stats(par, back=4):
                def step():
                    ended(back)
                    for t in range(T):
                        for m in range(MAPS):
                            i = t * MAPS + m
                            last = act.activation(st_b[:, i * P:(i + 1) * P], main[par][t][:, m * P:(m + 1) * P],
                                                  ACT.Square, accum_out=ssq[:, i:i + 1])
                    chained(last)
                    act.activation(rms[:, :], ssq[:, :], ACT.Sqrt, bias=eps_t[:, :], scale=1.0 / HD).then_inc(rms_done, 1)
                return step

            def move_tile0(dst):
                def step():
                    n["qk"].up(2)
                    act.wait_ge(qk_full, n["qk"](n["qk"].n - 1))
                    act.activation(dst[:, :, 0:P], tr[0][:, :].rearrange("p (m n) -> p m n", m=MAPS),
                                   ACT.Copy).then_inc(tr_free[0], 1)
                return step

            def values(par, back=4):
                def step():
                    ended(back)
                    act.activation(vv[:, 0, :], main[par][0][:, :], ACT.Copy)
                    act.activation(vv[:, 1, :], main[par][1][:, :], ACT.Copy).then_inc(read_out[par], 1)
                return step

            def exps(running):
                def step():
                    act.wait_ge(smx_done, n["smx"].up())
                    if running:
                        act.activation(corr8[:, :], diff8[:, :], ACT.Exp)
                    for m in range(MAPS):
                        act.activation(sm[:, m, 0:P], sm[:, m, 0:P], ACT.Exp, bias=neg8[:, 2 * m:2 * m + 1],
                                       accum_out=d8[:, 2 * m:2 * m + 1])
                        act.activation(sm[:, m, P:3 * P], sm[:, m, P:3 * P], ACT.Exp, bias=neg8[:, 2 * m + 1:2 * m + 2],
                                       accum_out=d8[:, 2 * m + 1:2 * m + 2]).then_inc(p_done, 1)
                return step

            def move_pt():
                n["pt"].up(2)
                act.wait_ge(pt_full, n["pt"](n["pt"].n - 1))
                act.activation(pT[:, 0, :], tr[0][:, 0:3 * P], ACT.Copy).then_inc(tr_free[0], 1)

            def sub_stats():
                act.wait_ge(ov_full, n["ov"].up())
                act.activation(st_b[:, 0:2 * HD], ov[:, 0:2 * HD], ACT.Square, accum_out=ssv[:, 0:1])
                chained(act.activation(st_b[:, 2 * HD:4 * HD], ov[:, 2 * HD:4 * HD], ACT.Square, accum_out=ssv[:, 1:2]))
                act.activation(rmsv[:, :], ssv[:, :], ACT.Sqrt, bias=eps_t[:, :],
                               scale=1.0 / (2 * HD)).then_inc(sub_rms, 1)

            def x_stats():
                act.activation(junk[:, 0, :], xs[:, 0, :], ACT.Square, accum_out=ssx[:, 0:1])
                chained(act.activation(junk[:, 1, :], xs[:, 1, :], ACT.Square, accum_out=ssx[:, 1:2]))
                act.activation(rmsx[:, :], ssx[:, :], ACT.Sqrt, bias=eps_t[:, :], scale=1.0 / D).then_inc(x_rms, 1)

            def build(pairs, modulate=True):
                if n["w"].n:
                    ended(0)
                for j in range(pairs):
                    dst = hT_hi[:, PK * j:PK * (j + 1), :].rearrange("p k n -> p (k n)")
                    if modulate:
                        act.wait_ge(modulated, n["modulated"].up())
                        act.activation(dst, stb[:, j % 2, :], ACT.Copy).then_inc(hi_part, 1)
                    else:
                        act.wait_ge(hT_full, n["hT"].n + j + 1)
                        act.activation(dst, tr[j % 2][:, :], ACT.Copy).then_inc(hi_part, 1)
                n["hT"].up(pairs)

            act.wait_ge(eps_set, 1)
            act.wait_ge(vec_done, 1)
            act.activation(c_act[:, :], vec[:, V_C, :], ACT.Exp, scale=-1.0).then_inc(c_exp, 1)
            act.wait_ge(lam_dot, 1)
            act.activation(lam[:, 2:4], lam[:, 0:2], ACT.Exp).then_inc(lam_exp, 1)
            act.wait_ge(trig, 1)
            act.activation(sin[:, :], small[:, 0:T * HALF], ACT.Sin)
            act.activation(cos[:, :], small[:, T * HALF:2 * T * HALF], ACT.Sin, bias=hpi_t[:, :],
                           scale=-1.0).then_inc(trig_done, 1)
            act.wait_ge(x_in_done, 16)
            x_stats()
            build(PIECES)
            q4, k4 = qT[:, 0:MAPS, :], kT[:, :, :]
            with repeat(act, GROUPS, n, w=6 * PIECES, seq=4, qk=8, smx=2, pt=8):
                chunk(PIECES)
                chunk(PIECES, {4: [qk_stats(0)], 8: [move_tile0(q4)]})
                chunk(PIECES, {4: [qk_stats(1)], 8: [move_tile0(k4)]})
                chunk(PIECES, {4: [values(0)]})
                chunk(PIECES, {4: [qk_stats(1)], 8: [move_tile0(q4), exps(True)]})
                chunk(PIECES, {4: [qk_stats(0), move_pt], 6: [move_pt], 8: [move_tile0(k4)]})
                values(1, 0)()
                exps(True)()
                move_pt()
                move_pt()
            build(PIECES // 2, False)
            for ch in range(4):
                chunk(PIECES // 2)

            def mlp(x_updates):
                act.wait_ge(x_done, x_updates)
                x_stats()
                build(PIECES)
                with repeat(act, 4, n, w=8 * PIECES, mid=8):
                    def relu(par):
                        def step():
                            ended(4)
                            for t in range(T):
                                last = act.activation(sta[:, t, :], main[par][t][:, :], ACT.Relu)
                            last.then_inc(relu_done, 1)
                        return step

                    def mid(c):
                        def step():
                            for kp in range(2):
                                act.wait_ge(mid_full, n["mid"].up())
                                kt = 4 * c + PK * kp
                                act.activation(mid_hi[:, kt:kt + PK, :],
                                               tr[kp][:, :].rearrange("p (k n) -> p k n", k=PK),
                                               ACT.Copy).then_inc(hi_part, 1)
                        return step

                    for c in range(4):
                        chunk(PIECES, {4: [relu(1 - c % 2)], 7: [mid(c - 1)]} if c else None)
                    for c in range(4):
                        chunk(PIECES, {4: [relu(1)], 7: [mid(3)]} if c == 0 else None)

            mlp(1)
            act.wait_ge(x_done, 2)
            x_stats()
            build(PIECES)
            for ch in range(4):
                chunk(PIECES, {4: [qk_stats(1 - ch % 2)],
                               8: [move_tile0(qT[:, (ch - 1) * MAPS:ch * MAPS, :])]} if ch else None)
            qk_stats(1, 0)()
            move_tile0(qT[:, 3 * MAPS:4 * MAPS, :])()
            build(PIECES)
            n["ov"].up(4 * GROUPS)
            for u in range(4):
                chunk(PIECES, {4: [values(1)], 8: [exps(False)]} if u else None)
                chunk(PIECES, {4: [qk_stats(0)] + [move_pt] * (u > 0), 6: [sub_stats] * (u > 0),
                               8: [move_tile0(k4)] + [sub_stats] * (u > 0)})
            values(1, 0)()
            exps(False)()
            move_pt()
            sub_stats()
            sub_stats()
            build(PIECES, False)
            for ch in range(4):
                chunk(PIECES)
            mlp(3)

        @block.vector
        def _(dve):
            n = Counts()

            def chained(ins):
                ins.then_inc(seq_v, 1)
                dve.wait_ge(seq_v, n["seq"].up())

            def split():
                n["w"].up()
                s = (n["w"].n - 1) % SLOTS
                dve.wait_ge(hi_done, n["w"]())
                dve.tensor_tensor(w_lo[:, s, :], w_raw[:, s, :], w_hi[:, s, :].bitcast(F32),
                                  ALU.subtract).then_inc(lo_done, 1)

            def ada_piece(kt, first=False):
                n["ada"].up()
                a, base = n["ada"].n, n["ada"].base
                s = (a - 1) % ADA_SLOTS
                fills = ((a - 1) // ADA_SLOTS + 1) * 16
                dve.wait_ge(ada_in[s], fills if base is None else base * (16 // ADA_SLOTS) + fills)
                c = c_act[:, kt:kt + 1] if isinstance(kt, int) else c_act[:, bass.ds(kt, 1)]
                if first:
                    ins = dve.tensor_scalar(acc[:, :], ada_raw[:, s, :], c, None, ALU.mult)
                else:
                    dve.wait_ge(ada_used, n["ada"](a - 1 + ADA_SLOTS))
                    ins = dve.scalar_tensor_tensor(out=acc[:, :], in0=ada_raw[:, s, :], scalar=c, in1=acc[:, :],
                                                   op0=ALU.mult, op1=ALU.add)
                ins.then_inc(ada_used, 1)

            def add_bias():
                n["sec"].up()
                sec = n["sec"]
                dve.wait_ge(bias_in, 16 * sec.n if sec.base is None else sec.base * 16 + 16 * sec.n)
                dve.wait_ge(ada_used, n["ada"](n["ada"].n + ADA_SLOTS))
                dve.tensor_tensor(acc[0:1, :], acc[0:1, :], bias_sb[:, :], ALU.add).then_inc(acc_full, 1)

            def section_piece(k):
                ada_piece(k, first=(k == 0))
                if k == KT - 1:
                    add_bias()

            def chunk(ch, pieces, side=None, ada=()):
                for j in range(pieces + 1):
                    for step in (side or {}).get(j, ()):
                        step()
                    if j < pieces:
                        split()
                        if (ch, j) in ada:
                            section_piece(ada.index((ch, j)))

            def move_columns():
                dve.wait_ge(col_full, n["col"].up())
                at = n["sec"](n["sec"].n - 1)
                dst = modc[:, at, :] if isinstance(at, int) else modc[:, bass.ds(at, 1), :].rearrange("p a k -> p (a k)")
                dve.tensor_copy(dst, tr[0][:, 0:KT]).then_inc(tr_free[0], 1)

            def move_rows():
                for c in range(4):
                    dve.wait_ge(row_full, n["row"].up())
                    dve.tensor_copy(acc_rows[:, c, :], tr[c % 2][:, :]).then_inc(tr_free[c % 2], 1)

            def settled():
                chained(dve.memset(scratch[:, :], 0.0))

            def norm(par, gain):
                def step():
                    dve.wait_ge(rms_done, n["rms"].up())
                    chained(dve.reciprocal(rstd[:, :], rms[:, :]))
                    for t in range(T):
                        for m in range(MAPS):
                            i = t * MAPS + m
                            last = dve.scalar_tensor_tensor(
                                out=sta[:, t, m * P:(m + 1) * P], in0=main[par][t][:, m * P:(m + 1) * P],
                                scalar=rstd[:, i:i + 1], in1=gain(m), op0=ALU.mult, op1=ALU.mult)
                    last.then_inc(read_out[par], 1)
                return step

            def move_tile1(dst):
                def step():
                    dve.wait_ge(qk_full, n["qk"].up(2))
                    dve.tensor_copy(dst[:, :, P:2 * P],
                                    tr[1][:, :].rearrange("p (m n) -> p m n", m=MAPS)).then_inc(tr_free[1], 1)
                return step

            def mask_scores(m, mask):
                def step():
                    dve.wait_ge(sc_full, n["sc"].up())
                    dve.memset(scratch[:, :], 0.0)
                    for t, c in ((0, slice(0, P)), (1, slice(P, 3 * P))):
                        last = dve.tensor_tensor_reduce(sm[:, m, c], sc[:, c], mask[:, c], SCALE, NEG, ALU.add,
                                                        ALU.max, m8[:, 2 * m + t:2 * m + t + 1])
                    last.then_inc(sc_free, 1)
                return step

            def running_max(quad):
                def step():
                    dve.wait_ge(sc_free, n["sc"](n["sc"].n + 1))
                    chained(dve.tensor_tensor(mn8[:, :], m8[:, :], m_old[:, quad, :], ALU.max))
                    dve.tensor_scalar(neg8[:, :], mn8[:, :], -1.0, None, ALU.mult)
                    chained(dve.tensor_tensor(diff8[:, :], m_old[:, quad, :], mn8[:, :], ALU.subtract))
                    dve.tensor_copy(m_old[:, quad, :], mn8[:, :]).then_inc(smx_done, 1)
                return step

            def negate_max():
                dve.wait_ge(sc_free, n["sc"](n["sc"].n + 1))
                dve.tensor_scalar(neg8[:, :], m8[:, :], -1.0, None, ALU.mult).then_inc(smx_done, 1)

            def move_pt():
                dve.wait_ge(pt_full, n["pt"].up(2))
                dve.tensor_copy(pT[:, 1, :], tr[1][:, 0:3 * P]).then_inc(tr_free[1], 1)

            def merge(quad, pair):
                def step():
                    dve.wait_ge(ov_full, n["ov"].up())
                    if pair == 1:
                        chained(dve.tensor_tensor(den[:, quad, :], den[:, quad, :], corr8[:, :], ALU.mult))
                        dve.tensor_tensor(den[:, quad, :], den[:, quad, :], d8[:, :], ALU.add)
                    for i in range(2):
                        for t in range(T):
                            m = 2 * pair + i
                            o = group_out[:, quad * MAPS + m, t, :]
                            last = dve.scalar_tensor_tensor(
                                out=o, in0=o, scalar=corr8[:, 2 * m + t:2 * m + t + 1],
                                in1=ov[:, (i * T + t) * HD:(i * T + t + 1) * HD], op0=ALU.mult, op1=ALU.add)
                    last.then_inc(ov_free, 1)
                return step

            def mix():
                dve.wait_ge(p_done, n["p"].up(MAPS))
                chained(dve.reciprocal(r8[:, :], d8[:, :]))
                r = r8[:, :].rearrange("p (h c t) -> p h c t", c=2, t=T)
                chained(dve.tensor_scalar(r[:, :, 1, :], r[:, :, 1, :], lam[:, 5:6], None, ALU.mult))
                tiles = [(h, t, slice(0, P) if t == 0 else slice(P, 3 * P)) for h in range(2) for t in range(T)]
                for h, t, c in tiles:
                    last = dve.tensor_scalar(sm[:, 2 * h, c], sm[:, 2 * h, c], r[:, h, 0, t:t + 1], None, ALU.mult)
                chained(last)
                for h, t, c in tiles:
                    last = dve.scalar_tensor_tensor(out=sm[:, 2 * h, c], in0=sm[:, 2 * h + 1, c],
                                                    scalar=r[:, h, 1, t:t + 1], in1=sm[:, 2 * h, c],
                                                    op0=ALU.mult, op1=ALU.add)
                    if t == 1:
                        last.then_inc(mix_done, 1)

            def sub_norm(head):
                def step():
                    dve.wait_ge(sub_rms, n["sub"].up())
                    chained(dve.reciprocal(rstdv[:, :], rmsv[:, :]))
                    chained(dve.tensor_scalar(rstdv[:, :], rstdv[:, :], 1.0 - LAM_INIT, None, ALU.mult))
                    for t in range(T):
                        last = dve.scalar_tensor_tensor(
                            out=head_out[:, head, t, :], in0=ov[:, t * 2 * HD:(t + 1) * 2 * HD],
                            scalar=rstdv[:, t:t + 1], in1=subg[:, :], op0=ALU.mult, op1=ALU.mult)
                    last.then_inc(ov_free, 1)
                return step

            def build(pairs, sections=None, g=None):
                if sections:
                    settled()
                    scale = modc[:, sections[0], :]
                    dve.scalar_tensor_tensor(out=scale, in0=scale, scalar=1.0, in1=vec[:, V_G + g, :], op0=ALU.add,
                                             op1=ALU.mult).then_inc(mod_done, 1)
                    dve.wait_ge(mod_done, n["mod"].up())

                split_before = n["split"].n
                n["split"].up(pairs if sections else 0)

                def modulate(j):
                    dve.wait_ge(hT_full, n["hT"].up())
                    if split_before + j > 1:
                        dve.wait_ge(hT_split, split_before + j - 1)
                    for k in range(PK):
                        g_col, s_col = (modc[:, x, PK * j + k:PK * j + k + 1] for x in sections)
                        last = dve.tensor_scalar(stb[:, j % 2, k * T * P:(k + 1) * T * P],
                                                 tr[j % 2][:, k * T * P:(k + 1) * T * P], g_col, s_col, ALU.mult, ALU.add)
                    return last

                def low(j, source):
                    dve.wait_ge(hi_part, n["hi"].up())
                    return dve.tensor_tensor(hT_lo[:, PK * j:PK * (j + 1), :].rearrange("p k n -> p (k n)"), source,
                                             hT_hi[:, PK * j:PK * (j + 1), :].rearrange("p k n -> p (k n)").bitcast(F32),
                                             ALU.subtract)

                if not sections:
                    for j in range(pairs):
                        n["hT"].up()
                        low(j, tr[j % 2][:, :]).then_inc(tr_free[j % 2], 1)
                    return
                for j in range(pairs + 1):
                    if j < pairs:
                        modulate(j).then_inc(modulated, 1)
                        dve.memset(marks[:, j:j + 1], 0.0).then_inc(tr_free[j % 2], 1)
                    if j:
                        low(j - 1, stb[:, (j - 1) % 2, :]).then_inc(hT_split, 1)

            def x_recip():
                dve.wait_ge(x_rms, n["xr"].up())
                dve.reciprocal(rstdx[:, :], rmsx[:, :]).then_inc(x_rstd, 1)

            def ended(back):
                dve.wait_ge(mm_done, n["w"](n["w"].n + SLOTS - back))

            def to_work(par, c, add, back=4):
                def step():
                    ended(back)
                    for t in range(T):
                        dst, src = y[:, t, c * NC:(c + 1) * NC], main[par][t][:, :]
                        last = dve.tensor_tensor(dst, src, dst, ALU.add) if add else dve.tensor_copy(dst, src)
                    last.then_inc(read_out[par], 1)
                return step

            def gated_update():
                parts = [(c, t) for c in range(4) for t in range(T)]
                settled()
                for i in range(len(parts) + 1):
                    if i < len(parts):
                        if i >= 2:
                            dve.wait_ge(seq_v, n["seq"]())
                        c, t = parts[i]
                        dve.tensor_tensor(stb[:, i % 2, :], y[:, t, c * NC:(c + 1) * NC], acc_rows[:, c, :],
                                          ALU.mult).then_inc(seq_v, 1)
                        n["seq"].up()
                    if i:
                        c, t = parts[i - 1]
                        xc = xs[:, t, c * NC:(c + 1) * NC]
                        dve.wait_ge(seq_v, n["seq"](n["seq"].n - (i < len(parts))))
                        last = dve.tensor_tensor(xc, xc, stb[:, (i - 1) % 2, :], ALU.add)
                        if i < len(parts):
                            last.then_inc(seq_v, 1)
                            n["seq"].up()
                last.then_inc(x_done, 1)

            dve.sem_inc(lo_done, SLOTS)
            dve.sem_inc(ada_used, ADA_SLOTS)
            for s in (acc_full, *read_out, *tr_free, sc_free, ov_free):
                dve.sem_inc(s, 1)
            dve.memset(eps_t[:, :], EPS)
            dve.memset(hpi_t[:, :], math.pi / 2).then_inc(eps_set, 1)
            freq = np.float32(500000.0) ** (-np.arange(0, ROT, 2, dtype=np.float32) / np.float32(ROT))
            for i in range(HALF):
                last = dve.memset(inv_freq[:, i:i + 1], float(freq[i]))
            chained(last)
            dve.wait_ge(dist_done, 1)
            for g, low_bits in enumerate((3, 15)):
                last = dve.tensor_scalar(residue_i[:, g * P:(g + 1) * P], dist[:, :], low_bits, None, ALU.bitwise_and)
            chained(last)
            dve.tensor_scalar(residue[:, :], residue_i[:, :], 0.0, NEG, ALU.is_gt, ALU.mult).then_inc(residue_done, 1)
            dve.wait_ge(small_in, 16 * 5)
            dve.wait_ge(vec_full, 1)
            dve.tensor_copy(vec[:, :, :].rearrange("p a b -> p (a b)"), tr[0][:, 0:96]).then_inc(tr_free[0], 1)
            dve.wait_ge(tr_free[0], 2)
            dve.sem_inc(vec_done, 1)
            dve.wait_ge(c_exp, 1)
            chained(dve.tensor_scalar(c_act[:, :], c_act[:, :], 1.0, None, ALU.add))
            chained(dve.reciprocal(c_act[:, :], c_act[:, :]))
            chained(dve.tensor_tensor(c_act[:, :], c_act[:, :], vec[:, V_C, :], ALU.mult))
            lm = st_a[:, 0:NC].rearrange("p (a b) -> p a b", a=4)
            dve.tensor_tensor_reduce(st_b[:, 0:P], lm[:, 0, :], lm[:, 1, :], 1.0, 0.0, ALU.mult, ALU.add, lam[:, 0:1])
            dve.tensor_tensor_reduce(st_b[:, P:2 * P], lm[:, 2, :], lm[:, 3, :], 1.0, 0.0, ALU.mult, ALU.add,
                                     lam[:, 1:2]).then_inc(lam_dot, 1)
            chained(dve.tensor_copy(pos_f[:, :], pos_i[:, :]))
            ang, mag = small[:, 0:T * HALF], small[:, T * HALF:2 * T * HALF]
            for t in range(T):
                last = dve.tensor_scalar(ang[:, t * HALF:(t + 1) * HALF], inv_freq[:, :], pos_f[:, t:t + 1], None, ALU.mult)
            chained(last)
            magic = 1.5 * 2.0 ** 23
            chained(dve.tensor_scalar(turns[:, :], ang, 1.0 / (2 * math.pi), magic, ALU.mult, ALU.add))
            chained(dve.tensor_scalar(turns[:, :], turns[:, :], -magic, None, ALU.add))
            c1 = 6.28125
            c2 = round((2 * math.pi - c1) * 2 ** 20) / 2 ** 20
            for part in (c1, c2, 2 * math.pi - c1 - c2):
                chained(dve.scalar_tensor_tensor(out=ang, in0=turns[:, :], scalar=-part, in1=ang, op0=ALU.mult,
                                                 op1=ALU.add))
            chained(dve.tensor_scalar(ang, ang, 3.1415925, -3.1415925, ALU.min, ALU.max))
            chained(dve.tensor_scalar(mag, ang, -1.0, None, ALU.mult))
            dve.tensor_tensor(mag, mag, ang, ALU.max).then_inc(trig, 1)
            dve.wait_ge(lam_exp, 1)
            chained(dve.tensor_tensor(lam[:, 4:5], lam[:, 3:4], lam[:, 2:3], ALU.subtract))
            chained(dve.tensor_scalar(lam[:, 5:6], lam[:, 4:5], -LAM_INIT, None, ALU.add))

            with repeat(dve, 2, n, ada=KT, sec=1, col=1):
                for k in range(KT):
                    section_piece(k)
                move_columns()
            x_recip()
            build(PIECES, (S_SCALE_T0, S_SHIFT_T0), 0)
            q4, k4 = qT[:, 0:MAPS, :], kT[:, :, :]

            def gain_of(i):
                return lambda m: gain_now[:, i * HD:(i + 1) * HD]

            dve.wait_ge(consts, 3)
            with repeat(dve, GROUPS, n, w=6 * PIECES, ada=KT, sec=1, col=1, seq=11, rms=4, qk=8, sc=8, pt=8, ov=4) as g:
                dve.tensor_copy(gain_now[:, 0:HD], gains[:, bass.ds(g * HD, HD)])
                dve.tensor_copy(gain_now[:, HD:2 * HD], gains[:, bass.ds(g * HD + GROUPS * HD, HD)])
                dve.tensor_copy(mask_now[:, :], masks[:, bass.ds(g, 1), :].rearrange("p a n -> p (a n)")).then_inc(seq_v, 1)
                dve.wait_ge(seq_v, n["seq"].up())
                sc4 = [mask_scores(m, mask_now) for m in range(MAPS)]
                chunk(0, PIECES, None, ADA_QKV)
                chunk(1, PIECES, {4: [norm(0, gain_of(0))], 8: [move_tile1(q4)]}, ADA_QKV)
                chunk(2, PIECES, {4: [norm(1, gain_of(1))], 8: [move_tile1(k4)]}, ADA_QKV)
                chunk(3, PIECES, None, ADA_QKV)
                chunk(4, PIECES, {4: [norm(1, gain_of(0)), sc4[0]], 5: [sc4[1]], 6: [sc4[2]], 7: [sc4[3]],
                                  8: [move_tile1(q4), running_max(0)]}, ADA_QKV)
                chunk(5, PIECES, {4: [move_pt, norm(0, gain_of(1))], 5: [merge(0, 0)], 6: [move_pt],
                                  7: [merge(0, 1)], 8: [move_tile1(k4)]}, ADA_QKV)
                for m in range(MAPS):
                    sc4[m]()
                running_max(1)()
                move_pt()
                merge(1, 0)()
                move_pt()
                merge(1, 1)()
                move_columns()
            settled()
            dve.reciprocal(rden[:, :], den[:, :, :].rearrange("p a b -> p (a b)")).then_inc(den_inv, 1)
            move_rows()
            build(PIECES // 2)
            for ch in range(4):
                chunk(ch, PIECES // 2, {4: [to_work(1 - ch % 2, ch - 1, False)]} if ch else None)
            to_work(1, 3, False, 0)()
            gated_update()

            def mlp(in_loop, sections, g):
                x_recip()
                build(PIECES, sections, g)
                rises = dict(w=8 * PIECES, relu=4, mid=8, hi=8)
                rises.update(dict(ada=KT, sec=1, col=1) if in_loop else dict(ada=4))
                if not in_loop:
                    chained(dve.memset(acc[:, :], 0.0))
                n["zero"].up()
                dve.wait_ge(work_zero, n["zero"]())
                with repeat(dve, 4, n, **rises) as i:
                    def square(par):
                        def step():
                            dve.wait_ge(relu_done, n["relu"].up())
                            for t in range(T):
                                last = dve.scalar_tensor_tensor(out=stb[:, t, :], in0=main[par][t][:, :], scalar=0.0,
                                                                in1=sta[:, t, :], op0=ALU.max, op1=ALU.mult)
                            last.then_inc(read_out[par], 1)
                        return step

                    def mid(c):
                        def step():
                            for kp in range(2):
                                dve.wait_ge(mid_full, n["mid"].up())
                                dve.wait_ge(hi_part, n["hi"].up())
                                kt = 4 * c + PK * kp
                                dve.tensor_tensor(mid_lo[:, kt:kt + PK, :],
                                                  tr[kp][:, :].rearrange("p (k n) -> p k n", k=PK),
                                                  mid_hi[:, kt:kt + PK, :].bitcast(F32),
                                                  ALU.subtract).then_inc(tr_free[kp], 1)
                        return step

                    def column(ch):
                        return lambda: ada_piece(i * 4 + ADA_MLP1.index((ch, 2)))

                    ada = ADA_MLP0 if in_loop else ()
                    for c in range(4):
                        side = {4: [square(1 - c % 2)], 7: [mid(c - 1)]} if c else {}
                        if not in_loop and (c, 2) in ADA_MLP1:
                            side[3] = [column(c)]
                        chunk(c, PIECES, side, ada)
                    for c in range(4):
                        side = {4: [to_work(1 - c % 2, c - 1, True)]} if c else {4: [square(1)], 7: [mid(3)]}
                        if not in_loop and (c + 4, 2) in ADA_MLP1:
                            side[3] = [column(c + 4)]
                        chunk(c + 4, PIECES, side, ada)
                    to_work(1, 3, True, 0)()
                    if in_loop:
                        move_columns()
                if not in_loop:
                    add_bias()
                move_rows()
                gated_update()

            mlp(True, (S_SCALE_M0, S_SHIFT_M0), 1)
            x_recip()
            build(PIECES, (S_SCALE_T1, S_SHIFT_T1), 2)

            def map_gain(row):
                return lambda m: gains[:, (row + m % 2) * HD:(row + m % 2 + 1) * HD]

            for ch in range(4):
                chunk(ch, PIECES, {4: [norm(1 - ch % 2, map_gain(8))],
                                   8: [move_tile1(qT[:, (ch - 1) * MAPS:ch * MAPS, :])]} if ch else None, ADA_FOUR)
            norm(1, map_gain(8))()
            move_tile1(qT[:, 3 * MAPS:4 * MAPS, :])()
            move_columns()
            build(PIECES, (S_SCALE_KV, S_SHIFT_KV), 4)
            n["p"].up(2 * MAPS * GROUPS)
            causal = [mask_scores(m, masks[:, 3, :]) for m in range(MAPS)]
            for u in range(4):
                c0 = 2 * (u % 2)
                if u == 0:
                    chunk(c0, PIECES, None, ADA_FOUR)
                    chunk(c0 + 1, PIECES, {4: [norm(0, map_gain(6))], 8: [move_tile1(k4)]}, ADA_FOUR)
                else:
                    chunk(c0, PIECES, {4: [causal[0]], 5: [causal[1]], 6: [causal[2]], 7: [causal[3]],
                                       8: [negate_max]}, ADA_FOUR)
                    chunk(c0 + 1, PIECES, {2: [mix], 4: [move_pt, norm(0, map_gain(6))], 6: [sub_norm(2 * u - 2)],
                                           8: [move_tile1(k4), sub_norm(2 * u - 1)]}, ADA_FOUR)
                if u % 2:
                    move_columns()
            for m in range(MAPS):
                causal[m]()
            negate_max()
            mix()
            move_pt()
            sub_norm(6)()
            sub_norm(7)()
            build(PIECES)
            for ch in range(4):
                chunk(ch, PIECES, {4: [to_work(1 - ch % 2, ch - 1, False)]} if ch else None, ADA_FOUR)
            to_work(1, 3, False, 0)()
            move_rows()
            gated_update()
            mlp(False, (S_SCALE_M1, S_SHIFT_M1), 3)

        @block.gpsimd
        def _(pool):
            n = Counts()

            def chained(ins):
                ins.then_inc(seq_g, 1)
                pool.wait_ge(seq_g, n["seq"].up())

            def stage(pairs, source):
                for j in range(pairs):
                    if n["hT"].n + j > 1:
                        pool.wait_ge(hT_full, n["hT"](n["hT"].n + j - 1))
                    for dst, src, scale in source(j, (j % 2) * NC):
                        last = pool.tensor_scalar(dst, src, scale, 1.0, ALU.mult, ALU.mult)
                    last.then_inc(staged, 1)
                n["hT"].up(pairs)

            def x_rows(j, at):
                return [(st_a[:, at + t * PK * P:at + (t + 1) * PK * P], xs[:, t, j * PK * P:(j + 1) * PK * P],
                         rstdx[:, t:t + 1]) for t in range(T)]

            def head_rows(j, at):
                return [(st_a[:, at + (t * PK + k) * P:at + (t * PK + k + 1) * P], group_out[:, PK * j + k, t, :],
                         rden[:, (PK * j + k) * T + t:(PK * j + k) * T + t + 1]) for t in range(T) for k in range(PK)]

            def rope(par):
                pool.wait_ge(read_out[par], n[f"ro{par}"](n[f"ro{par}"].n + 1))
                for t in range(T):
                    v = sta[:, t, :].rearrange("p (m e) -> p m e", m=MAPS)
                    t1, t2 = v[:, :, 0:HALF], v[:, :, HALF:ROT]
                    c = cos[:, t * HALF:(t + 1) * HALF].unsqueeze(1).to_broadcast([P, MAPS, HALF])
                    s = sin[:, t * HALF:(t + 1) * HALF].unsqueeze(1).to_broadcast([P, MAPS, HALF])
                    pool.tensor_tensor(rot[:, t, 0], t1, c, ALU.mult)
                    pool.tensor_tensor(rot[:, t, 1], t2, s, ALU.mult)
                    pool.tensor_tensor(rot[:, t, 2], t2, c, ALU.mult)
                    last = pool.tensor_tensor(rot[:, t, 3], t1, s, ALU.mult)
                chained(last)
                for t in range(T):
                    v = sta[:, t, :].rearrange("p (m e) -> p m e", m=MAPS)
                    pool.tensor_tensor(v[:, :, 0:HALF], rot[:, t, 0], rot[:, t, 1], ALU.subtract)
                    last = pool.tensor_tensor(v[:, :, HALF:ROT], rot[:, t, 2], rot[:, t, 3], ALU.add)
                last.then_inc(roped, 1)

            def passed(par):
                n[f"ro{par}"].up()

            chained(pool.memset(ident[:, :], 0.0))
            pool.affine_select(out=ident[:, :], in_=ident[:, :], compare_op=ALU.not_equal, fill=1.0, base=0,
                               pattern=[[-1, P]], channel_multiplier=1).then_inc(consts, 1)
            pool.memset(ones[:, :], 1.0).then_inc(consts, 1)
            pool.iota(dist[:, :], base=P, pattern=[[-1, P]], channel_multiplier=1).then_inc(dist_done, 1)
            pool.memset(work[:, :], 0.0)
            pool.memset(m_old[:, :, :], NEG)
            pool.memset(den[:, :, :], 0.0)
            chained(pool.memset(masks[:, :, :], 0.0))
            pool.wait_ge(residue_done, 1)
            for g in range(1, GROUPS):
                for b in range(3):
                    pool.tensor_copy(masks[:, g, b * P:(b + 1) * P], residue[:, (g - 1) * P:g * P])
            chained(pool.memset(scratch_g[:, :], 0.0))
            for g in range(4):
                for b in (0, 2):
                    last = pool.affine_select(out=masks[:, g, b * P:(b + 1) * P], in_=masks[:, g, b * P:(b + 1) * P],
                                              compare_op=ALU.is_ge, fill=NEG, base=0, pattern=[[-1, P]],
                                              channel_multiplier=1)
            last = pool.affine_select(out=masks[:, 0, P:2 * P], in_=masks[:, 0, P:2 * P], compare_op=ALU.is_ge,
                                      fill=NEG, base=0, pattern=[[1, P]], channel_multiplier=-1)
            last.then_inc(consts, 1)
            pool.wait_ge(trig_done, 1)
            pool.wait_ge(x_rstd, 1)
            stage(PIECES, x_rows)
            with repeat(pool, GROUPS, n, ro0=3, ro1=3, seq=4):
                passed(0)
                rope(0)
                passed(1)
                rope(1)
                passed(0)
                passed(1)
                rope(1)
                passed(0)
                rope(0)
                passed(1)
            pool.wait_ge(den_inv, 1)
            stage(PIECES // 2, head_rows)
            for u in range(2):
                passed(0), passed(1)

            def zero_work(x_updates):
                pool.wait_ge(x_done, x_updates)
                pool.memset(work[:, :], 0.0).then_inc(work_zero, 1)

            def mlp(x_updates, rstds):
                pool.wait_ge(x_rstd, rstds)
                stage(PIECES, x_rows)
                zero_work(x_updates)
                n["ro0"].up(16)
                n["ro1"].up(16)

            mlp(1, 2)
            pool.wait_ge(x_rstd, 3)
            stage(PIECES, x_rows)
            for ch in range(4):
                passed(ch % 2)
                rope(ch % 2)
            pool.wait_ge(hT_full, n["hT"]())
            pool.wait_ge(qk_full, 2 * (4 * GROUPS + 4))
            stage(PIECES, x_rows)
            for u in range(4):
                passed(0)
                rope(0)
                passed(1)
            n["hT"].up(PIECES)
            for u in range(2):
                passed(0), passed(1)
            mlp(3, 4)




def kernel(**inputs):
    from concourse import bacc
    from concourse.bass_utils import run_bass_kernel_spmd

    f = {k: np.asarray(v) for k, v in inputs.items()}

    def sections(a):
        own, kv = a
        at = {"l": lambda l, s: own[l][..., s * D:(s + 1) * D], "k": lambda _, s: kv[..., s * D:(s + 1) * D]}
        order = [("l", 0, 0), ("l", 0, 1), ("l", 0, 3), ("l", 0, 4), ("l", 0, 2), ("l", 1, 0), ("l", 1, 1),
                 ("k", 0, 0), ("l", 0, 5), ("k", 0, 1), ("l", 1, 3), ("l", 1, 4), ("l", 1, 2), ("l", 1, 5)]
        return np.stack([at[w](l, s) for w, l, s in order])

    def pieces(w):
        k, m = w.shape
        return w.reshape(k // (PK * P), PK, P, m // NC, NC).transpose(3, 0, 2, 1, 4).reshape(-1, PK * NC)

    qkv = f["a_w_qkv"][0].reshape(D, GROUPS, 3, 2, NC)
    stream = []
    for g in range(GROUPS):
        for quad in range(2):
            for part in range(3):
                stream.append(pieces(qkv[:, g, part, quad]))
    stream.append(pieces(f["a_w_o"][0]))
    for layer in range(LAYERS):
        if layer:
            stream.append(pieces(f["b_w_q"][0]))
            for u in range(4):
                stream += [pieces(f["kv_w_k"][:, cols(u, NC)]), pieces(f["kv_w_v"][:, cols(u, NC)])]
            stream.append(pieces(f["b_w_o"][0]))
        for b in range(4):
            stream += [pieces(f["mlp_w1"][layer][:, cols(b, D)]), pieces(f["mlp_w2"][layer][cols(b, D)])]
    vecs = np.concatenate([f["c"].reshape(-1, P), f["norm_g"].reshape(-1, P), f["kv_norm_g"].reshape(-1, P)])
    gains = np.concatenate([f["a_q_gain"][0], f["a_k_gain"][0], f["kv_k_gain"], f["b_q_gain"][0]])
    arrays = {
        "x": f["x"].reshape(SEQ, D),
        "vecs": vecs,
        "pos": f["positions"].reshape(T, P).T,
        "gains": gains.reshape(-1),
        "subg": f["b_subln_g"].reshape(-1),
        "lamb": f["b_lambda"].reshape(-1),
        "ada": sections((f["ada_w"], f["kv_ada_w"])).reshape(-1, D),
        "ada_bias": sections((f["ada_b"], f["kv_ada_b"])),
        "w": np.concatenate(stream),
    }
    nc = bacc.Bacc("TRN2", target_bir_lowering=False, num_devices=1)
    args = []
    arrays = {k: np.ascontiguousarray(a) for k, a in arrays.items()}
    for name, a in arrays.items():
        args.append(nc.dram_tensor(name, a.shape, mybir.dt.from_np(a.dtype), kind="ExternalInput").ap())
    args.append(nc.dram_tensor("out", (SEQ, D), F32, kind="ExternalOutput").ap())
    trunk(nc, *args)
    r = run_bass_kernel_spmd(nc, [arrays], core_ids=[0])
    return r.results[0]["out"].reshape(1, SEQ, D)
```

```python
import math
from contextlib import ExitStack, contextmanager

import numpy as np

import concourse.bass as bass
from concourse import mybir

P = 128
SEQ = 256
T = SEQ // P
D = 2048
KT = D // P
NC = 512
PK = 2
PIECES = KT // PK
SLOTS = 4
ADA_SLOTS = 2
HD = 128
HEADS_A = 8
GROUPS = 3
D_FF = 4 * D
ROT = 32
HALF = ROT // 2
EPS = 1e-6
NEG = -1e30
SCALE = float(HD) ** -0.5
LAM_INIT = 0.8 - 0.6 * math.exp(-0.3)
LAYERS = 2
MAPS = 4
V_C, V_G = 0, 1
(S_SHIFT_T0, S_SCALE_T0, S_SHIFT_M0, S_SCALE_M0, S_SHIFT_T1, S_SCALE_T1, S_SHIFT_KV, S_SCALE_KV, S_SHIFT_M1,
 S_SCALE_M1) = range(10)
MIXED = 4

ALU = mybir.AluOpType
ACT = mybir.ActivationFunctionType
F32 = mybir.dt.float32
F32R = mybir.dt.float32r
BF16 = mybir.dt.bfloat16
I32 = mybir.dt.int32


class Count:

    def __init__(self):
        self.n, self.base = 0, None

    def up(self, k=1):
        self.n += k
        return self()

    def __call__(self, at=None):
        v = self.n if at is None else at
        return v if self.base is None else self.base + v


class Counts(dict):
    def __missing__(self, name):
        self[name] = Count()
        return self[name]


@contextmanager
def repeat(eng, times, counts, **rises):
    before = {k: c.n for k, c in counts.items()}
    with eng.Fori(0, times) as i:
        for k, r in rises.items():
            counts[k].base = i * r
        yield i
        grown = {k: c.n - before.get(k, 0) for k, c in counts.items() if c.n != before.get(k, 0)}
        assert grown == rises, grown
    for k, r in rises.items():
        counts[k].n += (times - 1) * r
        counts[k].base = None


def cols(i, size):
    return slice(i * size, (i + 1) * size) if isinstance(i, int) else bass.ds(i * size, size)


ADA_QKV = [(c, j) for c, js in enumerate(((0, 3, 6), (0, 3, 6), (1, 4, 7), (0, 3, 6), (0, 2, 4, 6))) for j in js]
ADA_WO = [(1, 0), (1, 2), (2, 0), (2, 2), (3, 0)]
ADA_GATE = [(c, j) for c, js in enumerate(((1, 3, 5, 7), (1, 3, 5, 7), (0, 1, 3))) for j in js]
ADA_FIRST = [(c, j) for c, js in enumerate(((2, 4, 5, 7), (0, 2, 4, 6), (0, 2, 4, 6), (0, 1, 2, 4)), 3) for j in js]
ADA_MLP = [(c, j) for c, js in enumerate(((1, 5), (1, 5), (1, 5), (1, 5), (1, 5), (0, 2, 5), (0, 2, 4))) for j in js]
ADA_Q = [(c, j) for c, js in enumerate(((5, 7), (0, 2, 4, 6), (0, 2, 4, 6), (0, 2, 4, 6), (5, 7))) for j in js]
ADA_KV = [(c, j) for c, js in enumerate(((6, 7), (1, 4, 6), (2, 5), (1, 4, 6), (2, 5), (2, 5), (2, 5)), 1) for j in js]
ADA_WO_B = [(c, j) for c, js in enumerate(((5, 6, 7), (0, 2, 4, 5, 6), (0, 2, 4, 6), (0, 2, 4, 6))) for j in js]
ADA_GATE_B = [(c, j) for c, js in enumerate(((0, 2, 4, 5, 6), (0, 2, 4, 5, 6), (0, 2, 3, 5, 6), (0,))) for j in js]


def trunk(nc, x_in, vecs_in, pos_in, gains_in, subg_in, lamb_in, ada_in, bias_cols_in, bias_rows_in, w_in, out):
    ctx = ExitStack()
    with ctx:
        def sb(name, shape, dt=F32):
            return ctx.enter_context(nc.sbuf_tensor(name, shape, dt))

        sems = {}

        def sem(name):
            if name not in sems:
                sems[name] = ctx.enter_context(nc.semaphore(name))
            return sems[name]

        w_raw = sb("w_raw", [P, SLOTS, PK * NC])
        w_hi = sb("w_hi", [P, SLOTS, PK * NC], F32R)
        w_lo = sb("w_lo", [P, SLOTS, PK * NC], F32R)
        ada_raw = sb("ada_raw", [P, ADA_SLOTS, D])
        acc = sb("acc", [P, D])
        gate = sb("gate", [P, 4, NC])
        xs = sb("xs", [P, T, D])
        work = sb("work", [P, 2 * D])
        hT_hi = sb("hT_hi", [P, KT, T * P], F32R)
        hT_lo = sb("hT_lo", [P, KT, T * P], F32R)
        st_a = sb("st_a", [P, T * NC])
        st_b = sb("st_b", [P, T * NC])
        st_x = sb("st_x", [P, T * NC])
        pT = sb("pT", [P, 2, 3 * P])
        masks = sb("masks", [P, 4, 3 * P], BF16)
        gain_now = sb("gain_now", [P, 2 * HD])
        mask_now = sb("mask_now", [P, 3 * P], BF16)
        gains = sb("gains_sb", [P, 10 * HD])
        subg = sb("subg_sb", [P, 2 * HD])
        ident = sb("ident", [P, P])
        ones = sb("ones", [P, P])
        vec = sb("vec", [P, 6, KT])
        c_act = sb("c_act", [P, KT])
        modc = sb("modc", [P, 10, KT])
        sums = sb("sums", [P, KT])
        cos = sb("cos", [P, T * HALF])
        sin = sb("sin", [P, T * HALF])
        small = sb("small", [P, 64])
        ssq = sb("ssq", [P, 8])
        rms = sb("rms", [P, 8])
        rstd = sb("rstd", [P, 8])
        ssx = sb("ssx", [P, T, 4])
        pairx = sb("pairx", [P, T, 2])
        sumx = sb("sumx", [P, T])
        rmsx = sb("rmsx", [P, 2])
        rstdx = sb("rstdx", [P, 2])
        m8 = sb("m8", [P, 8])
        mn8 = sb("mn8", [P, 8])
        neg8 = sb("neg8", [P, 8])
        diff8 = sb("diff8", [P, 8])
        corr8 = sb("corr8", [P, 8])
        d8 = sb("d8", [P, 8])
        r8 = sb("r8", [P, 8])
        m_old = sb("m_old", [P, 2, 8])
        den = sb("den", [P, 2, 8])
        rden = sb("rden", [P, 16])
        eps_t = sb("eps_t", [P, 1])
        hpi_t = sb("hpi_t", [P, 1])
        lam = sb("lam", [P, 8])
        ssv = sb("ssv", [P, 2])
        rmsv = sb("rmsv", [P, 2])
        rstdv = sb("rstdv", [P, 2])
        inv_freq = sb("inv_freq", [P, HALF])
        pos_f = sb("pos_f", [P, T])
        turns = sb("turns", [P, T * HALF])
        rot = sb("rot", [P, T, 4, MAPS, HALF])
        scratch = sb("scratch", [P, 1])
        marks = sb("marks", [P, PIECES])
        scratch_g = sb("scratch_g", [P, 1])
        pos_i = sb("pos_i", [P, T], I32)

        with nc.sbuf_tensor("mid_hi", [P, KT, T * P], F32R) as mid_hi, \
                nc.sbuf_tensor("mid_lo", [P, KT, T * P], F32R) as mid_lo:
            pass
        qT = sb("qT", [P, 16, T * P])
        kT = sb("kT", [P, MAPS, T * P])
        vv = sb("vv", [P, T, NC])
        sm = sb("sm", [P, MAPS, 3 * P])
        residue_i = sm[:, 0, 0:2 * P].bitcast(I32)
        dist = sm[:, 1, 0:P].bitcast(I32)
        residue = sm[:, 2, 0:P].bitcast(BF16)
        cols_in = sm[:, 3, 0:P]
        ada_start = [ada_raw[:, 0, :], ada_raw[:, 1, :],
                     *(qT[:, a * 8:(a + 1) * 8, :].rearrange("p a b -> p (a b)") for a in range(2))]

        main = [[ctx.enter_context(nc.psum_tensor(f"main{p}{t}", [P, NC], F32)) for t in range(T)] for p in range(2)]
        tr = [ctx.enter_context(nc.psum_tensor(f"tr{b}", [P, NC], F32)) for b in range(2)]
        sc = ctx.enter_context(nc.psum_tensor("sc", [P, NC], F32))
        ov = ctx.enter_context(nc.psum_tensor("ov", [P, NC], F32))

        sta = st_a[:, :].rearrange("p (t n) -> p t n", t=T)
        stb = st_b[:, :].rearrange("p (t n) -> p t n", t=T)
        stx = st_x[:, :].rearrange("p (t n) -> p t n", t=T)
        acc_rows = acc[:, :].rearrange("p (n c) -> p n c", c=NC)
        group_out = work[:, 0:D].rearrange("p (h t e) -> p h t e", t=T, e=HD)
        head_out = work[:, :].rearrange("p (h t e) -> p h t e", t=T, e=2 * HD)
        wv = w_in.rearrange("(n p) c -> n p c", p=P)
        av = ada_in.rearrange("(n p) c -> n p c", p=P)

        raw_in = [sem(f"raw_in{s}") for s in range(SLOTS)]
        hi_done = sem("hi_done")
        lo_done = sem("lo_done")
        mm_done = sem("mm_done")
        ada_in = [sem(f"ada_in{s}") for s in range(ADA_SLOTS)]
        ada_start_in = [sem(f"ada_start_in{s}") for s in range(len(ada_start))]
        ada_used = sem("ada_used")
        gate_bias = sem("gate_bias")
        read_out = [sem(f"read_out{p}") for p in range(2)]
        tr_free = [sem(f"tr_free{b}") for b in range(2)]
        vec_full, col_full, row_full = sem("vec_full"), sem("col_full"), sem("row_full")
        hT_full, mid_full, qk_full, pt_full = sem("hT_full"), sem("mid_full"), sem("qk_full"), sem("pt_full")
        modulated = sem("modulated")
        hT_split = sem("hT_split")
        hi_part = sem("hi_part")
        sc_full, sc_free = sem("sc_full"), sem("sc_free")
        ov_full, ov_free = sem("ov_full"), sem("ov_free")
        rms_done, roped = sem("rms_done"), sem("roped")
        staged = sem("staged")
        x_rms, x_rstd, x_done = sem("x_rms"), sem("x_rstd"), sem("x_done")
        relu_done = sem("relu_done")
        smx_done, p_done, mix_done = sem("smx_done"), sem("p_done"), sem("mix_done")
        sub_rms, den_inv = sem("sub_rms"), sem("den_inv")
        mod_done, x_sq, x_sum = sem("mod_done"), sem("x_sq"), sem("x_sum")
        seq_v, seq_a, seq_g = sem("seq_v"), sem("seq_a"), sem("seq_g")
        small_in, x_in_done, stored = sem("small_in"), sem("x_in_done"), sem("stored")
        consts, trig, c_exp, c_done = sem("consts"), sem("trig"), sem("c_exp"), sem("c_done")
        eps_set, dist_done, residue_done = sem("eps_set"), sem("dist_done"), sem("residue_done")
        vec_done, lam_dot, lam_exp, trig_done = sem("vec_done"), sem("lam_dot"), sem("lam_exp"), sem("trig_done")

        block = ctx.enter_context(nc.Block())

        @block.sync
        def _(sp):
            n = Counts()

            def weight_piece():
                n["w"].up()
                s = (n["w"].n - 1) % SLOTS
                sp.wait_ge(lo_done, n["w"]())
                at = n["w"](n["w"].n - 1)
                src = wv[at] if isinstance(at, int) else wv[bass.ds(at, 1), :, :].rearrange("a p c -> p (a c)")
                sp.dma_start(w_raw[:, s, :], src).then_inc(raw_in[s], 16)

            def row(v, at):
                return v[at] if isinstance(at, int) else v[bass.ds(at, 1), :, :].rearrange("a p c -> p (a c)")

            def ada_piece():
                n["ada"].up()
                s = (n["ada"].n - 1) % ADA_SLOTS
                sp.wait_ge(ada_used, n["ada"]())
                sp.dma_start(ada_raw[:, s, :], row(av, n["ada"](n["ada"].n - 1))).then_inc(ada_in[s], 16)

            def bias(gate_no, updates):
                if updates:
                    sp.wait_ge(x_done, updates)
                sp.dma_start(gate[:, :, :].rearrange("p n c -> p (n c)"),
                             bias_rows_in[gate_no].partition_broadcast(P)).then_inc(gate_bias, 16)

            def chunk(ch, pieces=PIECES, ada=()):
                for j in range(pieces):
                    weight_piece()
                    if (ch, j) in ada:
                        ada_piece()

            sp.dma_start(cols_in[0:96, :], vecs_in).then_inc(small_in, 16)
            sp.dma_start(pos_i[:, :], pos_in).then_inc(small_in, 16)
            sp.dma_start(gains[:, :], gains_in.partition_broadcast(P)).then_inc(small_in, 16)
            sp.dma_start(subg[:, :], subg_in.partition_broadcast(P)).then_inc(small_in, 16)
            sp.dma_start(modc[:, :, :], bias_cols_in).then_inc(small_in, 16)
            sp.dma_start(st_a[:, 0:NC], lamb_in.partition_broadcast(P)).then_inc(small_in, 16)
            sp.dma_start(xs[:, :, :], x_in.rearrange("(t p) d -> p t d", p=P)).then_inc(x_in_done, 16)
            for a in range(2 * KT):
                s = a % len(ada_start)
                if a >= len(ada_start):
                    sp.wait_ge(ada_used, ADA_SLOTS + a + 1 - len(ada_start))
                sp.dma_start(ada_start[s], av[a]).then_inc(ada_start_in[s], 16)
            n["ada"].up(2 * KT)
            chunk(0)
            with repeat(sp, GROUPS - 1, n, ada=KT, w=6 * PIECES):
                for ch in range(6):
                    chunk(ch, ada=ADA_QKV)
            bias(0, 0)
            for ch in range(5):
                chunk(ch, ada=ADA_QKV)
            for ch in range(4):
                chunk(ch, PIECES // 2, ADA_WO)
            chunk(0)
            bias(1, 4)
            for ch in range(8):
                chunk(ch, ada=ADA_GATE + ADA_FIRST)
            with repeat(sp, 2, n, ada=KT, w=8 * PIECES):
                for ch in range(8):
                    chunk(ch, ada=ADA_MLP)
            for ch in range(7):
                chunk(ch, ada=ADA_MLP)
            chunk(0, ada=ADA_Q)
            bias(2, 4 + 16)
            for ch in range(1, 5):
                chunk(ch, ada=ADA_Q)
            for ch in range(1, 8):
                chunk(ch, ada=ADA_KV)
            for ch in range(4):
                chunk(ch, ada=ADA_WO_B)
            chunk(0)
            bias(3, 4 + 16 + 4)
            for ch in range(8):
                chunk(ch, ada=ADA_GATE_B)
            with repeat(sp, 2, n, w=8 * PIECES):
                for ch in range(8):
                    chunk(ch)
            for ch in range(7):
                chunk(ch)
            sp.wait_ge(x_done, 4 + 16 + 4 + 16)
            sp.dma_start(out.rearrange("(t p) d -> p t d", p=P), xs[:, :, :]).then_inc(stored, 16)
            sp.wait_ge(stored, 16)

        @block.tensor
        def _(pe):
            n = Counts()

            def claim_tr(b):
                n[f"tr{b}"].up()
                pe.wait_ge(tr_free[b], n[f"tr{b}"]())

            def claim_main(par):
                n[f"ro{par}"].up()
                pe.wait_ge(read_out[par], n[f"ro{par}"]())

            def gemm(par, pairs, hi, lo, side=None, ready=None):
                claim_main(par)
                for j in range(pairs):
                    n["w"].up()
                    s = (n["w"].n - 1) % SLOTS
                    if ready:
                        ready(j)
                    pe.wait_ge(lo_done, n["w"](n["w"].n + SLOTS))
                    for k in range(PK):
                        kt = PK * j + k
                        wc = slice(k * NC, (k + 1) * NC)
                        for t in range(T):
                            acc_ps, tc = main[par][t], slice(t * P, (t + 1) * P)
                            pe.matmul(acc_ps[:, :], hi[:, kt, tc], w_hi[:, s, wc], start=(kt == 0), stop=False)
                            pe.matmul(acc_ps[:, :], hi[:, kt, tc], w_lo[:, s, wc], start=False, stop=False)
                            last = pe.matmul(acc_ps[:, :], lo[:, kt, tc], w_hi[:, s, wc], start=False,
                                             stop=(kt == PK * pairs - 1))
                    last.then_inc(mm_done, 1)
                    for step in (side or {}).get(j, ()):
                        step()

            def pair_transposes(b, source):
                for k in range(PK):
                    for t in range(T):
                        at = k * T * P + t * P
                        last = pe.transpose(tr[b][:, at:at + P], source(k, t), ident[:, :])
                return last

            def build(pairs=PIECES, source=None, modulate=True):
                first, made, made_split = [n["tr0"].n, n["tr1"].n], [0], n["split"].n
                n["split"].up(pairs if modulate else 0)

                def transposes():
                    j = made[0]
                    made[0] += 1
                    claim_tr(j % 2)
                    if source is None:
                        n["staged"].up()
                        pe.wait_ge(staged, n["staged"]())
                        last = pair_transposes(j % 2, lambda k, t: stx[:, j % 2, (t * PK + k) * P:(t * PK + k + 1) * P])
                    else:
                        last = pair_transposes(j % 2, lambda k, t: source(PK * j + k, t))
                    last.then_inc(hT_full, 1)

                def ready(j):
                    if modulate:
                        pe.wait_ge(hT_split, made_split + j + 1)
                    else:
                        pe.wait_ge(tr_free[j % 2], first[j % 2] + j // 2 + 2)

                for _ in range(4):
                    transposes()
                return {j: [transposes] for j in range(pairs - 4)}, ready

            def sum_columns(quarter):
                def step():
                    if quarter == 0:
                        n["ada"].up(KT)
                        pe.wait_ge(ada_used, n["ada"](n["ada"].n + ADA_SLOTS))
                    b = quarter % 2
                    claim_tr(b)
                    for k in range(4):
                        last = pe.transpose(tr[b][:, k * P:(k + 1) * P], acc_rows[:, quarter, k * P:(k + 1) * P],
                                            ident[:, :])
                    last.then_inc(col_full, 1)
                return step

            def sum_rows(quarter):
                def step():
                    if quarter == 0:
                        n["ada"].up(KT)
                        pe.wait_ge(ada_used, n["ada"](n["ada"].n + ADA_SLOTS))
                    claim_tr(quarter % 2)
                    pe.matmul(tr[quarter % 2][:, :], ones[:, :], acc_rows[:, quarter, :], start=True,
                              stop=True).then_inc(row_full, 1)
                return step

            def qk_transposes():
                pe.wait_ge(roped, n["roped"].up())
                for t in range(T):
                    claim_tr(t)
                    for m in range(MAPS):
                        last = pe.transpose(tr[t][:, m * P:(m + 1) * P], sta[:, t, m * P:(m + 1) * P], ident[:, :])
                    last.then_inc(qk_full, 1)

            def scores(m, q0=0):
                def step():
                    if m == 0:
                        for b in range(2):
                            pe.wait_ge(tr_free[b], n[f"tr{b}"](n[f"tr{b}"].n + 1))
                    pe.wait_ge(sc_free, n["sc"].up())
                    q, k = qT[:, q0 + m, :], kT[:, m, :]
                    pe.matmul(sc[:, 0:P], q[:, 0:P], k[:, 0:P], start=True, stop=True)
                    pe.matmul(sc[:, P:3 * P], q[:, P:2 * P], k[:, :], start=True, stop=True).then_inc(sc_full, 1)
                return step

            def p_transposes(i, m, ready, name):
                def step():
                    pe.wait_ge(ready, n[name].up())
                    claim_tr(i)
                    for c in range(3):
                        last = pe.transpose(tr[i][:, c * P:(c + 1) * P], sm[:, m, c * P:(c + 1) * P], ident[:, :])
                    last.then_inc(pt_full, 1)
                return step

            def pv(i, width, at, v0):
                a, b = ov[:, at:at + width], ov[:, at + width:at + 2 * width]
                pe.matmul(a, pT[:, i, 0:P], vv[:, 0, v0:v0 + width], start=True, stop=True)
                pe.matmul(b, pT[:, i, P:2 * P], vv[:, 0, v0:v0 + width], start=True, stop=False)
                return pe.matmul(b, pT[:, i, 2 * P:3 * P], vv[:, 1, v0:v0 + width], start=False, stop=True)

            def wait_pt(i, later=0):
                pe.wait_ge(tr_free[i], n[f"tr{i}"](n[f"tr{i}"].n + 1 - later))

            def values_ready(par, back):
                pe.wait_ge(read_out[par], n[f"ro{par}"](n[f"ro{par}"].n + 1 - back))

            def pv_pair(pair, par, back):
                def step():
                    pe.wait_ge(ov_free, n["ov"].up())
                    values_ready(par, back)
                    for i in range(2):
                        wait_pt(i)
                        last = pv(i, HD, 2 * HD * i, (2 * pair + i) * HD)
                    last.then_inc(ov_full, 1)
                return step

            def pv_head(h, back, later=0):
                def step():
                    pe.wait_ge(ov_free, n["ov"].up())
                    values_ready(1, back)
                    wait_pt(h, later)
                    pv(h, 2 * HD, 0, h * 2 * HD).then_inc(ov_full, 1)
                return step

            def attn_a(par, back):
                pt = [[p_transposes(i, 2 * pair + i, p_done, "p") for i in range(2)] for pair in range(2)]
                return ({m: [scores(m)] for m in range(MAPS)},
                        {0: pt[0], 1: [pv_pair(0, par, back)], 2: pt[1], 3: [pv_pair(1, par, back)]})

            def attn_b(q0, back):
                pt = [p_transposes(h, 2 * h, mix_done, "mix") for h in range(2)]
                return ({m: [scores(m, q0)] for m in range(MAPS)},
                        {1: pt, 2: [pv_head(0, back)], 4: [pv_head(1, back, back)]})

            def also(side, *others):
                side = {j: list(steps) for j, steps in side.items()}
                for other in others:
                    for j, steps in other.items():
                        side[j] = side.get(j, []) + list(steps)
                return side

            def halves(sum_of, j):
                return {j: [sum_of(0), sum_of(1)], j + 1: [sum_of(2), sum_of(3)]}

            def all_of(*sides):
                for side in sides:
                    for j in sorted(side):
                        for step in side[j]:
                            step()

            qk = {3: [qk_transposes]}
            pe.sem_inc(mm_done, SLOTS)
            pe.wait_ge(consts, 2)
            pe.wait_ge(small_in, 16 * 6)
            claim_tr(0)
            pe.transpose(tr[0][:, 0:96], cols_in[0:96, :], ident[0:96, 0:96]).then_inc(vec_full, 1)
            for _ in range(2):
                all_of(halves(sum_columns, 0))

            h = (PIECES, hT_hi, hT_lo)
            side, ready = build()
            gemm(0, *h, side=side, ready=ready)

            def group(last):
                gemm(1, *h, side=also(attn_a(1, 1)[1], qk))
                gemm(0, *h, side=qk)
                gemm(1, *h)
                scores_, values_ = attn_a(0, 1)
                gemm(0, *h, side=also(scores_, qk))
                gemm(1, *h, side=also(values_, qk))
                if not last:
                    gemm(0, *h, side=also(attn_a(1, 1)[0], halves(sum_columns, 1)))

            with repeat(pe, GROUPS - 1, n, ada=KT, w=6 * PIECES, ro0=3, ro1=3, roped=4, tr0=10, tr1=10, sc=8,
                        p=8, ov=4):
                group(False)
            group(True)
            scores_, values_ = attn_a(1, 0)
            all_of(scores_, halves(sum_rows, 0), values_)
            side, ready = build(PIECES // 2, modulate=False)
            for ch in range(4):
                gemm(ch % 2, PIECES // 2, hT_hi, hT_lo, ready=ready if ch == 0 else None)

            def mlp(sums, gate_at):
                side, ready = build()
                gemm(0, *h, side=side, ready=ready)

                def block(number, last=False):
                    first = [n["tr0"].n, n["tr1"].n]

                    def hidden(par):
                        def step():
                            pe.wait_ge(read_out[par], n[f"ro{par}"](n[f"ro{par}"].n + 1))
                            for kp in range(2):
                                claim_tr(kp)
                                pair_transposes(
                                    kp, lambda k, t: stb[:, t, (PK * kp + k) * P:(PK * kp + k + 1) * P]
                                ).then_inc(mid_full, 1)
                        return step

                    gaps = [0]

                    def mid_ready(j):
                        late = gaps[0] if j >= 6 else 0
                        pe.wait_ge(tr_free[j % 2], n[f"tr{j % 2}"](first[j % 2] + j // 2 + 2 + late))

                    sides = [{2: [hidden(1 - c % 2)]} for c in range(1, 5)] + [{}, {}, {}]
                    if number == 0:
                        sides[gate_at] = also(sides[gate_at], halves(sum_rows, 5))
                        gaps[0] = 2 if gate_at < 3 else 0
                    if sums:
                        sides[6] = halves(sum_columns, 3)
                    for c in range(1, 4):
                        gemm(c % 2, *h, side=sides[c - 1])
                    for c in range(4):
                        gemm(c % 2, PIECES, mid_hi, mid_lo, side=sides[c + 3], ready=mid_ready if c == 0 else None)
                    if not last:
                        gemm(0, *h)

                rises = dict(w=8 * PIECES, ro0=4, ro1=4, tr0=4, tr1=4)
                if sums:
                    rises.update(ada=KT, tr0=6, tr1=6)
                block(0)
                with repeat(pe, 2, n, **rises):
                    block(None)
                block(3, True)

            mlp(True, 2)

            side, ready = build()
            for ch in range(4):
                gemm(ch % 2, *h, side=qk if ch else side, ready=None if ch else ready)
            side, ready = build()
            gemm(0, *h, side=also(side, qk), ready=ready)
            gemm(1, *h, side=also(halves(sum_rows, 0), qk))
            for u in range(1, 4):
                scores_, values_ = attn_b((u - 1) * MAPS, 1)
                gemm(0, *h, side=scores_)
                gemm(1, *h, side=also(values_, qk))
            scores_, values_ = attn_b(3 * MAPS, 0)
            all_of(scores_, halves(sum_columns, 0), values_)
            pe.wait_ge(ov_free, n["ov"](n["ov"].n + 1))
            side, ready = build(source=lambda kt, t: head_out[:, kt // 2, t, (kt % 2) * P:(kt % 2 + 1) * P],
                                modulate=False)
            gemm(0, *h, side=side, ready=ready)
            for ch in range(1, 4):
                gemm(ch % 2, *h)
            all_of(halves(sum_columns, 0))
            mlp(False, 3)

        @block.scalar
        def _(act):
            n = Counts()

            def split():
                n["w"].up()
                w, base = n["w"].n, n["w"].base
                s = (w - 1) % SLOTS
                fills = ((w - 1) // SLOTS + 1) * 16
                act.wait_ge(raw_in[s], fills if base is None else base * (16 // SLOTS) + fills)
                act.wait_ge(mm_done, n["w"]())
                act.activation(w_hi[:, s, :], w_raw[:, s, :], ACT.Copy).then_inc(hi_done, 1)

            def chunk(pieces, side=None):
                for j in range(pieces + 1):
                    for step in (side or {}).get(j, ()):
                        step()
                    if j < pieces:
                        split()

            def ended(back):
                act.wait_ge(mm_done, n["w"](n["w"].n + SLOTS - back))

            def chained(ins):
                ins.then_inc(seq_a, 1)
                act.wait_ge(seq_a, n["seq"].up())

            def qk_stats(par, back=4):
                def step():
                    ended(back)
                    for t in range(T):
                        for m in range(MAPS):
                            i = t * MAPS + m
                            last = act.activation(st_b[:, i * P:(i + 1) * P], main[par][t][:, m * P:(m + 1) * P],
                                                  ACT.Square, accum_out=ssq[:, i:i + 1])
                    chained(last)
                    act.activation(rms[:, :], ssq[:, :], ACT.Sqrt, bias=eps_t[:, :], scale=1.0 / HD).then_inc(rms_done, 1)
                return step

            def move_tile0(dst):
                def step():
                    n["qk"].up(2)
                    act.wait_ge(qk_full, n["qk"](n["qk"].n - 1))
                    act.activation(dst[:, :, 0:P], tr[0][:, :].rearrange("p (m n) -> p m n", m=MAPS),
                                   ACT.Copy).then_inc(tr_free[0], 1)
                return step

            def values(par, back=4):
                def step():
                    ended(back)
                    act.activation(vv[:, 0, :], main[par][0][:, :], ACT.Copy)
                    act.activation(vv[:, 1, :], main[par][1][:, :], ACT.Copy).then_inc(read_out[par], 1)
                return step

            def exps(running):
                def step():
                    act.wait_ge(smx_done, n["smx"].up())
                    if running:
                        act.activation(corr8[:, :], diff8[:, :], ACT.Exp)
                    for m in range(MAPS):
                        act.activation(sm[:, m, 0:P], sm[:, m, 0:P], ACT.Exp, bias=neg8[:, 2 * m:2 * m + 1],
                                       accum_out=d8[:, 2 * m:2 * m + 1])
                        act.activation(sm[:, m, P:3 * P], sm[:, m, P:3 * P], ACT.Exp, bias=neg8[:, 2 * m + 1:2 * m + 2],
                                       accum_out=d8[:, 2 * m + 1:2 * m + 2]).then_inc(p_done, 1)
                return step

            def move_pt():
                n["pt"].up(2)
                act.wait_ge(pt_full, n["pt"](n["pt"].n - 1))
                act.activation(pT[:, 0, :], tr[0][:, 0:3 * P], ACT.Copy).then_inc(tr_free[0], 1)

            def sub_stats():
                act.wait_ge(ov_full, n["ov"].up())
                act.activation(st_b[:, 0:2 * HD], ov[:, 0:2 * HD], ACT.Square, accum_out=ssv[:, 0:1])
                chained(act.activation(st_b[:, 2 * HD:4 * HD], ov[:, 2 * HD:4 * HD], ACT.Square, accum_out=ssv[:, 1:2]))
                act.activation(rmsv[:, :], ssv[:, :], ACT.Sqrt, bias=eps_t[:, :],
                               scale=1.0 / (2 * HD)).then_inc(sub_rms, 1)

            def squares(c):
                if n["sq"].n:
                    act.wait_ge(x_sq, n["sq"]())
                for t, bank in enumerate((sc, ov)):
                    last = act.activation(bank[:, :], xs[:, t, cols(c, NC)], ACT.Square, accum_out=ssx[:, t, c:c + 1])
                n["sq"].up()
                last.then_inc(x_sq, 1)

            def squares_of(c):
                def step():
                    act.wait_ge(x_done, n["x"].up())
                    squares(c)
                return step

            def root():
                act.wait_ge(x_sum, n["xs"].up())
                act.activation(rmsx[:, :], sumx[:, :], ACT.Sqrt, bias=eps_t[:, :], scale=1.0 / D).then_inc(x_rms, 1)

            def high(j, modulate=True, new=False):
                def step():
                    if j == 0 and n["w"].n > SLOTS:
                        ended(4)
                    n["hT"].up()
                    dst = hT_hi[:, PK * j:PK * (j + 1), :].rearrange("p k n -> p (k n)")
                    if modulate:
                        act.wait_ge(modulated, n["modulated"].up())
                        act.activation(dst, stb[:, j % 2, :], ACT.Copy).then_inc(hi_part, 1)
                    else:
                        act.wait_ge(hT_full, n["hT"]())
                        act.activation(dst, tr[j % 2][:, :], ACT.Copy).then_inc(hi_part, 1)
                return step

            def entry(before, modulate=True, pairs=PIECES, after=()):
                side = {4: list(before) + [high(j, modulate) for j in range(4)]}
                for j in range(4, pairs):
                    side[j + 1] = [high(j, modulate)]
                side[pairs] = side.get(pairs, []) + list(after)
                return side

            act.wait_ge(eps_set, 1)
            act.wait_ge(vec_done, 1)
            act.activation(c_act[:, :], vec[:, V_C, :], ACT.Exp, scale=-1.0).then_inc(c_exp, 1)
            act.wait_ge(lam_dot, 1)
            act.activation(lam[:, 2:4], lam[:, 0:2], ACT.Exp).then_inc(lam_exp, 1)
            act.wait_ge(trig, 1)
            act.activation(sin[:, :], small[:, 0:T * HALF], ACT.Sin)
            act.activation(cos[:, :], small[:, T * HALF:2 * T * HALF], ACT.Sin, bias=hpi_t[:, :],
                           scale=-1.0).then_inc(trig_done, 1)
            act.wait_ge(x_in_done, 16)
            for c in range(4):
                squares(c)
            root()
            q4, k4 = qT[:, 0:MAPS, :], kT[:, :, :]
            chunk(PIECES, entry([]))

            def group(last):
                chunk(PIECES, {4: [qk_stats(0), move_pt], 6: [move_pt], 8: [move_tile0(q4)]})
                chunk(PIECES, {4: [qk_stats(1)], 8: [move_tile0(k4)]})
                chunk(PIECES, {4: [values(0)]})
                chunk(PIECES, {4: [qk_stats(1)], 8: [move_tile0(q4), exps(True)]})
                chunk(PIECES, {4: [qk_stats(0), move_pt], 6: [move_pt], 8: [move_tile0(k4)]})
                if not last:
                    chunk(PIECES, {4: [values(1)], 8: [exps(True)]})

            with repeat(act, GROUPS - 1, n, w=6 * PIECES, seq=4, qk=8, smx=2, pt=8):
                group(False)
            group(True)
            chunk(PIECES // 2, entry([values(1), exps(True), move_pt, move_pt], False, 4))
            chunk(PIECES // 2)
            for c in range(2):
                chunk(PIECES // 2, {4: [squares_of(c)]})

            def mlp(final):
                chunk(PIECES, entry([squares_of(2), squares_of(3), root]))

                def block(last=False):
                    def relu(par):
                        def step():
                            ended(4)
                            for t in range(T):
                                last = act.activation(sta[:, t, :], main[par][t][:, :], ACT.Relu)
                            last.then_inc(relu_done, 1)
                        return step

                    def mid(c):
                        def step():
                            for kp in range(2):
                                act.wait_ge(mid_full, n["mid"].up())
                                kt = 4 * c + PK * kp
                                act.activation(mid_hi[:, kt:kt + PK, :],
                                               tr[kp][:, :].rearrange("p (k n) -> p k n", k=PK),
                                               ACT.Copy).then_inc(hi_part, 1)
                        return step

                    for c in range(1, 4):
                        chunk(PIECES, {4: [relu(1 - c % 2)], 7: [mid(c - 1)]})
                    chunk(PIECES, {4: [relu(1)], 7: [mid(3)]})
                    for c in range(1, 4):
                        chunk(PIECES, {6: [squares_of(c - 1)]} if last and not final else None)
                    if not last:
                        chunk(PIECES)
                        n["x"].up(4)
                block()
                with repeat(act, 2, n, w=8 * PIECES, mid=8, x=4):
                    block()
                block(True)

            mlp(False)
            for ch in range(4):
                chunk(PIECES, {4: [qk_stats(1 - ch % 2)], 8: [move_tile0(qT[:, (ch - 1) * MAPS:ch * MAPS, :])]} if ch
                      else entry([squares_of(3), root]))
            chunk(PIECES, entry([qk_stats(1)], after=[move_tile0(qT[:, 3 * MAPS:4 * MAPS, :])]))
            n["ov"].up(4 * GROUPS + 2)
            chunk(PIECES, {4: [qk_stats(0)], 8: [move_tile0(k4)]})
            for u in range(1, 4):
                chunk(PIECES, {4: [values(1)], 8: [exps(False)]})
                chunk(PIECES, {4: [qk_stats(0), move_pt], 6: [sub_stats], 8: [move_tile0(k4), sub_stats]})
            chunk(PIECES, entry([values(1), exps(False), move_pt, sub_stats, sub_stats], False))
            chunk(PIECES)
            for c in range(2):
                chunk(PIECES, {4: [squares_of(c)]})
            mlp(True)

        @block.vector
        def _(dve):
            n = Counts()

            def chained(ins):
                ins.then_inc(seq_v, 1)
                dve.wait_ge(seq_v, n["seq"].up())

            def split():
                n["w"].up()
                s = (n["w"].n - 1) % SLOTS
                dve.wait_ge(hi_done, n["w"]())
                dve.tensor_tensor(w_lo[:, s, :], w_raw[:, s, :], w_hi[:, s, :].bitcast(F32),
                                  ALU.subtract).then_inc(lo_done, 1)

            def ada_piece(kt):
                n["landed"].up()
                a, base = n["landed"].n, n["landed"].base
                s = (a - 1) % ADA_SLOTS
                fills = ((a - 1) // ADA_SLOTS + 1) * 16
                dve.wait_ge(ada_in[s], fills if base is None else base * (16 // ADA_SLOTS) + fills)
                accumulate(kt, ada_raw[:, s, :])

            def accumulate(kt, piece):
                n["ada"].up()
                a = n["ada"].n
                if kt == 0:
                    ins = dve.tensor_scalar(acc[:, :], piece, c_act[:, 0:1], None, ALU.mult)
                else:
                    dve.wait_ge(ada_used, n["ada"](a - 1 + ADA_SLOTS))
                    ins = dve.scalar_tensor_tensor(out=acc[:, :], in0=piece, scalar=c_act[:, kt:kt + 1],
                                                   in1=acc[:, :], op0=ALU.mult, op1=ALU.add)
                ins.then_inc(ada_used, 1)

            def chunk(ch, pieces, side=None, ada=(), kt0=0):
                for j in range(pieces + 1):
                    for step in (side or {}).get(j, ()):
                        step()
                    if j < pieces:
                        split()
                        if (ch, j) in ada:
                            ada_piece((kt0 + ada.index((ch, j))) % KT)

            def column_sums(quarter):
                def step():
                    dve.wait_ge(col_full, n["col"].up())
                    dve.tensor_reduce(sums[:, quarter * 4:(quarter + 1) * 4],
                                      tr[quarter % 2][:, :].rearrange("p (k n) -> p k n", k=4),
                                      mybir.AxisListType.X, ALU.add).then_inc(tr_free[quarter % 2], 1)
                return step

            def add_columns(at):
                def step():
                    settled()
                    dst = modc[:, at, :] if isinstance(at, int) else modc[:, bass.ds(at, 1), :].rearrange("p a k -> p (a k)")
                    dve.tensor_tensor(dst, dst, sums[:, :], ALU.add)
                return step

            def add_mixed_columns(i):
                def step():
                    settled()
                    dst = modc[:, S_SHIFT_T1:S_SHIFT_T1 + MIXED, cols(i, 4)]
                    dve.tensor_tensor(dst, dst, sums[:, :].rearrange("p (s k) -> p s k", s=MIXED), ALU.add)
                return step

            all_sums = [column_sums(quarter) for quarter in range(4)]

            def move_rows(quarter):
                def step():
                    if quarter == 0:
                        dve.wait_ge(gate_bias, n["gate"].up(16))
                    dve.wait_ge(row_full, n["row"].up())
                    dve.tensor_tensor(gate[:, quarter, :], tr[quarter % 2][:, :], gate[:, quarter, :],
                                      ALU.add).then_inc(tr_free[quarter % 2], 1)
                return step

            all_rows = [move_rows(quarter) for quarter in range(4)]

            def settled():
                chained(dve.memset(scratch[:, :], 0.0))

            def norm(par, gain):
                def step():
                    dve.wait_ge(rms_done, n["rms"].up())
                    chained(dve.reciprocal(rstd[:, :], rms[:, :]))
                    for t in range(T):
                        for m in range(MAPS):
                            i = t * MAPS + m
                            last = dve.scalar_tensor_tensor(
                                out=sta[:, t, m * P:(m + 1) * P], in0=main[par][t][:, m * P:(m + 1) * P],
                                scalar=rstd[:, i:i + 1], in1=gain(m), op0=ALU.mult, op1=ALU.mult)
                    last.then_inc(read_out[par], 1)
                return step

            def move_tile1(dst):
                def step():
                    dve.wait_ge(qk_full, n["qk"].up(2))
                    dve.tensor_copy(dst[:, :, P:2 * P],
                                    tr[1][:, :].rearrange("p (m n) -> p m n", m=MAPS)).then_inc(tr_free[1], 1)
                return step

            def mask_scores(m, mask):
                def step():
                    dve.wait_ge(sc_full, n["sc"].up())
                    dve.memset(scratch[:, :], 0.0)
                    for t, c in ((0, slice(0, P)), (1, slice(P, 3 * P))):
                        last = dve.tensor_tensor_reduce(sm[:, m, c], sc[:, c], mask[:, c], SCALE, NEG, ALU.add,
                                                        ALU.max, m8[:, 2 * m + t:2 * m + t + 1])
                    last.then_inc(sc_free, 1)
                return step

            def running_max(quad):
                def step():
                    dve.wait_ge(sc_free, n["sc"](n["sc"].n + 1))
                    chained(dve.tensor_tensor(mn8[:, :], m8[:, :], m_old[:, quad, :], ALU.max))
                    dve.tensor_scalar(neg8[:, :], mn8[:, :], -1.0, None, ALU.mult)
                    chained(dve.tensor_tensor(diff8[:, :], m_old[:, quad, :], mn8[:, :], ALU.subtract))
                    dve.tensor_copy(m_old[:, quad, :], mn8[:, :]).then_inc(smx_done, 1)
                return step

            def negate_max():
                dve.wait_ge(sc_free, n["sc"](n["sc"].n + 1))
                dve.tensor_scalar(neg8[:, :], m8[:, :], -1.0, None, ALU.mult).then_inc(smx_done, 1)

            def move_pt():
                dve.wait_ge(pt_full, n["pt"].up(2))
                dve.tensor_copy(pT[:, 1, :], tr[1][:, 0:3 * P]).then_inc(tr_free[1], 1)

            def merge(quad, pair):
                def step():
                    dve.wait_ge(ov_full, n["ov"].up())
                    if pair == 1:
                        chained(dve.tensor_tensor(den[:, quad, :], den[:, quad, :], corr8[:, :], ALU.mult))
                        dve.tensor_tensor(den[:, quad, :], den[:, quad, :], d8[:, :], ALU.add)
                    for i in range(2):
                        for t in range(T):
                            m = 2 * pair + i
                            o = group_out[:, quad * MAPS + m, t, :]
                            last = dve.scalar_tensor_tensor(
                                out=o, in0=o, scalar=corr8[:, 2 * m + t:2 * m + t + 1],
                                in1=ov[:, (i * T + t) * HD:(i * T + t + 1) * HD], op0=ALU.mult, op1=ALU.add)
                    last.then_inc(ov_free, 1)
                return step

            def mix():
                dve.wait_ge(p_done, n["p"].up(MAPS))
                chained(dve.reciprocal(r8[:, :], d8[:, :]))
                r = r8[:, :].rearrange("p (h c t) -> p h c t", c=2, t=T)
                chained(dve.tensor_scalar(r[:, :, 1, :], r[:, :, 1, :], lam[:, 5:6], None, ALU.mult))
                tiles = [(h, t, slice(0, P) if t == 0 else slice(P, 3 * P)) for h in range(2) for t in range(T)]
                for h, t, c in tiles:
                    last = dve.tensor_scalar(sm[:, 2 * h, c], sm[:, 2 * h, c], r[:, h, 0, t:t + 1], None, ALU.mult)
                chained(last)
                for h, t, c in tiles:
                    last = dve.scalar_tensor_tensor(out=sm[:, 2 * h, c], in0=sm[:, 2 * h + 1, c],
                                                    scalar=r[:, h, 1, t:t + 1], in1=sm[:, 2 * h, c],
                                                    op0=ALU.mult, op1=ALU.add)
                    if t == 1:
                        last.then_inc(mix_done, 1)

            def sub_norm(head):
                def step():
                    dve.wait_ge(sub_rms, n["sub"].up())
                    chained(dve.reciprocal(rstdv[:, :], rmsv[:, :]))
                    chained(dve.tensor_scalar(rstdv[:, :], rstdv[:, :], 1.0 - LAM_INIT, None, ALU.mult))
                    for t in range(T):
                        last = dve.scalar_tensor_tensor(
                            out=head_out[:, head, t, :], in0=ov[:, t * 2 * HD:(t + 1) * 2 * HD],
                            scalar=rstdv[:, t:t + 1], in1=subg[:, :], op0=ALU.mult, op1=ALU.mult)
                    last.then_inc(ov_free, 1)
                return step

            def modulate(j, sections):
                dve.wait_ge(hT_full, n["hT"].up())
                if n["modulated"].n >= 2:
                    dve.wait_ge(hT_split, n["modulated"].n - 1)
                n["modulated"].up()
                for k in range(PK):
                    g_col, s_col = (modc[:, x, PK * j + k:PK * j + k + 1] for x in sections)
                    last = dve.tensor_scalar(stb[:, j % 2, k * T * P:(k + 1) * T * P],
                                             tr[j % 2][:, k * T * P:(k + 1) * T * P], g_col, s_col, ALU.mult, ALU.add)
                last.then_inc(modulated, 1)
                dve.memset(marks[:, j:j + 1], 0.0).then_inc(tr_free[j % 2], 1)

            def low(j, source, done):
                dve.wait_ge(hi_part, n["hi"].up())
                dve.tensor_tensor(hT_lo[:, PK * j:PK * (j + 1), :].rearrange("p k n -> p (k n)"), source,
                                  hT_hi[:, PK * j:PK * (j + 1), :].rearrange("p k n -> p (k n)").bitcast(F32),
                                  ALU.subtract).then_inc(done, 1)

            def low_modulated(j):
                low(j, stb[:, j % 2, :], hT_split)

            def entry(before, sections, g, after=()):
                def start():
                    settled()
                    scale = modc[:, sections[0], :]
                    chained(dve.scalar_tensor_tensor(out=scale, in0=scale, scalar=1.0, in1=vec[:, V_G + g, :],
                                                     op0=ALU.add, op1=ALU.mult))

                def pair(j):
                    def step():
                        if j < PIECES:
                            modulate(j, sections)
                        if j:
                            low_modulated(j - 1)
                    return step

                side = {4: list(before) + [start] + [pair(j) for j in range(4)]}
                for j in range(4, PIECES):
                    side[j + 1] = [pair(j)]
                side[PIECES] = side[PIECES] + [pair(PIECES)] + list(after)
                return side

            def entry_of_heads(before, pairs, after=()):
                def pair(j):
                    def step():
                        n["hT"].up()
                        low(j, tr[j % 2][:, :], tr_free[j % 2])
                    return step

                side = {4: list(before) + [pair(j) for j in range(4)]}
                for j in range(4, pairs):
                    side[j + 1] = [pair(j)]
                side[pairs] = side[pairs] + list(after)
                return side

            def sum_x():
                dve.wait_ge(x_sq, n["sq"].up(4))
                chained(dve.tensor_tensor(pairx[:, :, :], ssx[:, :, 0:2], ssx[:, :, 2:4], ALU.add))
                dve.tensor_tensor(sumx[:, :], pairx[:, :, 0], pairx[:, :, 1], ALU.add).then_inc(x_sum, 1)

            def x_recip():
                dve.wait_ge(x_rms, n["xr"].up())
                dve.reciprocal(rstdx[:, :], rmsx[:, :]).then_inc(x_rstd, 1)

            def ended(back):
                dve.wait_ge(mm_done, n["w"](n["w"].n + SLOTS - back))

            def update(c, back=4):
                def step():
                    ended(back)
                    settled()
                    for t in range(T):
                        last = dve.tensor_tensor(stb[:, t, :], main[c % 2][t][:, :], gate[:, c, :], ALU.mult)
                    last.then_inc(read_out[c % 2], 1)
                    settled()
                    for t in range(T):
                        xc = xs[:, t, cols(c, NC)]
                        last = dve.tensor_tensor(xc, xc, stb[:, t, :], ALU.add)
                    last.then_inc(x_done, 1)
                return step

            dve.sem_inc(lo_done, SLOTS)
            dve.sem_inc(ada_used, ADA_SLOTS)
            for s in (*read_out, *tr_free, sc_free, ov_free):
                dve.sem_inc(s, 1)
            dve.memset(eps_t[:, :], EPS)
            dve.memset(hpi_t[:, :], math.pi / 2).then_inc(eps_set, 1)
            freq = np.float32(500000.0) ** (-np.arange(0, ROT, 2, dtype=np.float32) / np.float32(ROT))
            for i in range(HALF):
                last = dve.memset(inv_freq[:, i:i + 1], float(freq[i]))
            chained(last)
            dve.wait_ge(dist_done, 1)
            for g, low_bits in enumerate((3, 15)):
                last = dve.tensor_scalar(residue_i[:, g * P:(g + 1) * P], dist[:, :], low_bits, None, ALU.bitwise_and)
            chained(last)
            dve.tensor_scalar(residue[:, :], residue_i[:, :], 0.0, NEG, ALU.is_gt, ALU.mult).then_inc(residue_done, 1)
            dve.wait_ge(small_in, 16 * 6)
            dve.wait_ge(vec_full, 1)
            dve.tensor_copy(vec[:, :, :].rearrange("p a b -> p (a b)"), tr[0][:, 0:96]).then_inc(tr_free[0], 1)
            dve.wait_ge(tr_free[0], 2)
            dve.sem_inc(vec_done, 1)
            dve.wait_ge(c_exp, 1)
            chained(dve.tensor_scalar(c_act[:, :], c_act[:, :], 1.0, None, ALU.add))
            chained(dve.reciprocal(c_act[:, :], c_act[:, :]))
            chained(dve.tensor_tensor(c_act[:, :], c_act[:, :], vec[:, V_C, :], ALU.mult))
            lm = st_a[:, 0:NC].rearrange("p (a b) -> p a b", a=4)
            dve.tensor_tensor_reduce(st_b[:, 0:P], lm[:, 0, :], lm[:, 1, :], 1.0, 0.0, ALU.mult, ALU.add, lam[:, 0:1])
            dve.tensor_tensor_reduce(st_b[:, P:2 * P], lm[:, 2, :], lm[:, 3, :], 1.0, 0.0, ALU.mult, ALU.add,
                                     lam[:, 1:2]).then_inc(lam_dot, 1)
            chained(dve.tensor_copy(pos_f[:, :], pos_i[:, :]))
            ang, mag = small[:, 0:T * HALF], small[:, T * HALF:2 * T * HALF]
            for t in range(T):
                last = dve.tensor_scalar(ang[:, t * HALF:(t + 1) * HALF], inv_freq[:, :], pos_f[:, t:t + 1], None, ALU.mult)
            chained(last)
            magic = 1.5 * 2.0 ** 23
            chained(dve.tensor_scalar(turns[:, :], ang, 1.0 / (2 * math.pi), magic, ALU.mult, ALU.add))
            chained(dve.tensor_scalar(turns[:, :], turns[:, :], -magic, None, ALU.add))
            c1 = 6.28125
            c2 = round((2 * math.pi - c1) * 2 ** 20) / 2 ** 20
            for part in (c1, c2, 2 * math.pi - c1 - c2):
                chained(dve.scalar_tensor_tensor(out=ang, in0=turns[:, :], scalar=-part, in1=ang, op0=ALU.mult,
                                                 op1=ALU.add))
            chained(dve.tensor_scalar(ang, ang, 3.1415925, -3.1415925, ALU.min, ALU.max))
            chained(dve.tensor_scalar(mag, ang, -1.0, None, ALU.mult))
            dve.tensor_tensor(mag, mag, ang, ALU.max).then_inc(trig, 1)
            dve.wait_ge(lam_exp, 1)
            chained(dve.tensor_tensor(lam[:, 4:5], lam[:, 3:4], lam[:, 2:3], ALU.subtract))
            chained(dve.tensor_scalar(lam[:, 5:6], lam[:, 4:5], -LAM_INIT, None, ALU.add))

            sum_x()
            for sec in range(2):
                for kt in range(KT):
                    fills, s = divmod(sec * KT + kt, len(ada_start))
                    dve.wait_ge(ada_start_in[s], 16 * (fills + 1))
                    accumulate(kt, ada_start[s])
                for step in (*all_sums, add_columns(sec)):
                    step()
            x_recip()
            q4, k4 = qT[:, 0:MAPS, :], kT[:, :, :]

            def gain_of(i):
                return lambda m: gain_now[:, i * HD:(i + 1) * HD]

            sc4 = [mask_scores(m, mask_now) for m in range(MAPS)]

            def group(g, last):
                if last:
                    q_gain, k_gain, mask = (gains[:, cols(g, HD)], gains[:, cols(g + GROUPS, HD)], masks[:, g, :])
                else:
                    q_gain, k_gain = gains[:, bass.ds(g * HD, HD)], gains[:, bass.ds(g * HD + GROUPS * HD, HD)]
                    mask = masks[:, bass.ds(g, 1), :].rearrange("p a n -> p (a n)")
                dve.tensor_copy(gain_now[:, 0:HD], q_gain)
                dve.tensor_copy(gain_now[:, HD:2 * HD], k_gain)
                chained(dve.tensor_copy(mask_now[:, :], mask))
                chunk(0, PIECES, {4: [move_pt, norm(0, gain_of(0))], 5: [merge(1, 0)], 6: [move_pt],
                                  7: [merge(1, 1)], 8: [move_tile1(q4)]}, ADA_QKV)
                chunk(1, PIECES, {4: [norm(1, gain_of(1))], 8: [move_tile1(k4)]}, ADA_QKV)
                chunk(2, PIECES, None, ADA_QKV)
                chunk(3, PIECES, {4: [norm(1, gain_of(0)), sc4[0]], 5: [sc4[1]], 6: [sc4[2]], 7: [sc4[3]],
                                  8: [move_tile1(q4), running_max(0)]}, ADA_QKV)
                chunk(4, PIECES, {4: [move_pt, norm(0, gain_of(1))], 5: [merge(0, 0)], 6: [move_pt],
                                  7: [merge(0, 1)], 8: [move_tile1(k4)]}, ADA_QKV)
                if not last:
                    chunk(5, PIECES, {4: [sc4[0]], 5: [sc4[1]], 6: [sc4[2], *all_sums[0:2]],
                                      7: [sc4[3], *all_sums[2:4]], 8: [running_max(1), add_columns(g + S_SHIFT_M0)]})

            chunk(0, PIECES, entry([], (S_SCALE_T0, S_SHIFT_T0), 0))
            dve.wait_ge(consts, 3)
            with repeat(dve, GROUPS - 1, n, w=6 * PIECES, ada=KT, landed=KT, col=4, seq=12, rms=4, qk=8, sc=8, pt=8, ov=4) as g:
                group(g, False)
            group(GROUPS - 1, True)

            def invert_den():
                settled()
                dve.reciprocal(rden[:, :], den[:, :, :].rearrange("p a b -> p (a b)")).then_inc(den_inv, 1)

            chunk(0, PIECES // 2, entry_of_heads(
                [*sc4, running_max(1), *all_rows, move_pt, merge(1, 0), move_pt, merge(1, 1), invert_den], 4))
            for c in range(1, 4):
                chunk(c, PIECES // 2, {4: [update(c - 1)]}, ADA_WO)

            def mlp(before, sections, g, ada, first_ada, kt0, gate_at):
                chunk(0, PIECES, entry([update(3), sum_x, *before, x_recip], sections, g))

                def square(par):
                    def step():
                        dve.wait_ge(relu_done, n["relu"].up())
                        for t in range(T):
                            last = dve.scalar_tensor_tensor(out=stb[:, t, :], in0=main[par][t][:, :], scalar=0.0,
                                                            in1=sta[:, t, :], op0=ALU.max, op1=ALU.mult)
                        last.then_inc(read_out[par], 1)
                    return step

                def mid(c):
                    def step():
                        for kp in range(2):
                            dve.wait_ge(mid_full, n["mid"].up())
                            dve.wait_ge(hi_part, n["hi"].up())
                            kt = 4 * c + PK * kp
                            dve.tensor_tensor(mid_lo[:, kt:kt + PK, :],
                                              tr[kp][:, :].rearrange("p (k n) -> p k n", k=PK),
                                              mid_hi[:, kt:kt + PK, :].bitcast(F32),
                                              ALU.subtract).then_inc(tr_free[kp], 1)
                    return step

                def block(i, last=False):
                    sides = [{4: [square(1 - c % 2)], 7: [mid(c - 1)]} for c in range(1, 5)]
                    sides += [{4: [update(c)]} for c in range(3)]
                    first = isinstance(i, int) and i == 0
                    if first:
                        sides[gate_at][1], sides[gate_at][2] = all_rows[0:2], all_rows[2:4]
                    if ada:
                        sides[6][PIECES] = [*all_sums, add_mixed_columns(i)]
                    for c in range(7):
                        chunk(c, PIECES, sides[c], first_ada if first else ada, kt0 if first else 0)
                    if not last:
                        chunk(7, PIECES, {4: [update(3)]})

                rises = dict(w=8 * PIECES, relu=4, mid=8, hi=8, seq=8)
                if ada:
                    rises.update(ada=KT, landed=KT, col=4, seq=9)
                block(0)
                with repeat(dve, 2, n, **rises) as i:
                    block(i + 1)
                block(3, True)

            mlp([], (S_SCALE_M0, S_SHIFT_M0), 1, ADA_MLP, ADA_GATE + ADA_FIRST, len(ADA_WO), 3)

            def map_gain(row):
                return lambda m: gains[:, (row + m % 2) * HD:(row + m % 2 + 1) * HD]

            for ch in range(4):
                chunk(ch, PIECES, {4: [norm(1 - ch % 2, map_gain(8))],
                                   8: [move_tile1(qT[:, (ch - 1) * MAPS:ch * MAPS, :])]} if ch else
                      entry([update(3), sum_x, x_recip], (S_SCALE_T1, S_SHIFT_T1), 2), ADA_Q)
            causal = [mask_scores(m, masks[:, 3, :]) for m in range(MAPS)]
            chunk(4, PIECES, entry([norm(1, map_gain(8))], (S_SCALE_KV, S_SHIFT_KV), 4,
                                   [move_tile1(qT[:, 3 * MAPS:4 * MAPS, :])]), ADA_Q)
            n["p"].up(2 * MAPS * GROUPS + MAPS)
            chunk(1, PIECES, {4: [norm(0, map_gain(6))], 5: all_rows[0:2], 6: all_rows[2:4], 8: [move_tile1(k4)]}, ADA_KV)
            for u in range(1, 4):
                chunk(2 * u, PIECES, {4: [causal[0]], 5: [causal[1]], 6: [causal[2]], 7: [causal[3]],
                                      8: [negate_max]}, ADA_KV)
                chunk(2 * u + 1, PIECES, {2: [mix], 4: [move_pt, norm(0, map_gain(6))], 6: [sub_norm(2 * u - 2)],
                                          8: [move_tile1(k4), sub_norm(2 * u - 1)]}, ADA_KV)
            chunk(0, PIECES, entry_of_heads([*causal, negate_max, *all_sums, add_columns(S_SCALE_M1), mix, move_pt,
                                             sub_norm(6), sub_norm(7)], PIECES), ADA_WO_B)
            for c in range(1, 4):
                chunk(c, PIECES, {4: [update(c - 1)]}, ADA_WO_B)
            mlp([*all_sums, add_columns(S_SHIFT_M1)], (S_SCALE_M1, S_SHIFT_M1), 3, (), ADA_GATE_B, 0, 4)
            update(3, 0)()

        @block.gpsimd
        def _(pool):
            n = Counts()

            def chained(ins):
                ins.then_inc(seq_g, 1)
                pool.wait_ge(seq_g, n["seq"].up())

            def stage(pairs, source):
                for j in pairs:
                    if n["hT"].n > 1:
                        pool.wait_ge(hT_full, n["hT"](n["hT"].n - 1))
                    n["hT"].up()
                    for dst, src, scale in source(j, stx[:, j % 2, :]):
                        last = pool.tensor_scalar(dst, src, scale, 1.0, ALU.mult, ALU.mult)
                    last.then_inc(staged, 1)

            def x_rows(j, dst):
                return [(dst[:, t * PK * P:(t + 1) * PK * P], xs[:, t, j * PK * P:(j + 1) * PK * P],
                         rstdx[:, t:t + 1]) for t in range(T)]

            def head_rows(j, dst):
                return [(dst[:, (t * PK + k) * P:(t * PK + k + 1) * P], group_out[:, PK * j + k, t, :],
                         rden[:, (PK * j + k) * T + t:(PK * j + k) * T + t + 1]) for t in range(T) for k in range(PK)]

            def rope(par):
                pool.wait_ge(read_out[par], n[f"ro{par}"](n[f"ro{par}"].n + 1))
                for t in range(T):
                    v = sta[:, t, :].rearrange("p (m e) -> p m e", m=MAPS)
                    t1, t2 = v[:, :, 0:HALF], v[:, :, HALF:ROT]
                    c = cos[:, t * HALF:(t + 1) * HALF].unsqueeze(1).to_broadcast([P, MAPS, HALF])
                    s = sin[:, t * HALF:(t + 1) * HALF].unsqueeze(1).to_broadcast([P, MAPS, HALF])
                    pool.tensor_tensor(rot[:, t, 0], t1, c, ALU.mult)
                    pool.tensor_tensor(rot[:, t, 1], t2, s, ALU.mult)
                    pool.tensor_tensor(rot[:, t, 2], t2, c, ALU.mult)
                    last = pool.tensor_tensor(rot[:, t, 3], t1, s, ALU.mult)
                chained(last)
                for t in range(T):
                    v = sta[:, t, :].rearrange("p (m e) -> p m e", m=MAPS)
                    pool.tensor_tensor(v[:, :, 0:HALF], rot[:, t, 0], rot[:, t, 1], ALU.subtract)
                    last = pool.tensor_tensor(v[:, :, HALF:ROT], rot[:, t, 2], rot[:, t, 3], ALU.add)
                last.then_inc(roped, 1)

            def passed(par):
                n[f"ro{par}"].up()

            chained(pool.memset(ident[:, :], 0.0))
            pool.affine_select(out=ident[:, :], in_=ident[:, :], compare_op=ALU.not_equal, fill=1.0, base=0,
                               pattern=[[-1, P]], channel_multiplier=1).then_inc(consts, 1)
            pool.memset(ones[:, :], 1.0).then_inc(consts, 1)
            pool.iota(dist[:, :], base=P, pattern=[[-1, P]], channel_multiplier=1).then_inc(dist_done, 1)
            pool.memset(group_out[:, :, :, :], 0.0)
            pool.memset(m_old[:, :, :], NEG)
            pool.memset(den[:, :, :], 0.0)
            pool.memset(d8[:, :], 0.0)
            pool.memset(corr8[:, :], 1.0)
            pool.memset(vv[:, :, :], 0.0)
            chained(pool.memset(masks[:, :, :], 0.0))
            pool.wait_ge(residue_done, 1)
            for g in range(1, GROUPS):
                for b in range(3):
                    pool.tensor_copy(masks[:, g, b * P:(b + 1) * P], residue[:, (g - 1) * P:g * P])
            chained(pool.memset(scratch_g[:, :], 0.0))
            for g in range(4):
                for b in (0, 2):
                    last = pool.affine_select(out=masks[:, g, b * P:(b + 1) * P], in_=masks[:, g, b * P:(b + 1) * P],
                                              compare_op=ALU.is_ge, fill=NEG, base=0, pattern=[[-1, P]],
                                              channel_multiplier=1)
            last = pool.affine_select(out=masks[:, 0, P:2 * P], in_=masks[:, 0, P:2 * P], compare_op=ALU.is_ge,
                                      fill=NEG, base=0, pattern=[[1, P]], channel_multiplier=-1)
            last.then_inc(consts, 1)
            pool.wait_ge(vec_full, 1)
            pool.memset(sm[:, :, :], 0.0).then_inc(p_done, MAPS)
            pool.wait_ge(trig_done, 1)
            pool.wait_ge(x_rstd, 1)
            pairs = range(PIECES)
            stage(pairs, x_rows)

            def group():
                passed(0)
                rope(0)
                passed(1)
                rope(1)
                passed(0)
                passed(1)
                rope(1)
                passed(0)
                rope(0)
                passed(1)

            with repeat(pool, GROUPS, n, ro0=3, ro1=3, seq=4):
                group()
            pool.wait_ge(den_inv, 1)
            stage(range(PIECES // 2), head_rows)
            n["ro0"].up(2)
            n["ro1"].up(2)
            pool.wait_ge(x_rstd, 2)
            stage(pairs, x_rows)
            n["ro0"].up(16)
            n["ro1"].up(16)
            pool.wait_ge(x_rstd, 3)
            stage(pairs, x_rows)
            for ch in range(3):
                passed(ch % 2)
                rope(ch % 2)
            stage(range(6), x_rows)
            passed(1)
            rope(1)
            stage(range(6, PIECES), x_rows)
            for u in range(4):
                passed(0)
                rope(0)
                passed(1)
            n["hT"].up(PIECES)
            n["ro0"].up(2)
            n["ro1"].up(2)
            pool.wait_ge(x_rstd, 4)
            stage(pairs, x_rows)


def kernel(**inputs):
    from concourse import bacc
    from concourse.bass_utils import run_bass_kernel_spmd

    f = {k: np.asarray(v) for k, v in inputs.items()}

    def section(name, s):
        w, b = (f["kv_ada_w"], f["kv_ada_b"]) if name == "kv" else (f["ada_w"][name], f["ada_b"][name])
        return w[:, cols(s, D)], b[cols(s, D)]

    order = [section(*a) for a in ((0, 0), (0, 1), (0, 3), (0, 4), (0, 2), (0, 5), (1, 0), (1, 1), ("kv", 0), ("kv", 1),
                                   (1, 2), (1, 4), (1, 3), (1, 5))]
    ada = [w for w, _ in order]
    ada[6:10] = [np.concatenate([w[:, cols(i, NC)] for w in ada[6:10]], axis=1) for i in range(4)]
    bias = [b for _, b in order]
    bias_cols = np.stack([b.reshape(KT, P) for b in (*bias[0:4], *bias[6:10], bias[12], bias[11])])

    def pieces(w):
        k, m = w.shape
        return w.reshape(k // (PK * P), PK, P, m // NC, NC).transpose(3, 0, 2, 1, 4).reshape(-1, PK * NC)

    qkv = f["a_w_qkv"][0].reshape(D, GROUPS, 3, 2, NC)
    stream = []
    for g in range(GROUPS):
        for quad in range(2):
            for part in range(3):
                stream.append(pieces(qkv[:, g, part, quad]))
    stream.append(pieces(f["a_w_o"][0]))
    for layer in range(LAYERS):
        if layer:
            stream.append(pieces(f["b_w_q"][0]))
            for u in range(4):
                stream += [pieces(f["kv_w_k"][:, cols(u, NC)]), pieces(f["kv_w_v"][:, cols(u, NC)])]
            stream.append(pieces(f["b_w_o"][0]))
        for b in range(4):
            stream += [pieces(f["mlp_w1"][layer][:, cols(b, D)]), pieces(f["mlp_w2"][layer][cols(b, D)])]
    vecs = np.concatenate([f["c"].reshape(-1, P), f["norm_g"].reshape(-1, P), f["kv_norm_g"].reshape(-1, P)])
    gains = np.concatenate([f["a_q_gain"][0], f["a_k_gain"][0], f["kv_k_gain"], f["b_q_gain"][0]])
    arrays = {
        "x": f["x"].reshape(SEQ, D),
        "vecs": vecs,
        "pos": f["positions"].reshape(T, P).T,
        "gains": gains.reshape(-1),
        "subg": f["b_subln_g"].reshape(-1),
        "lamb": f["b_lambda"].reshape(-1),
        "ada": np.concatenate(ada),
        "bias_cols": bias_cols.transpose(2, 0, 1),
        "bias_rows": np.stack([bias[4], bias[5], bias[10], bias[13]]),
        "w": np.concatenate(stream),
    }
    nc = bacc.Bacc("TRN2", target_bir_lowering=False, num_devices=1)
    args = []
    arrays = {k: np.ascontiguousarray(a) for k, a in arrays.items()}
    for name, a in arrays.items():
        args.append(nc.dram_tensor(name, a.shape, mybir.dt.from_np(a.dtype), kind="ExternalInput").ap())
    args.append(nc.dram_tensor("out", (SEQ, D), F32, kind="ExternalOutput").ap())
    trunk(nc, *args)
    r = run_bass_kernel_spmd(nc, [arrays], core_ids=[0])
    return r.results[0]["out"].reshape(1, SEQ, D)
```

```python
import math
from contextlib import ExitStack, contextmanager

import numpy as np

import concourse.bass as bass
from concourse import mybir

P = 128
SEQ = 256
T = SEQ // P
D = 2048
KT = D // P
NC = 512
PK = 2
PIECES = KT // PK
SLOTS = 4
ADA_SLOTS = 2
HD = 128
HEADS_A = 8
GROUPS = 3
D_FF = 4 * D
ROT = 32
HALF = ROT // 2
EPS = 1e-6
NEG = -1e30
SCALE = float(HD) ** -0.5
LAM_INIT = 0.8 - 0.6 * math.exp(-0.3)
LAYERS = 2
MAPS = 4
V_C, V_G = 0, 1
(S_SHIFT_T0, S_SCALE_T0, S_SHIFT_M0, S_SCALE_M0, S_SHIFT_T1, S_SCALE_T1, S_SHIFT_KV, S_SCALE_KV, S_SHIFT_M1,
 S_SCALE_M1) = range(10)
MIXED = 4

ALU = mybir.AluOpType
ACT = mybir.ActivationFunctionType
F32 = mybir.dt.float32
F32R = mybir.dt.float32r
BF16 = mybir.dt.bfloat16
I32 = mybir.dt.int32


class Count:

    def __init__(self):
        self.n, self.base = 0, None

    def up(self, k=1):
        self.n += k
        return self()

    def __call__(self, at=None):
        v = self.n if at is None else at
        return v if self.base is None else self.base + v


class Counts(dict):
    def __missing__(self, name):
        self[name] = Count()
        return self[name]


@contextmanager
def repeat(eng, times, counts, **rises):
    before = {k: c.n for k, c in counts.items()}
    with eng.Fori(0, times) as i:
        for k, r in rises.items():
            counts[k].base = i * r
        yield i
        grown = {k: c.n - before.get(k, 0) for k, c in counts.items() if c.n != before.get(k, 0)}
        assert grown == rises, grown
    for k, r in rises.items():
        counts[k].n += (times - 1) * r
        counts[k].base = None


def cols(i, size):
    return slice(i * size, (i + 1) * size) if isinstance(i, int) else bass.ds(i * size, size)


def after(*lists, first=0):
    return [(c, j) for c, js in enumerate(lists, first) for j in js]


ADA_QKV = after((0, 5, 7), (0, 5, 7), (0, 2, 4, 6), (0, 5, 7), (0, 5, 7))
DRAIN = 2
ADA_WO = after((0, 2), (0, 2), (0,), first=1)
ADA_ENTRY = after((5, 7))
ADA_GATE = after((1, 3, 5, 7), (0, 2, 4))
ADA_FIRST = after((3, 5, 7), (1, 4, 7), (0, 2, 5), (0, 2, 5), (0, 1, 2, 4), first=2)
ADA_MLP = after((1, 5), (1, 5), (1, 5), (1, 5), (1, 5), (0, 2, 5), (0, 2, 4))
ADA_Q = after((), (0, 5, 7), (0, 5, 7), (0, 5, 7), (7,), (0, 5, 7), (0, 1, 2))
ADA_K = after((7,), (0, 1, 5, 7), (0, 2, 5, 7), (0, 1, 5, 7), (0, 1, 2), first=2)
ADA_V = after((7,), (0, 5, 7), (0, 2), (5, 6, 7), (0, 5, 6, 7), (0, 5, 7), first=6)
ADA_GATE_B = after((0, 2, 5, 7), (0, 2, 5, 7), (0, 3, 6), (0, 2, 4))


def trunk(nc, x_in, vecs_in, pos_in, gains_in, subg_in, lamb_in, ada_in, bias_cols_in, bias_rows_in, w_in, out):
    ctx = ExitStack()
    with ctx:
        def sb(name, shape, dt=F32):
            return ctx.enter_context(nc.sbuf_tensor(name, shape, dt))

        sems = {}

        def sem(name):
            if name not in sems:
                sems[name] = ctx.enter_context(nc.semaphore(name))
            return sems[name]

        w_raw = sb("w_raw", [P, SLOTS, PK * NC])
        w_hi = sb("w_hi", [P, SLOTS, PK * NC], F32R)
        w_lo = sb("w_lo", [P, SLOTS, PK * NC], F32R)
        ada_raw = sb("ada_raw", [P, ADA_SLOTS, D])
        acc = sb("acc", [P, D])
        gate = sb("gate", [P, 4, NC])
        xs = sb("xs", [P, T, D])
        work = sb("work", [P, 2 * D])
        hT_hi = sb("hT_hi", [P, KT, T * P], F32R)
        hT_lo = sb("hT_lo", [P, KT, T * P], F32R)
        st_a = sb("st_a", [P, T * NC])
        st_b = sb("st_b", [P, T * NC])
        st_x = sb("st_x", [P, T * NC])
        pT = sb("pT", [P, 2, 3 * P])
        masks = sb("masks", [P, 4, 3 * P], BF16)
        gain_now = sb("gain_now", [P, 2 * HD])
        mask_now = sb("mask_now", [P, 3 * P], BF16)
        gains = sb("gains_sb", [P, 10 * HD])
        subg = sb("subg_sb", [P, 2 * HD])
        ident = sb("ident", [P, P])
        ones = sb("ones", [P, P])
        vec = sb("vec", [P, 6, KT])
        c_act = sb("c_act", [P, KT])
        modc = sb("modc", [P, 10, KT])
        sums = sb("sums", [P, KT])
        cos = sb("cos", [P, T * HALF])
        sin = sb("sin", [P, T * HALF])
        small = sb("small", [P, 64])
        ssq = sb("ssq", [P, 8])
        rms = sb("rms", [P, 8])
        rstd = sb("rstd", [P, 8])
        ssx = sb("ssx", [P, T, 4])
        pairx = sb("pairx", [P, T, 2])
        sumx = sb("sumx", [P, T])
        rmsx = sb("rmsx", [P, 2])
        rstdx = sb("rstdx", [P, 2])
        m8 = sb("m8", [P, 8])
        mn8 = sb("mn8", [P, 8])
        neg8 = sb("neg8", [P, 8])
        diff8 = sb("diff8", [P, 8])
        corr8 = sb("corr8", [P, 8])
        d8 = sb("d8", [P, 8])
        r8 = sb("r8", [P, 8])
        m_old = sb("m_old", [P, 2, 8])
        den = sb("den", [P, 2, 8])
        rden = sb("rden", [P, 16])
        eps_t = sb("eps_t", [P, 1])
        hpi_t = sb("hpi_t", [P, 1])
        lam = sb("lam", [P, 8])
        ssv = sb("ssv", [P, 2])
        rmsv = sb("rmsv", [P, 2])
        rstdv = sb("rstdv", [P, 2])
        inv_freq = sb("inv_freq", [P, HALF])
        pos_f = sb("pos_f", [P, T])
        turns = sb("turns", [P, T * HALF])
        rot = sb("rot", [P, T, 4, MAPS, HALF])
        scratch = sb("scratch", [P, 1])
        marks = sb("marks", [P, PIECES])
        scratch_g = sb("scratch_g", [P, 1])
        pos_i = sb("pos_i", [P, T], I32)

        with nc.sbuf_tensor("mid_hi", [P, KT, T * P], F32R) as mid_hi, \
                nc.sbuf_tensor("mid_lo", [P, KT, T * P], F32R) as mid_lo:
            pass
        qT = sb("qT", [P, 16, T * P])
        kT = sb("kT", [P, MAPS, T * P])
        vv = sb("vv", [P, T, NC])
        sm = sb("sm", [P, MAPS, 3 * P])
        residue_i = sm[:, 0, 0:2 * P].bitcast(I32)
        dist = sm[:, 1, 0:P].bitcast(I32)
        residue = sm[:, 2, 0:P].bitcast(BF16)
        cols_in = sm[:, 3, 0:P]
        ada_start = [ada_raw[:, 0, :], ada_raw[:, 1, :],
                     *(qT[:, a * 8:(a + 1) * 8, :].rearrange("p a b -> p (a b)") for a in range(2))]

        main = [[ctx.enter_context(nc.psum_tensor(f"main{p}{t}", [P, NC], F32)) for t in range(T)] for p in range(2)]
        tr = [ctx.enter_context(nc.psum_tensor(f"tr{b}", [P, NC], F32)) for b in range(2)]
        sc = ctx.enter_context(nc.psum_tensor("sc", [P, NC], F32))
        ov = ctx.enter_context(nc.psum_tensor("ov", [P, NC], F32))

        sta = st_a[:, :].rearrange("p (t n) -> p t n", t=T)
        stb = st_b[:, :].rearrange("p (t n) -> p t n", t=T)
        stx = st_x[:, :].rearrange("p (t n) -> p t n", t=T)
        acc_rows = acc[:, :].rearrange("p (n c) -> p n c", c=NC)
        group_out = work[:, 0:D].rearrange("p (h t e) -> p h t e", t=T, e=HD)
        head_out = work[:, :].rearrange("p (h t e) -> p h t e", t=T, e=2 * HD)
        wv = w_in.rearrange("(n p) c -> n p c", p=P)
        av = ada_in.rearrange("(n p) c -> n p c", p=P)

        raw_in = [sem(f"raw_in{s}") for s in range(SLOTS)]
        hi_done = sem("hi_done")
        lo_done = sem("lo_done")
        mm_done = sem("mm_done")
        ada_in = [sem(f"ada_in{s}") for s in range(ADA_SLOTS)]
        ada_start_in = [sem(f"ada_start_in{s}") for s in range(len(ada_start))]
        ada_used = sem("ada_used")
        gate_bias = sem("gate_bias")
        read_out = [sem(f"read_out{p}") for p in range(2)]
        tr_free = [sem(f"tr_free{b}") for b in range(2)]
        vec_full, col_full, row_full = sem("vec_full"), sem("col_full"), sem("row_full")
        hT_full, mid_full, qk_full, pt_full = sem("hT_full"), sem("mid_full"), sem("qk_full"), sem("pt_full")
        modulated = sem("modulated")
        hT_split = sem("hT_split")
        hi_part = sem("hi_part")
        sc_full, sc_free = sem("sc_full"), sem("sc_free")
        ov_full, ov_free = sem("ov_full"), sem("ov_free")
        rms_done, roped = sem("rms_done"), sem("roped")
        staged = sem("staged")
        x_rms, x_rstd, x_done = sem("x_rms"), sem("x_rstd"), sem("x_done")
        relu_done = sem("relu_done")
        smx_done, p_done, mix_done = sem("smx_done"), sem("p_done"), sem("mix_done")
        sub_rms, den_inv = sem("sub_rms"), sem("den_inv")
        mod_done, x_sq, x_sum = sem("mod_done"), sem("x_sq"), sem("x_sum")
        seq_v, seq_a, seq_g = sem("seq_v"), sem("seq_a"), sem("seq_g")
        small_in, x_in_done, stored = sem("small_in"), sem("x_in_done"), sem("stored")
        consts, trig, c_exp, c_done = sem("consts"), sem("trig"), sem("c_exp"), sem("c_done")
        eps_set, dist_done, residue_done = sem("eps_set"), sem("dist_done"), sem("residue_done")
        vec_done, lam_dot, lam_exp, trig_done = sem("vec_done"), sem("lam_dot"), sem("lam_exp"), sem("trig_done")

        block = ctx.enter_context(nc.Block())

        @block.sync
        def _(sp):
            n = Counts()

            def weight_piece():
                n["w"].up()
                s = (n["w"].n - 1) % SLOTS
                sp.wait_ge(lo_done, n["w"]())
                at = n["w"](n["w"].n - 1)
                src = wv[at] if isinstance(at, int) else wv[bass.ds(at, 1), :, :].rearrange("a p c -> p (a c)")
                sp.dma_start(w_raw[:, s, :], src).then_inc(raw_in[s], 16)

            def row(v, at):
                return v[at] if isinstance(at, int) else v[bass.ds(at, 1), :, :].rearrange("a p c -> p (a c)")

            def ada_piece():
                n["ada"].up()
                s = (n["ada"].n - 1) % ADA_SLOTS
                sp.wait_ge(ada_used, n["ada"]())
                sp.dma_start(ada_raw[:, s, :], row(av, n["ada"](n["ada"].n - 1))).then_inc(ada_in[s], 16)

            def bias(gate_no, updates):
                if updates:
                    sp.wait_ge(x_done, updates)
                sp.dma_start(gate[:, :, :].rearrange("p n c -> p (n c)"),
                             bias_rows_in[gate_no].partition_broadcast(P)).then_inc(gate_bias, 16)

            def chunk(ch, pieces=PIECES, ada=()):
                for j in range(pieces):
                    weight_piece()
                    if (ch, j) in ada:
                        ada_piece()

            sp.dma_start(cols_in[0:96, :], vecs_in).then_inc(small_in, 16)
            sp.dma_start(pos_i[:, :], pos_in).then_inc(small_in, 16)
            sp.dma_start(gains[:, :], gains_in.partition_broadcast(P)).then_inc(small_in, 16)
            sp.dma_start(subg[:, :], subg_in.partition_broadcast(P)).then_inc(small_in, 16)
            sp.dma_start(modc[:, :, :], bias_cols_in).then_inc(small_in, 16)
            sp.dma_start(st_a[:, 0:NC], lamb_in.partition_broadcast(P)).then_inc(small_in, 16)
            sp.dma_start(xs[:, :, :], x_in.rearrange("(t p) d -> p t d", p=P)).then_inc(x_in_done, 16)
            for a in range(2 * KT):
                s = a % len(ada_start)
                if a >= len(ada_start):
                    sp.wait_ge(ada_used, ADA_SLOTS + a + 1 - len(ada_start))
                sp.dma_start(ada_start[s], av[a]).then_inc(ada_start_in[s], 16)
            n["ada"].up(2 * KT)
            chunk(0)
            with repeat(sp, GROUPS - 1, n, ada=KT, w=6 * PIECES):
                for ch in range(6):
                    chunk(ch, ada=ADA_QKV)
            bias(0, 0)
            for ch in range(5):
                chunk(ch, ada=ADA_QKV)
            for ch in range(4):
                chunk(ch, PIECES // 2, after((2, 3)) + ADA_WO)
            chunk(0, ada=ADA_ENTRY)
            bias(1, 4)
            for ch in range(8):
                chunk(ch, ada=ADA_GATE + ADA_FIRST)
            with repeat(sp, 2, n, ada=KT, w=8 * PIECES):
                for ch in range(8):
                    chunk(ch, ada=ADA_MLP)
            for ch in range(7):
                chunk(ch, ada=ADA_MLP)
            chunk(0, ada=ADA_Q)
            bias(2, 4 + 16)
            for ch in range(1, 4):
                chunk(ch, ada=ADA_Q)
            for ch in range(12):
                chunk(ch, ada=[(c - 4, j) for c, j in ADA_Q] + [(c, j) for c, j in ADA_K + ADA_V])
            chunk(0, ada=ADA_ENTRY)
            bias(3, 4 + 16 + 4)
            for ch in range(8):
                chunk(ch, ada=ADA_GATE_B)
            with repeat(sp, 2, n, w=8 * PIECES):
                for ch in range(8):
                    chunk(ch)
            for ch in range(7):
                chunk(ch)
            for c in range(4):
                sp.wait_ge(x_done, 4 + 16 + 4 + 12 + c + 1)
                sp.dma_start(out.rearrange("(t p) d -> p t d", p=P)[:, :, cols(c, NC)],
                             xs[:, :, cols(c, NC)]).then_inc(stored, 16)
            sp.wait_ge(stored, 4 * 16)

        @block.tensor
        def _(pe):
            n = Counts()

            def claim_tr(b):
                n[f"tr{b}"].up()
                pe.wait_ge(tr_free[b], n[f"tr{b}"]())

            def claim_main(par):
                n[f"ro{par}"].up()
                pe.wait_ge(read_out[par], n[f"ro{par}"]())

            def gemm(par, pairs, hi, lo, side=None, ready=None):
                claim_main(par)
                for j in range(pairs):
                    n["w"].up()
                    s = (n["w"].n - 1) % SLOTS
                    if ready:
                        ready(j)
                    pe.wait_ge(lo_done, n["w"](n["w"].n + SLOTS))
                    for k in range(PK):
                        kt = PK * j + k
                        wc = slice(k * NC, (k + 1) * NC)
                        for t in range(T):
                            acc_ps, tc = main[par][t], slice(t * P, (t + 1) * P)
                            pe.matmul(acc_ps[:, :], hi[:, kt, tc], w_hi[:, s, wc], start=(kt == 0), stop=False)
                            pe.matmul(acc_ps[:, :], hi[:, kt, tc], w_lo[:, s, wc], start=False, stop=False)
                            last = pe.matmul(acc_ps[:, :], lo[:, kt, tc], w_hi[:, s, wc], start=False,
                                             stop=(kt == PK * pairs - 1))
                    last.then_inc(mm_done, 1)
                    for step in (side or {}).get(j, ()):
                        step()

            def pair_transposes(b, source):
                for k in range(PK):
                    for t in range(T):
                        at = k * T * P + t * P
                        last = pe.transpose(tr[b][:, at:at + P], source(k, t), ident[:, :])
                return last

            def build(pairs=PIECES, source=None, modulate=True, ahead=4, between=0):
                first, made, made_split = [n["tr0"].n, n["tr1"].n], [0], n["split"].n
                n["split"].up(pairs if modulate else 0)

                def transposes():
                    j = made[0]
                    made[0] += 1
                    claim_tr(j % 2)
                    if source is None:
                        n["staged"].up()
                        pe.wait_ge(staged, n["staged"]())
                        last = pair_transposes(j % 2, lambda k, t: stx[:, j % 2, (t * PK + k) * P:(t * PK + k + 1) * P])
                    else:
                        last = pair_transposes(j % 2, lambda k, t: source(PK * j + k, t))
                    last.then_inc(hT_full, 1)

                def ready(j):
                    if modulate:
                        pe.wait_ge(hT_split, made_split + j + 1)
                    else:
                        late = between if j >= pairs - 2 else 0
                        pe.wait_ge(tr_free[j % 2], first[j % 2] + j // 2 + 2 + late)

                for _ in range(ahead):
                    transposes()
                return {j: [transposes] for j in range(pairs - ahead)}, ready

            def sum_columns(quarter):
                def step():
                    if quarter == 0:
                        n["ada"].up(KT)
                        pe.wait_ge(ada_used, n["ada"](n["ada"].n + ADA_SLOTS))
                    b = quarter % 2
                    claim_tr(b)
                    for k in range(4):
                        last = pe.transpose(tr[b][:, k * P:(k + 1) * P], acc_rows[:, quarter, k * P:(k + 1) * P],
                                            ident[:, :])
                    last.then_inc(col_full, 1)
                return step

            def sum_rows(quarter):
                def step():
                    if quarter == 0:
                        n["ada"].up(KT)
                        pe.wait_ge(ada_used, n["ada"](n["ada"].n + ADA_SLOTS))
                    claim_tr(quarter % 2)
                    pe.matmul(tr[quarter % 2][:, :], ones[:, :], acc_rows[:, quarter, :], start=True,
                              stop=True).then_inc(row_full, 1)
                return step

            def qk_transposes():
                pe.wait_ge(roped, n["roped"].up())
                for t in range(T):
                    claim_tr(t)
                    for m in range(MAPS):
                        last = pe.transpose(tr[t][:, m * P:(m + 1) * P], sta[:, t, m * P:(m + 1) * P], ident[:, :])
                    last.then_inc(qk_full, 1)

            def scores(m, q0=0):
                def step():
                    if m == 0:
                        for b in range(2):
                            pe.wait_ge(tr_free[b], n[f"tr{b}"](n[f"tr{b}"].n + 1))
                    pe.wait_ge(sc_free, n["sc"].up())
                    q, k = qT[:, q0 + m, :], kT[:, m, :]
                    pe.matmul(sc[:, 0:P], q[:, 0:P], k[:, 0:P], start=True, stop=True)
                    pe.matmul(sc[:, P:3 * P], q[:, P:2 * P], k[:, :], start=True, stop=True).then_inc(sc_full, 1)
                return step

            def p_transposes(i, m, ready, name):
                def step():
                    pe.wait_ge(ready, n[name].up())
                    claim_tr(i)
                    for c in range(3):
                        last = pe.transpose(tr[i][:, c * P:(c + 1) * P], sm[:, m, c * P:(c + 1) * P], ident[:, :])
                    last.then_inc(pt_full, 1)
                return step

            def pv(i, width, at, v0):
                a, b = ov[:, at:at + width], ov[:, at + width:at + 2 * width]
                pe.matmul(a, pT[:, i, 0:P], vv[:, 0, v0:v0 + width], start=True, stop=True)
                pe.matmul(b, pT[:, i, P:2 * P], vv[:, 0, v0:v0 + width], start=True, stop=False)
                return pe.matmul(b, pT[:, i, 2 * P:3 * P], vv[:, 1, v0:v0 + width], start=False, stop=True)

            def wait_pt(i, later=0):
                pe.wait_ge(tr_free[i], n[f"tr{i}"](n[f"tr{i}"].n + 1 - later))

            def values_ready(par, back):
                pe.wait_ge(read_out[par], n[f"ro{par}"](n[f"ro{par}"].n + 1 - back))

            def pv_pair(pair, par, back):
                def step():
                    pe.wait_ge(ov_free, n["ov"].up())
                    values_ready(par, back)
                    for i in range(2):
                        wait_pt(i)
                        last = pv(i, HD, 2 * HD * i, (2 * pair + i) * HD)
                    last.then_inc(ov_full, 1)
                return step

            def pv_head(h, back, later=0):
                def step():
                    pe.wait_ge(ov_free, n["ov"].up())
                    values_ready(1, back)
                    wait_pt(h, later)
                    pv(h, 2 * HD, 0, h * 2 * HD).then_inc(ov_full, 1)
                return step

            def attn_a(par, back):
                pt = [[p_transposes(i, 2 * pair + i, p_done, "p") for i in range(2)] for pair in range(2)]
                return ({m: [scores(m)] for m in range(MAPS)},
                        {0: pt[0], 1: [pv_pair(0, par, back)], 2: pt[1], 3: [pv_pair(1, par, back)]})

            def attn_b(q0, back):
                pt = [p_transposes(h, 2 * h, mix_done, "mix") for h in range(2)]
                return ({m: [scores(m, q0)] for m in range(MAPS)},
                        {1: pt, 2: [pv_head(0, back)], 4: [pv_head(1, back, back)]})

            def also(side, *others):
                side = {j: list(steps) for j, steps in side.items()}
                for other in others:
                    for j, steps in other.items():
                        side[j] = side.get(j, []) + list(steps)
                return side

            def halves(sum_of, j):
                return {j: [sum_of(0), sum_of(1)], j + 1: [sum_of(2), sum_of(3)]}

            def all_of(*sides):
                for side in sides:
                    for j in sorted(side):
                        for step in side[j]:
                            step()

            qk = {3: [qk_transposes]}
            pe.sem_inc(mm_done, SLOTS)
            pe.wait_ge(consts, 2)
            pe.wait_ge(small_in, 16 * 6)
            claim_tr(0)
            pe.transpose(tr[0][:, 0:96], cols_in[0:96, :], ident[0:96, 0:96]).then_inc(vec_full, 1)
            for _ in range(2):
                all_of(halves(sum_columns, 0))

            h = (PIECES, hT_hi, hT_lo)
            side, ready = build()
            gemm(0, *h, side=side, ready=ready)

            def group(last):
                gemm(1, *h, side=also(attn_a(1, 1)[1], qk))
                gemm(0, *h, side=qk)
                gemm(1, *h)
                scores_, values_ = attn_a(0, 1)
                gemm(0, *h, side=also(scores_, qk))
                early = {5 + m: attn_a(1, 0)[0][m] for m in range(3)} if last else {}
                gemm(1, *h, side=also(values_, qk, early))
                if not last:
                    gemm(0, *h, side=also(attn_a(1, 1)[0], halves(sum_columns, 1)))

            with repeat(pe, GROUPS - 1, n, ada=KT, w=6 * PIECES, ro0=3, ro1=3, roped=4, tr0=10, tr1=10, sc=8,
                        p=8, ov=4):
                group(False)
            group(True)
            scores_, values_ = attn_a(1, 0)
            scores_[3][0]()
            side, ready = build(PIECES // 2, modulate=False, ahead=2, between=4)
            attention = [step for j in range(4) for step in values_[j]]
            for ch in range(4):
                gemm(ch % 2, PIECES // 2, hT_hi, hT_lo, ready=ready if ch == 0 else None,
                     side={0: [sum_rows(quarter) for quarter in range(4)], 1: attention + side[0] + side[1]}
                     if ch == 0 else None)

            def mlp(sums, gate_at):
                side, ready = build()
                gemm(0, *h, side=side, ready=ready)

                def block(number, last=False):
                    first = [n["tr0"].n, n["tr1"].n]

                    def hidden(par):
                        def step():
                            pe.wait_ge(read_out[par], n[f"ro{par}"](n[f"ro{par}"].n + 1))
                            for kp in range(2):
                                claim_tr(kp)
                                pair_transposes(
                                    kp, lambda k, t: stb[:, t, (PK * kp + k) * P:(PK * kp + k + 1) * P]
                                ).then_inc(mid_full, 1)
                        return step

                    def mid_ready(j):
                        late = 2 if number == 0 and j >= 2 * (gate_at + 1) else 0
                        pe.wait_ge(tr_free[j % 2], n[f"tr{j % 2}"](first[j % 2] + j // 2 + 2 + late))

                    sides = [{2: [hidden(1 - c % 2)]} for c in range(1, 5)] + [{}, {}, {}]
                    if number == 0:
                        sides[gate_at] = also(sides[gate_at], halves(sum_rows, 5))
                    if sums:
                        sides[6] = halves(sum_columns, 3)
                    for c in range(1, 4):
                        gemm(c % 2, *h, side=sides[c - 1])
                    for c in range(4):
                        gemm(c % 2, PIECES, mid_hi, mid_lo, side=sides[c + 3], ready=mid_ready if c == 0 else None)
                    if not last:
                        gemm(0, *h)

                rises = dict(w=8 * PIECES, ro0=4, ro1=4, tr0=4, tr1=4)
                if sums:
                    rises.update(ada=KT, tr0=6, tr1=6)
                block(0)
                with repeat(pe, 2, n, **rises):
                    block(None)
                block(3, True)

            mlp(True, 1)

            side, ready = build()
            for ch in range(4):
                gemm(ch % 2, *h, side=qk if ch else side, ready=None if ch else ready)
            side, ready = build()
            gemm(0, *h, side=also(side, {5: [qk_transposes]}), ready=ready)
            gemm(1, *h, side=qk)
            for u in range(1, 4):
                scores_, values_ = attn_b((u - 1) * MAPS, 1)
                sums = {1: halves(sum_rows, 1), 3: halves(sum_columns, 1)}.get(u, {})
                gemm(0, *h, side=also(scores_, sums))
                last_unit = attn_b(3 * MAPS, 0)
                early = {5: last_unit[0][0], 6: last_unit[0][1], 7: last_unit[0][2]} if u == 3 else {}
                gemm(1, *h, side=also(values_, qk, early))
            pe.wait_ge(ov_free, n["ov"](n["ov"].n + 1))
            scores_, values_ = last_unit
            scores_[3][0]()
            side, ready = build(source=lambda kt, t: head_out[:, kt // 2, t, (kt % 2) * P:(kt % 2 + 1) * P],
                                modulate=False, between=1)

            def last_pair():
                pe.wait_ge(ov_free, n["ov"](n["ov"].n + 1))
                side[3][0]()

            gemm(0, *h, side={0: side[0], 1: side[1], 3: values_[1], 4: values_[2], 5: values_[4] + side[2],
                              6: [last_pair]}, ready=ready)
            for ch in range(1, 4):
                gemm(ch % 2, *h)
            all_of(halves(sum_columns, 0))
            mlp(False, 3)

        @block.scalar
        def _(act):
            n = Counts()

            def split():
                n["w"].up()
                w, base = n["w"].n, n["w"].base
                s = (w - 1) % SLOTS
                fills = ((w - 1) // SLOTS + 1) * 16
                act.wait_ge(raw_in[s], fills if base is None else base * (16 // SLOTS) + fills)
                act.wait_ge(mm_done, n["w"]())
                act.activation(w_hi[:, s, :], w_raw[:, s, :], ACT.Copy).then_inc(hi_done, 1)

            def chunk(pieces, side=None):
                for j in range(pieces + 1):
                    for step in (side or {}).get(j, ()):
                        step()
                    if j < pieces:
                        split()

            def ended(back):
                act.wait_ge(mm_done, n["w"](n["w"].n + SLOTS - back))

            def chained(ins):
                ins.then_inc(seq_a, 1)
                act.wait_ge(seq_a, n["seq"].up())

            def qk_stats(par, back=4, places=None):
                def step():
                    ended(back)
                    for t in range(T):
                        for m in range(MAPS):
                            i = t * MAPS + m
                            square = places[t][:, m * P:(m + 1) * P] if places else st_b[:, i * P:(i + 1) * P]
                            last = act.activation(square, main[par][t][:, m * P:(m + 1) * P],
                                                  ACT.Square, accum_out=ssq[:, i:i + 1])
                    chained(last)
                    act.activation(rms[:, :], ssq[:, :], ACT.Sqrt, bias=eps_t[:, :], scale=1.0 / HD).then_inc(rms_done, 1)
                return step

            def move_tile0(dst):
                def step():
                    n["qk"].up(2)
                    act.wait_ge(qk_full, n["qk"](n["qk"].n - 1))
                    act.activation(dst[:, :, 0:P], tr[0][:, :].rearrange("p (m n) -> p m n", m=MAPS),
                                   ACT.Copy).then_inc(tr_free[0], 1)
                return step

            def values(par, back=4):
                def step():
                    ended(back)
                    act.activation(vv[:, 0, :], main[par][0][:, :], ACT.Copy)
                    act.activation(vv[:, 1, :], main[par][1][:, :], ACT.Copy).then_inc(read_out[par], 1)
                return step

            def exps(running):
                def step():
                    act.wait_ge(smx_done, n["smx"].up())
                    if running:
                        act.activation(corr8[:, :], diff8[:, :], ACT.Exp)
                    for m in range(MAPS):
                        act.activation(sm[:, m, 0:P], sm[:, m, 0:P], ACT.Exp, bias=neg8[:, 2 * m:2 * m + 1],
                                       accum_out=d8[:, 2 * m:2 * m + 1])
                        act.activation(sm[:, m, P:3 * P], sm[:, m, P:3 * P], ACT.Exp, bias=neg8[:, 2 * m + 1:2 * m + 2],
                                       accum_out=d8[:, 2 * m + 1:2 * m + 2]).then_inc(p_done, 1)
                return step

            def move_pt():
                n["pt"].up(2)
                act.wait_ge(pt_full, n["pt"](n["pt"].n - 1))
                act.activation(pT[:, 0, :], tr[0][:, 0:3 * P], ACT.Copy).then_inc(tr_free[0], 1)

            def sub_stats():
                act.wait_ge(ov_full, n["ov"].up())
                act.activation(st_b[:, 0:2 * HD], ov[:, 0:2 * HD], ACT.Square, accum_out=ssv[:, 0:1])
                chained(act.activation(st_b[:, 2 * HD:4 * HD], ov[:, 2 * HD:4 * HD], ACT.Square, accum_out=ssv[:, 1:2]))
                act.activation(rmsv[:, :], ssv[:, :], ACT.Sqrt, bias=eps_t[:, :],
                               scale=1.0 / (2 * HD)).then_inc(sub_rms, 1)

            def squares(c):
                if n["sq"].n:
                    act.wait_ge(x_sq, n["sq"]())
                for t, bank in enumerate((sc, ov)):
                    last = act.activation(bank[:, :], xs[:, t, cols(c, NC)], ACT.Square, accum_out=ssx[:, t, c:c + 1])
                n["sq"].up()
                last.then_inc(x_sq, 1)

            def squares_of(c):
                def step():
                    act.wait_ge(x_done, n["x"].up())
                    squares(c)
                return step

            def root():
                act.wait_ge(x_sum, n["xs"].up())
                act.activation(rmsx[:, :], sumx[:, :], ACT.Sqrt, bias=eps_t[:, :], scale=1.0 / D).then_inc(x_rms, 1)

            def high(j, sections):
                def step():
                    if j == 0 and n["w"].n > SLOTS:
                        ended(4)
                    n["hT"].up()
                    act.wait_ge(hT_full, n["hT"]())
                    source = tr[j % 2][:, :]
                    if sections:
                        if j == 0:
                            act.wait_ge(mod_done, n["mod"].up())
                        if n["modulated"].n >= 2:
                            act.wait_ge(hT_split, n["modulated"].n - 1)
                        for k in range(PK):
                            g_col, s_col = (modc[:, x, PK * j + k:PK * j + k + 1] for x in sections)
                            part = slice(k * T * P, (k + 1) * T * P)
                            last = act.activation(stb[:, j % 2, part], tr[j % 2][:, part], ACT.Identity, bias=s_col,
                                                  scale=g_col)
                        last.then_inc(modulated, 1)
                        act.wait_ge(modulated, n["modulated"].up())
                        source = stb[:, j % 2, :]
                    act.activation(hT_hi[:, PK * j:PK * (j + 1), :].rearrange("p k n -> p (k n)"), source,
                                   ACT.Copy).then_inc(hi_part, 1)
                return step

            def entry(before, sections=None, pairs=PIECES):
                side = {4: list(before) + [high(j, sections) for j in range(4)]}
                for j in range(4, pairs):
                    side[j + 1] = [high(j, sections)]
                return side

            act.wait_ge(eps_set, 1)
            act.wait_ge(vec_done, 1)
            act.activation(c_act[:, :], vec[:, V_C, :], ACT.Exp, scale=-1.0).then_inc(c_exp, 1)
            act.wait_ge(lam_dot, 1)
            act.activation(lam[:, 2:4], lam[:, 0:2], ACT.Exp).then_inc(lam_exp, 1)
            act.wait_ge(trig, 1)
            act.activation(sin[:, :], small[:, 0:T * HALF], ACT.Sin)
            act.activation(cos[:, :], small[:, T * HALF:2 * T * HALF], ACT.Sin, bias=hpi_t[:, :],
                           scale=-1.0).then_inc(trig_done, 1)
            act.wait_ge(x_in_done, 16)
            for c in range(4):
                squares(c)
            root()
            q4, k4 = qT[:, 0:MAPS, :], kT[:, :, :]
            chunk(PIECES, entry([], (S_SCALE_T0, S_SHIFT_T0)))

            def group(last):
                chunk(PIECES, {4: [qk_stats(0), move_pt], 6: [move_pt], 8: [move_tile0(q4)]})
                chunk(PIECES, {4: [qk_stats(1)], 8: [move_tile0(k4)]})
                chunk(PIECES, {4: [values(0)]})
                chunk(PIECES, {4: [qk_stats(1)], 8: [move_tile0(q4), exps(True)]})
                chunk(PIECES, {4: [qk_stats(0), move_pt], 6: [move_pt], 8: [move_tile0(k4)]})
                if not last:
                    chunk(PIECES, {4: [values(1)], 8: [exps(True)]})

            with repeat(act, GROUPS - 1, n, w=6 * PIECES, seq=4, qk=8, smx=2, pt=8):
                group(False)
            group(True)
            heads = [high(j, None) for j in range(PIECES)]
            chunk(PIECES // 2, {4: [*heads[0:2], values(1), exps(True), move_pt, move_pt, *heads[2:4]]})
            chunk(PIECES // 2)
            for c in range(2):
                chunk(PIECES // 2, {4: [squares_of(c)]})

            def mlp(final, sections):
                chunk(PIECES, entry([squares_of(2), squares_of(3), root], sections))

                def block(last=False):
                    def relu(par):
                        def step():
                            ended(4)
                            for t in range(T):
                                last = act.activation(sta[:, t, :], main[par][t][:, :], ACT.Relu)
                            last.then_inc(relu_done, 1)
                        return step

                    def mid(c):
                        def step():
                            for kp in range(2):
                                act.wait_ge(mid_full, n["mid"].up())
                                kt = 4 * c + PK * kp
                                act.activation(mid_hi[:, kt:kt + PK, :],
                                               tr[kp][:, :].rearrange("p (k n) -> p k n", k=PK),
                                               ACT.Copy).then_inc(hi_part, 1)
                        return step

                    for c in range(1, 4):
                        chunk(PIECES, {4: [relu(1 - c % 2)], 7: [mid(c - 1)]})
                    chunk(PIECES, {4: [relu(1)], 7: [mid(3)]})
                    for c in range(1, 4):
                        chunk(PIECES, {6: [squares_of(c - 1)]} if last and not final else None)
                    if not last:
                        chunk(PIECES)
                        n["x"].up(4)
                block()
                with repeat(act, 2, n, w=8 * PIECES, mid=8, x=4):
                    block()
                block(True)

            mlp(False, (S_SCALE_M0, S_SHIFT_M0))
            for ch in range(4):
                chunk(PIECES, {4: [qk_stats(1 - ch % 2)], 8: [move_tile0(qT[:, (ch - 1) * MAPS:ch * MAPS, :])]} if ch
                      else entry([squares_of(3), root], (S_SCALE_T1, S_SHIFT_T1)))
            side = entry([], (S_SCALE_KV, S_SHIFT_KV))
            side[6].append(qk_stats(1, 6, (sc, ov)))
            chunk(PIECES, side)
            n["ov"].up(4 * GROUPS + 2)
            chunk(PIECES, {2: [move_tile0(qT[:, 3 * MAPS:4 * MAPS, :])], 4: [qk_stats(0)], 8: [move_tile0(k4)]})
            for u in range(1, 4):
                chunk(PIECES, {4: [values(1)], 8: [exps(False)]})
                chunk(PIECES, {4: [qk_stats(0), move_pt], 6: [sub_stats], 8: [move_tile0(k4), sub_stats]})
            chunk(PIECES, {4: [*heads[0:4], values(1), exps(False)], 5: [heads[4]], 6: [heads[5]], 8: [move_pt]})
            chunk(PIECES, {1: [sub_stats], 2: [heads[6], sub_stats], 3: [heads[7]]})
            for c in range(2):
                chunk(PIECES, {4: [squares_of(c)]})
            mlp(True, (S_SCALE_M1, S_SHIFT_M1))

        @block.vector
        def _(dve):
            n = Counts()

            def chained(ins):
                ins.then_inc(seq_v, 1)
                dve.wait_ge(seq_v, n["seq"].up())

            def split():
                n["w"].up()
                s = (n["w"].n - 1) % SLOTS
                dve.wait_ge(hi_done, n["w"]())
                dve.tensor_tensor(w_lo[:, s, :], w_raw[:, s, :], w_hi[:, s, :].bitcast(F32),
                                  ALU.subtract).then_inc(lo_done, 1)

            def ada_piece(kt):
                n["landed"].up()
                a, base = n["landed"].n, n["landed"].base
                s = (a - 1) % ADA_SLOTS
                fills = ((a - 1) // ADA_SLOTS + 1) * 16
                dve.wait_ge(ada_in[s], fills if base is None else base * (16 // ADA_SLOTS) + fills)
                accumulate(kt, ada_raw[:, s, :])

            def accumulate(kt, piece):
                n["ada"].up()
                a = n["ada"].n
                if kt == 0:
                    ins = dve.tensor_scalar(acc[:, :], piece, c_act[:, 0:1], None, ALU.mult)
                else:
                    dve.wait_ge(ada_used, n["ada"](a - 1 + ADA_SLOTS))
                    ins = dve.scalar_tensor_tensor(out=acc[:, :], in0=piece, scalar=c_act[:, kt:kt + 1],
                                                   in1=acc[:, :], op0=ALU.mult, op1=ALU.add)
                ins.then_inc(ada_used, 1)

            def chunk(ch, pieces, side=None, ada=(), kt0=0):
                for j in range(pieces + 1):
                    for step in (side or {}).get(j, ()):
                        step()
                    if j < pieces:
                        split()
                        if (ch, j) in ada:
                            ada_piece((kt0 + ada.index((ch, j))) % KT)

            def column_sums(quarter):
                def step():
                    dve.wait_ge(col_full, n["col"].up())
                    dve.tensor_reduce(sums[:, quarter * 4:(quarter + 1) * 4],
                                      tr[quarter % 2][:, :].rearrange("p (k n) -> p k n", k=4),
                                      mybir.AxisListType.X, ALU.add).then_inc(tr_free[quarter % 2], 1)
                return step

            def add_columns(at):
                def step():
                    settled()
                    dst = modc[:, at, :] if isinstance(at, int) else modc[:, bass.ds(at, 1), :].rearrange("p a k -> p (a k)")
                    dve.tensor_tensor(dst, dst, sums[:, :], ALU.add)
                return step

            def add_mixed_columns(i):
                def step():
                    settled()
                    dst = modc[:, S_SHIFT_T1:S_SHIFT_T1 + MIXED, cols(i, 4)]
                    dve.tensor_tensor(dst, dst, sums[:, :].rearrange("p (s k) -> p s k", s=MIXED), ALU.add)
                return step

            all_sums = [column_sums(quarter) for quarter in range(4)]

            def move_rows(quarter):
                def step():
                    if quarter == 0:
                        dve.wait_ge(gate_bias, n["gate"].up(16))
                    dve.wait_ge(row_full, n["row"].up())
                    dve.tensor_tensor(gate[:, quarter, :], tr[quarter % 2][:, :], gate[:, quarter, :],
                                      ALU.add).then_inc(tr_free[quarter % 2], 1)
                return step

            all_rows = [move_rows(quarter) for quarter in range(4)]

            def settled():
                chained(dve.memset(scratch[:, :], 0.0))

            def norm(par, gain):
                def step():
                    dve.wait_ge(rms_done, n["rms"].up())
                    chained(dve.reciprocal(rstd[:, :], rms[:, :]))
                    for t in range(T):
                        for m in range(MAPS):
                            i = t * MAPS + m
                            last = dve.scalar_tensor_tensor(
                                out=sta[:, t, m * P:(m + 1) * P], in0=main[par][t][:, m * P:(m + 1) * P],
                                scalar=rstd[:, i:i + 1], in1=gain(m), op0=ALU.mult, op1=ALU.mult)
                    last.then_inc(read_out[par], 1)
                return step

            def move_tile1(dst):
                def step():
                    dve.wait_ge(qk_full, n["qk"].up(2))
                    dve.tensor_copy(dst[:, :, P:2 * P],
                                    tr[1][:, :].rearrange("p (m n) -> p m n", m=MAPS)).then_inc(tr_free[1], 1)
                return step

            def mask_scores(m, mask):
                def step():
                    dve.wait_ge(sc_full, n["sc"].up())
                    dve.memset(scratch[:, :], 0.0)
                    for t, c in ((0, slice(0, P)), (1, slice(P, 3 * P))):
                        last = dve.tensor_tensor_reduce(sm[:, m, c], sc[:, c], mask[:, c], SCALE, NEG, ALU.add,
                                                        ALU.max, m8[:, 2 * m + t:2 * m + t + 1])
                    last.then_inc(sc_free, 1)
                return step

            def running_max(quad):
                def step():
                    dve.wait_ge(sc_free, n["sc"](n["sc"].n + 1))
                    chained(dve.tensor_tensor(mn8[:, :], m8[:, :], m_old[:, quad, :], ALU.max))
                    dve.tensor_scalar(neg8[:, :], mn8[:, :], -1.0, None, ALU.mult)
                    chained(dve.tensor_tensor(diff8[:, :], m_old[:, quad, :], mn8[:, :], ALU.subtract))
                    dve.tensor_copy(m_old[:, quad, :], mn8[:, :]).then_inc(smx_done, 1)
                return step

            def negate_max():
                dve.wait_ge(sc_free, n["sc"](n["sc"].n + 1))
                dve.tensor_scalar(neg8[:, :], m8[:, :], -1.0, None, ALU.mult).then_inc(smx_done, 1)

            def move_pt():
                dve.wait_ge(pt_full, n["pt"].up(2))
                dve.tensor_copy(pT[:, 1, :], tr[1][:, 0:3 * P]).then_inc(tr_free[1], 1)

            def merge(quad, pair):
                def step():
                    dve.wait_ge(ov_full, n["ov"].up())
                    if pair == 1:
                        chained(dve.tensor_tensor(den[:, quad, :], den[:, quad, :], corr8[:, :], ALU.mult))
                        dve.tensor_tensor(den[:, quad, :], den[:, quad, :], d8[:, :], ALU.add)
                    for i in range(2):
                        for t in range(T):
                            m = 2 * pair + i
                            o = group_out[:, quad * MAPS + m, t, :]
                            last = dve.scalar_tensor_tensor(
                                out=o, in0=o, scalar=corr8[:, 2 * m + t:2 * m + t + 1],
                                in1=ov[:, (i * T + t) * HD:(i * T + t + 1) * HD], op0=ALU.mult, op1=ALU.add)
                    last.then_inc(ov_free, 1)
                return step

            def mix():
                dve.wait_ge(p_done, n["p"].up(MAPS))
                chained(dve.reciprocal(r8[:, :], d8[:, :]))
                r = r8[:, :].rearrange("p (h c t) -> p h c t", c=2, t=T)
                chained(dve.tensor_scalar(r[:, :, 1, :], r[:, :, 1, :], lam[:, 5:6], None, ALU.mult))
                tiles = [(h, t, slice(0, P) if t == 0 else slice(P, 3 * P)) for h in range(2) for t in range(T)]
                for h, t, c in tiles:
                    last = dve.tensor_scalar(sm[:, 2 * h, c], sm[:, 2 * h, c], r[:, h, 0, t:t + 1], None, ALU.mult)
                chained(last)
                for h, t, c in tiles:
                    last = dve.scalar_tensor_tensor(out=sm[:, 2 * h, c], in0=sm[:, 2 * h + 1, c],
                                                    scalar=r[:, h, 1, t:t + 1], in1=sm[:, 2 * h, c],
                                                    op0=ALU.mult, op1=ALU.add)
                    if t == 1:
                        last.then_inc(mix_done, 1)

            def sub_norm(head):
                def step():
                    dve.wait_ge(sub_rms, n["sub"].up())
                    chained(dve.reciprocal(rstdv[:, :], rmsv[:, :]))
                    chained(dve.tensor_scalar(rstdv[:, :], rstdv[:, :], 1.0 - LAM_INIT, None, ALU.mult))
                    for t in range(T):
                        last = dve.scalar_tensor_tensor(
                            out=head_out[:, head, t, :], in0=ov[:, t * 2 * HD:(t + 1) * 2 * HD],
                            scalar=rstdv[:, t:t + 1], in1=subg[:, :], op0=ALU.mult, op1=ALU.mult)
                    last.then_inc(ov_free, 1)
                return step

            def low(j, source, done):
                dve.tensor_tensor(hT_lo[:, PK * j:PK * (j + 1), :].rearrange("p k n -> p (k n)"), source,
                                  hT_hi[:, PK * j:PK * (j + 1), :].rearrange("p k n -> p (k n)").bitcast(F32),
                                  ALU.subtract).then_inc(done, 1)

            def entry(before, sections, g):
                def start():
                    settled()
                    scale = modc[:, sections[0], :]
                    dve.scalar_tensor_tensor(out=scale, in0=scale, scalar=1.0, in1=vec[:, V_G + g, :],
                                             op0=ALU.add, op1=ALU.mult).then_inc(mod_done, 1)

                def pair(j):
                    def step():
                        dve.wait_ge(hi_part, n["hi"].up())
                        dve.memset(marks[:, j:j + 1], 0.0).then_inc(tr_free[j % 2], 1)
                        low(j, stb[:, j % 2, :], hT_split)
                    return step

                side = {4: list(before) + [start] + [pair(j) for j in range(4)]}
                for j in range(4, PIECES):
                    side[j + 1] = [pair(j)]
                return side

            def low_of_heads(j):
                def step():
                    dve.wait_ge(hi_part, n["hi"].up())
                    low(j, tr[j % 2][:, :], tr_free[j % 2])
                return step

            def sum_x():
                dve.wait_ge(x_sq, n["sq"].up(4))
                chained(dve.tensor_tensor(pairx[:, :, :], ssx[:, :, 0:2], ssx[:, :, 2:4], ALU.add))
                dve.tensor_tensor(sumx[:, :], pairx[:, :, 0], pairx[:, :, 1], ALU.add).then_inc(x_sum, 1)

            def x_recip():
                dve.wait_ge(x_rms, n["xr"].up())
                dve.reciprocal(rstdx[:, :], rmsx[:, :]).then_inc(x_rstd, 1)

            def ended(back):
                dve.wait_ge(mm_done, n["w"](n["w"].n + SLOTS - back))

            def update(c, back=4):
                def step():
                    ended(back)
                    settled()
                    for t in range(T):
                        last = dve.tensor_tensor(stb[:, t, :], main[c % 2][t][:, :], gate[:, c, :], ALU.mult)
                    last.then_inc(read_out[c % 2], 1)
                    settled()
                    for t in range(T):
                        xc = xs[:, t, cols(c, NC)]
                        last = dve.tensor_tensor(xc, xc, stb[:, t, :], ALU.add)
                    last.then_inc(x_done, 1)
                return step

            dve.sem_inc(lo_done, SLOTS)
            dve.sem_inc(ada_used, ADA_SLOTS)
            for s in (*read_out, *tr_free, sc_free, ov_free):
                dve.sem_inc(s, 1)
            dve.memset(eps_t[:, :], EPS)
            dve.memset(hpi_t[:, :], math.pi / 2).then_inc(eps_set, 1)
            freq = np.float32(500000.0) ** (-np.arange(0, ROT, 2, dtype=np.float32) / np.float32(ROT))
            for i in range(HALF):
                last = dve.memset(inv_freq[:, i:i + 1], float(freq[i]))
            chained(last)
            dve.wait_ge(dist_done, 1)
            for g, low_bits in enumerate((3, 15)):
                last = dve.tensor_scalar(residue_i[:, g * P:(g + 1) * P], dist[:, :], low_bits, None, ALU.bitwise_and)
            chained(last)
            dve.tensor_scalar(residue[:, :], residue_i[:, :], 0.0, NEG, ALU.is_gt, ALU.mult).then_inc(residue_done, 1)
            dve.wait_ge(small_in, 16 * 6)
            dve.wait_ge(vec_full, 1)
            dve.tensor_copy(vec[:, :, :].rearrange("p a b -> p (a b)"), tr[0][:, 0:96]).then_inc(tr_free[0], 1)
            dve.wait_ge(tr_free[0], 2)
            dve.sem_inc(vec_done, 1)
            dve.wait_ge(c_exp, 1)
            chained(dve.tensor_scalar(c_act[:, :], c_act[:, :], 1.0, None, ALU.add))
            chained(dve.reciprocal(c_act[:, :], c_act[:, :]))
            chained(dve.tensor_tensor(c_act[:, :], c_act[:, :], vec[:, V_C, :], ALU.mult))
            lm = st_a[:, 0:NC].rearrange("p (a b) -> p a b", a=4)
            dve.tensor_tensor_reduce(st_b[:, 0:P], lm[:, 0, :], lm[:, 1, :], 1.0, 0.0, ALU.mult, ALU.add, lam[:, 0:1])
            dve.tensor_tensor_reduce(st_b[:, P:2 * P], lm[:, 2, :], lm[:, 3, :], 1.0, 0.0, ALU.mult, ALU.add,
                                     lam[:, 1:2]).then_inc(lam_dot, 1)
            chained(dve.tensor_copy(pos_f[:, :], pos_i[:, :]))
            ang, mag = small[:, 0:T * HALF], small[:, T * HALF:2 * T * HALF]
            for t in range(T):
                last = dve.tensor_scalar(ang[:, t * HALF:(t + 1) * HALF], inv_freq[:, :], pos_f[:, t:t + 1], None, ALU.mult)
            chained(last)
            magic = 1.5 * 2.0 ** 23
            chained(dve.tensor_scalar(turns[:, :], ang, 1.0 / (2 * math.pi), magic, ALU.mult, ALU.add))
            chained(dve.tensor_scalar(turns[:, :], turns[:, :], -magic, None, ALU.add))
            c1 = 6.28125
            c2 = round((2 * math.pi - c1) * 2 ** 20) / 2 ** 20
            for part in (c1, c2, 2 * math.pi - c1 - c2):
                chained(dve.scalar_tensor_tensor(out=ang, in0=turns[:, :], scalar=-part, in1=ang, op0=ALU.mult,
                                                 op1=ALU.add))
            chained(dve.tensor_scalar(ang, ang, 3.1415925, -3.1415925, ALU.min, ALU.max))
            chained(dve.tensor_scalar(mag, ang, -1.0, None, ALU.mult))
            dve.tensor_tensor(mag, mag, ang, ALU.max).then_inc(trig, 1)
            dve.wait_ge(lam_exp, 1)
            chained(dve.tensor_tensor(lam[:, 4:5], lam[:, 3:4], lam[:, 2:3], ALU.subtract))
            chained(dve.tensor_scalar(lam[:, 5:6], lam[:, 4:5], -LAM_INIT, None, ALU.add))

            sum_x()
            for sec in range(2):
                for kt in range(KT):
                    fills, s = divmod(sec * KT + kt, len(ada_start))
                    dve.wait_ge(ada_start_in[s], 16 * (fills + 1))
                    accumulate(kt, ada_start[s])
                for step in (*all_sums, add_columns(sec)):
                    step()
            x_recip()
            q4, k4 = qT[:, 0:MAPS, :], kT[:, :, :]

            def gain_of(i):
                return lambda m: gain_now[:, i * HD:(i + 1) * HD]

            sc4 = [mask_scores(m, mask_now) for m in range(MAPS)]

            def invert_den(quad):
                def step():
                    settled()
                    dve.reciprocal(rden[:, quad * 8:(quad + 1) * 8], den[:, quad, :]).then_inc(den_inv, 1)
                return step

            def group(g, last):
                if last:
                    q_gain, k_gain, mask = (gains[:, cols(g, HD)], gains[:, cols(g + GROUPS, HD)], masks[:, g, :])
                else:
                    q_gain, k_gain = gains[:, bass.ds(g * HD, HD)], gains[:, bass.ds(g * HD + GROUPS * HD, HD)]
                    mask = masks[:, bass.ds(g, 1), :].rearrange("p a n -> p (a n)")
                dve.tensor_copy(gain_now[:, 0:HD], q_gain)
                dve.tensor_copy(gain_now[:, HD:2 * HD], k_gain)
                chained(dve.tensor_copy(mask_now[:, :], mask))
                chunk(0, PIECES, {4: [move_pt, norm(0, gain_of(0))], 5: [merge(1, 0)], 6: [move_pt],
                                  7: [merge(1, 1)], 8: [move_tile1(q4)]}, ADA_QKV)
                chunk(1, PIECES, {4: [norm(1, gain_of(1))], 8: [move_tile1(k4)]}, ADA_QKV)
                chunk(2, PIECES, None, ADA_QKV)
                chunk(3, PIECES, {4: [norm(1, gain_of(0)), sc4[0]], 5: [sc4[1]], 6: [sc4[2]], 7: [sc4[3]],
                                  8: [move_tile1(q4), running_max(0)]}, ADA_QKV)
                chunk(4, PIECES, {4: [move_pt, norm(0, gain_of(1))], 5: [merge(0, 0)], 6: [move_pt],
                                  7: [merge(0, 1)], 8: [move_tile1(k4), *([invert_den(0)] if last else [])]},
                      ADA_QKV)
                if not last:
                    chunk(5, PIECES, {4: [sc4[0]], 5: [sc4[1]], 6: [sc4[2], *all_sums[0:2]],
                                      7: [sc4[3], *all_sums[2:4]], 8: [running_max(1), add_columns(g + S_SHIFT_M0)]},
                          ADA_QKV)

            chunk(0, PIECES, entry([], (S_SCALE_T0, S_SHIFT_T0), 0))
            dve.wait_ge(consts, 3)
            with repeat(dve, GROUPS - 1, n, w=6 * PIECES, ada=KT, landed=KT, col=4, seq=12, rms=4, qk=8, sc=8, pt=8, ov=4) as g:
                group(g, False)
            group(GROUPS - 1, True)

            lows = [low_of_heads(j) for j in range(PIECES)]
            chunk(0, PIECES // 2, {1: [sc4[0]], 2: [sc4[1]], 3: [sc4[2]],
                                   4: [sc4[3], running_max(1), *lows[0:2], *all_rows, lambda: ada_piece(0), move_pt,
                                       merge(1, 0), move_pt, merge(1, 1), invert_den(1), lambda: ada_piece(1),
                                       *lows[2:4]]})
            for c in range(1, 4):
                chunk(c, PIECES // 2, {4: [update(c - 1)]}, ADA_WO, DRAIN)

            def mlp(before, sections, g, ada, first_ada, kt0, gate_at):
                chunk(0, PIECES, entry([update(3), sum_x, *before, x_recip], sections, g), ADA_ENTRY, kt0)
                kt0 += len(ADA_ENTRY)

                def square(par):
                    def step():
                        dve.wait_ge(relu_done, n["relu"].up())
                        for t in range(T):
                            last = dve.scalar_tensor_tensor(out=stb[:, t, :], in0=main[par][t][:, :], scalar=0.0,
                                                            in1=sta[:, t, :], op0=ALU.max, op1=ALU.mult)
                        last.then_inc(read_out[par], 1)
                    return step

                def mid(c):
                    def step():
                        for kp in range(2):
                            dve.wait_ge(mid_full, n["mid"].up())
                            dve.wait_ge(hi_part, n["hi"].up())
                            kt = 4 * c + PK * kp
                            dve.tensor_tensor(mid_lo[:, kt:kt + PK, :],
                                              tr[kp][:, :].rearrange("p (k n) -> p k n", k=PK),
                                              mid_hi[:, kt:kt + PK, :].bitcast(F32),
                                              ALU.subtract).then_inc(tr_free[kp], 1)
                    return step

                def block(i, last=False):
                    sides = [{4: [square(1 - c % 2)], 7: [mid(c - 1)]} for c in range(1, 5)]
                    sides += [{4: [update(c)]} for c in range(3)]
                    first = isinstance(i, int) and i == 0
                    if first:
                        sides[gate_at][1], sides[gate_at][2] = all_rows[0:2], all_rows[2:4]
                    if ada:
                        sides[6][PIECES] = [*all_sums, add_mixed_columns(i)]
                    for c in range(7):
                        chunk(c, PIECES, sides[c], first_ada if first else ada, kt0 if first else 0)
                    if not last:
                        chunk(7, PIECES, {4: [update(3)]})

                rises = dict(w=8 * PIECES, relu=4, mid=8, hi=8, seq=8)
                if ada:
                    rises.update(ada=KT, landed=KT, col=4, seq=9)
                block(0)
                with repeat(dve, 2, n, **rises) as i:
                    block(i + 1)
                block(3, True)

            mlp([], (S_SCALE_M0, S_SHIFT_M0), 1, ADA_MLP, ADA_GATE + ADA_FIRST, DRAIN + len(ADA_WO), 2)

            def map_gain(row):
                return lambda m: gains[:, (row + m % 2) * HD:(row + m % 2 + 1) * HD]

            for ch in range(4):
                chunk(ch, PIECES, {4: [norm(1 - ch % 2, map_gain(8))],
                                   8: [move_tile1(qT[:, (ch - 1) * MAPS:ch * MAPS, :])]} if ch else
                      entry([update(3), sum_x, x_recip], (S_SCALE_T1, S_SHIFT_T1), 2), ADA_Q)
            causal = [mask_scores(m, masks[:, 3, :]) for m in range(MAPS)]
            kv_ada = [(c - 4, j) for c, j in ADA_Q] + ADA_K + ADA_V

            def section_chunk(ch, side):
                chunk(ch, PIECES, side, kv_ada)

            side = entry([], (S_SCALE_KV, S_SHIFT_KV), 4)
            side[7].append(norm(1, map_gain(8)))
            section_chunk(0, side)
            n["p"].up(2 * MAPS * GROUPS + MAPS)
            section_chunk(1, {2: [move_tile1(qT[:, 3 * MAPS:4 * MAPS, :])], 4: [norm(0, map_gain(6))],
                              8: [move_tile1(k4)]})
            for u in range(1, 4):
                side = {4: [causal[0]], 5: [causal[1]], 6: [causal[2]], 7: [causal[3]], 8: [negate_max]}
                if u == 1:
                    side[6] += all_rows[0:2]
                    side[7] += all_rows[2:4]
                if u == 3:
                    side[6] += all_sums[0:2]
                    side[7] += all_sums[2:4]
                    side[8] += [add_columns(S_SCALE_M1)]
                section_chunk(2 * u, side)
                section_chunk(2 * u + 1, {2: [mix], 4: [move_pt, norm(0, map_gain(6))], 6: [sub_norm(2 * u - 2)],
                                          8: [move_tile1(k4), sub_norm(2 * u - 1)]})
            section_chunk(8, {1: [causal[0]], 2: [causal[1]], 3: [causal[2]],
                              4: [causal[3], negate_max, *lows[0:4]], 5: [lows[4]], 6: [lows[5], mix], 8: [move_pt]})
            section_chunk(9, {1: [sub_norm(6)], 2: [lows[6], sub_norm(7)], 3: [lows[7]],
                              4: [update(0)]})
            for c in range(2, 4):
                section_chunk(8 + c, {4: [update(c - 1)]})
            mlp([*all_sums, add_columns(S_SHIFT_M1)], (S_SCALE_M1, S_SHIFT_M1), 3, (), ADA_GATE_B, 0, 4)
            update(3, 0)()

        @block.gpsimd
        def _(pool):
            n = Counts()

            def chained(ins):
                ins.then_inc(seq_g, 1)
                pool.wait_ge(seq_g, n["seq"].up())

            def stage(pairs, source):
                for j in pairs:
                    if n["hT"].n > 1:
                        pool.wait_ge(hT_full, n["hT"](n["hT"].n - 1))
                    n["hT"].up()
                    for dst, src, scale in source(j, stx[:, j % 2, :]):
                        last = pool.tensor_scalar(dst, src, scale, 1.0, ALU.mult, ALU.mult)
                    last.then_inc(staged, 1)

            def x_rows(j, dst):
                return [(dst[:, t * PK * P:(t + 1) * PK * P], xs[:, t, j * PK * P:(j + 1) * PK * P],
                         rstdx[:, t:t + 1]) for t in range(T)]

            def head_rows(j, dst):
                return [(dst[:, (t * PK + k) * P:(t * PK + k + 1) * P], group_out[:, PK * j + k, t, :],
                         rden[:, (PK * j + k) * T + t:(PK * j + k) * T + t + 1]) for t in range(T) for k in range(PK)]

            def rope(par):
                pool.wait_ge(read_out[par], n[f"ro{par}"](n[f"ro{par}"].n + 1))
                for t in range(T):
                    v = sta[:, t, :].rearrange("p (m e) -> p m e", m=MAPS)
                    t1, t2 = v[:, :, 0:HALF], v[:, :, HALF:ROT]
                    c = cos[:, t * HALF:(t + 1) * HALF].unsqueeze(1).to_broadcast([P, MAPS, HALF])
                    s = sin[:, t * HALF:(t + 1) * HALF].unsqueeze(1).to_broadcast([P, MAPS, HALF])
                    pool.tensor_tensor(rot[:, t, 0], t1, c, ALU.mult)
                    pool.tensor_tensor(rot[:, t, 1], t2, s, ALU.mult)
                    pool.tensor_tensor(rot[:, t, 2], t2, c, ALU.mult)
                    last = pool.tensor_tensor(rot[:, t, 3], t1, s, ALU.mult)
                chained(last)
                for t in range(T):
                    v = sta[:, t, :].rearrange("p (m e) -> p m e", m=MAPS)
                    pool.tensor_tensor(v[:, :, 0:HALF], rot[:, t, 0], rot[:, t, 1], ALU.subtract)
                    last = pool.tensor_tensor(v[:, :, HALF:ROT], rot[:, t, 2], rot[:, t, 3], ALU.add)
                last.then_inc(roped, 1)

            def passed(par):
                n[f"ro{par}"].up()

            chained(pool.memset(ident[:, :], 0.0))
            pool.affine_select(out=ident[:, :], in_=ident[:, :], compare_op=ALU.not_equal, fill=1.0, base=0,
                               pattern=[[-1, P]], channel_multiplier=1).then_inc(consts, 1)
            pool.memset(ones[:, :], 1.0).then_inc(consts, 1)
            pool.iota(dist[:, :], base=P, pattern=[[-1, P]], channel_multiplier=1).then_inc(dist_done, 1)
            pool.memset(group_out[:, :, :, :], 0.0)
            pool.memset(m_old[:, :, :], NEG)
            pool.memset(den[:, :, :], 0.0)
            pool.memset(d8[:, :], 0.0)
            pool.memset(corr8[:, :], 1.0)
            pool.memset(vv[:, :, :], 0.0)
            chained(pool.memset(masks[:, :, :], 0.0))
            pool.wait_ge(residue_done, 1)
            for g in range(1, GROUPS):
                for b in range(3):
                    pool.tensor_copy(masks[:, g, b * P:(b + 1) * P], residue[:, (g - 1) * P:g * P])
            chained(pool.memset(scratch_g[:, :], 0.0))
            for g in range(4):
                for b in (0, 2):
                    last = pool.affine_select(out=masks[:, g, b * P:(b + 1) * P], in_=masks[:, g, b * P:(b + 1) * P],
                                              compare_op=ALU.is_ge, fill=NEG, base=0, pattern=[[-1, P]],
                                              channel_multiplier=1)
            last = pool.affine_select(out=masks[:, 0, P:2 * P], in_=masks[:, 0, P:2 * P], compare_op=ALU.is_ge,
                                      fill=NEG, base=0, pattern=[[1, P]], channel_multiplier=-1)
            last.then_inc(consts, 1)
            pool.wait_ge(vec_full, 1)
            pool.memset(sm[:, :, :], 0.0).then_inc(p_done, MAPS)
            pool.wait_ge(trig_done, 1)
            pool.wait_ge(x_rstd, 1)
            stage(range(PIECES), x_rows)

            def group():
                passed(0)
                rope(0)
                passed(1)
                rope(1)
                passed(0)
                passed(1)
                rope(1)
                passed(0)
                rope(0)
                passed(1)

            with repeat(pool, GROUPS, n, ro0=3, ro1=3, seq=4):
                group()
            for quad in range(2):
                pool.wait_ge(den_inv, quad + 1)
                stage(range(2 * quad, 2 * quad + 2), head_rows)
            n["ro0"].up(2)
            n["ro1"].up(2)
            pool.wait_ge(x_rstd, 2)
            stage(range(PIECES), x_rows)
            n["ro0"].up(16)
            n["ro1"].up(16)
            pool.wait_ge(x_rstd, 3)
            stage(range(PIECES), x_rows)
            for ch in range(3):
                passed(ch % 2)
                rope(ch % 2)
            stage(range(PIECES), x_rows)
            passed(1)
            rope(1)
            for u in range(4):
                passed(0)
                rope(0)
                passed(1)
            n["hT"].up(PIECES)
            n["ro0"].up(2)
            n["ro1"].up(2)
            pool.wait_ge(x_rstd, 4)
            stage(range(PIECES), x_rows)


def kernel(**inputs):
    from concourse import bacc
    from concourse.bass_utils import run_bass_kernel_spmd

    f = {k: np.asarray(v) for k, v in inputs.items()}

    def section(name, s):
        w, b = (f["kv_ada_w"], f["kv_ada_b"]) if name == "kv" else (f["ada_w"][name], f["ada_b"][name])
        return w[:, cols(s, D)], b[cols(s, D)]

    order = [section(*a) for a in ((0, 0), (0, 1), (0, 3), (0, 4), (0, 2), (0, 5), (1, 0), (1, 1), ("kv", 0), ("kv", 1),
                                   (1, 2), (1, 4), (1, 3), (1, 5))]
    ada = [w for w, _ in order]
    ada[6:10] = [np.concatenate([w[:, cols(i, NC)] for w in ada[6:10]], axis=1) for i in range(4)]
    bias = [b for _, b in order]
    bias_cols = np.stack([b.reshape(KT, P) for b in (*bias[0:4], *bias[6:10], bias[12], bias[11])])

    def pieces(w):
        k, m = w.shape
        return w.reshape(k // (PK * P), PK, P, m // NC, NC).transpose(3, 0, 2, 1, 4).reshape(-1, PK * NC)

    qkv = f["a_w_qkv"][0].reshape(D, GROUPS, 3, 2, NC)
    stream = []
    for g in range(GROUPS):
        for quad in range(2):
            for part in range(3):
                stream.append(pieces(qkv[:, g, part, quad]))
    stream.append(pieces(f["a_w_o"][0]))
    for layer in range(LAYERS):
        if layer:
            stream.append(pieces(f["b_w_q"][0]))
            for u in range(4):
                stream += [pieces(f["kv_w_k"][:, cols(u, NC)]), pieces(f["kv_w_v"][:, cols(u, NC)])]
            stream.append(pieces(f["b_w_o"][0]))
        for b in range(4):
            stream += [pieces(f["mlp_w1"][layer][:, cols(b, D)]), pieces(f["mlp_w2"][layer][cols(b, D)])]
    vecs = np.concatenate([f["c"].reshape(-1, P), f["norm_g"].reshape(-1, P), f["kv_norm_g"].reshape(-1, P)])
    gains = np.concatenate([f["a_q_gain"][0], f["a_k_gain"][0], f["kv_k_gain"], f["b_q_gain"][0]])
    arrays = {
        "x": f["x"].reshape(SEQ, D),
        "vecs": vecs,
        "pos": f["positions"].reshape(T, P).T,
        "gains": gains.reshape(-1),
        "subg": f["b_subln_g"].reshape(-1),
        "lamb": f["b_lambda"].reshape(-1),
        "ada": np.concatenate(ada),
        "bias_cols": bias_cols.transpose(2, 0, 1),
        "bias_rows": np.stack([bias[4], bias[5], bias[10], bias[13]]),
        "w": np.concatenate(stream),
    }
    nc = bacc.Bacc("TRN2", target_bir_lowering=False, num_devices=1)
    args = []
    arrays = {k: np.ascontiguousarray(a) for k, a in arrays.items()}
    for name, a in arrays.items():
        args.append(nc.dram_tensor(name, a.shape, mybir.dt.from_np(a.dtype), kind="ExternalInput").ap())
    args.append(nc.dram_tensor("out", (SEQ, D), F32, kind="ExternalOutput").ap())
    trunk(nc, *args)
    r = run_bass_kernel_spmd(nc, [arrays], core_ids=[0])
    return r.results[0]["out"].reshape(1, SEQ, D)
```
